# Optimizing a Trainium2 kernel written in Bass

```python
import jax, jax.numpy as jnp
from jax import lax
import numpy as np

D_MODEL = 1024
BATCH = 1
SEQ = 512
DEPTH = 2

N_MIXERS = 2
N_ATTN_LAYERS = (DEPTH + 1) // 2
N_RWKV_LAYERS = DEPTH // 2

HEAD_DIM = 64
ATTN_Q_HEADS = D_MODEL // HEAD_DIM
ATTN_KV_HEADS = 4
ATTN_GROUP = ATTN_Q_HEADS // ATTN_KV_HEADS
QKV_WIDTH = (ATTN_Q_HEADS + 2 * ATTN_KV_HEADS) * HEAD_DIM
WINDOW = 128
BLOCK = WINDOW
ROPE_THETA = 10000.0

RWKV_HEAD = 64
RWKV_HEADS = D_MODEL // RWKV_HEAD
DECAY_LORA = 64
ICLR_LORA = 64
GATE_LORA = 160
LNX_EPS = 64e-5

D_FF = 2816
RMS_EPS = 1e-6

kernel_name = "hybrid_swa_sink_rwkv7_macaron"

def rms_norm(x, g):
    xf = x.astype(jnp.float32)
    y = xf * lax.rsqrt(jnp.mean(xf * xf, axis=-1, keepdims=True) + RMS_EPS) * g
    return y.astype(x.dtype)

def swiglu(h, w_in, w_out):
    gu = h @ w_in
    gate, up = gu[..., :D_FF], gu[..., D_FF:]
    return (jax.nn.silu(gate) * up) @ w_out

def rope_tables(seq):
    inv_freq = ROPE_THETA ** (-jnp.arange(0, HEAD_DIM, 2, dtype=jnp.float32) / HEAD_DIM)
    ang = jnp.arange(seq, dtype=jnp.float32)[:, None] * inv_freq[None, :]
    return jnp.cos(ang)[:, None, :], jnp.sin(ang)[:, None, :]

def apply_rope(x, cos, sin):
    xf = x.astype(jnp.float32)
    x1, x2 = xf[..., :HEAD_DIM // 2], xf[..., HEAD_DIM // 2:]
    out = jnp.concatenate([x1 * cos - x2 * sin, x2 * cos + x1 * sin], axis=-1)
    return out.astype(x.dtype)

def swa_sink_attention(h, w_qkv, b_qkv, sinks, w_o):
    B, S, _ = h.shape
    nb = S // BLOCK
    qkv = h @ w_qkv + b_qkv
    nq = ATTN_Q_HEADS * HEAD_DIM
    nk = ATTN_KV_HEADS * HEAD_DIM
    q = qkv[..., :nq].reshape(B, S, ATTN_Q_HEADS, HEAD_DIM)
    k = qkv[..., nq:nq + nk].reshape(B, S, ATTN_KV_HEADS, HEAD_DIM)
    v = qkv[..., nq + nk:].reshape(B, S, ATTN_KV_HEADS, HEAD_DIM)
    cos, sin = rope_tables(S)
    q = apply_rope(q, cos, sin)
    k = apply_rope(k, cos, sin)

    qb = q.reshape(B, nb, BLOCK, ATTN_KV_HEADS, ATTN_GROUP, HEAD_DIM)
    pad = ((0, 0), (BLOCK, 0), (0, 0), (0, 0))
    kb = jnp.pad(k, pad).reshape(B, nb + 1, BLOCK, ATTN_KV_HEADS, HEAD_DIM)
    vb = jnp.pad(v, pad).reshape(B, nb + 1, BLOCK, ATTN_KV_HEADS, HEAD_DIM)
    k_band = jnp.concatenate([kb[:, :-1], kb[:, 1:]], axis=2)
    v_band = jnp.concatenate([vb[:, :-1], vb[:, 1:]], axis=2)

    scale = HEAD_DIM ** -0.5
    s = jnp.einsum('bnqhgd,bnkhd->bnhgqk', qb, k_band).astype(jnp.float32) * scale
    qi = jnp.arange(BLOCK)[:, None]
    kj = jnp.arange(2 * BLOCK)[None, :]
    diff = qi - kj + BLOCK
    kpos = jnp.arange(nb)[:, None, None] * BLOCK - BLOCK + kj[None]
    mask = (diff >= 0) & (diff < WINDOW) & (kpos >= 0)
    mask = mask[None, :, None, None]
    s = jnp.where(mask, s, -jnp.inf)
    sink = sinks.astype(jnp.float32).reshape(ATTN_KV_HEADS, ATTN_GROUP)[None, None, :, :, None, None]
    m = jnp.maximum(jnp.max(s, axis=-1, keepdims=True), sink)
    p = jnp.exp(s - m)
    denom = jnp.sum(p, axis=-1, keepdims=True) + jnp.exp(sink - m)
    p = p / denom
    o = jnp.einsum('bnhgqk,bnkhd->bnqhgd', p, v_band.astype(jnp.float32))
    o = o.reshape(B, S, ATTN_Q_HEADS * HEAD_DIM).astype(h.dtype)
    return o @ w_o

def wkv7_scan(r, w, k, v, a, b):
    B, S, H, N = r.shape

    def step(state, inp):
        r_t, w_t, k_t, v_t, a_t, b_t = inp
        sa = jnp.einsum('bhij,bhj->bhi', state, a_t)
        state = (state * w_t[:, :, None, :]
                 + sa[..., None] * b_t[:, :, None, :]
                 + v_t[..., None] * k_t[:, :, None, :])
        y = jnp.einsum('bhij,bhj->bhi', state, r_t)
        return state, y

    xs = tuple(jnp.moveaxis(t, 1, 0) for t in (r, w, k, v, a, b))
    s0 = jnp.zeros((B, H, N, N), jnp.float32)
    _, ys = lax.scan(step, s0, xs)
    return jnp.moveaxis(ys, 0, 1)

def rwkv7_time_mix(h, mix, w_rkv, w_o, w0, w1, w2, a0, a1, a2, g1, g2,
                   k_k, k_a, r_k, lnx_g, lnx_b):
    B, S, D = h.shape
    H, N = RWKV_HEADS, RWKV_HEAD
    xx = jnp.pad(h, ((0, 0), (1, 0), (0, 0)))[:, :-1] - h
    xr = h + xx * mix[0]
    xw = h + xx * mix[1]
    xk = h + xx * mix[2]
    xv = h + xx * mix[3]
    xa = h + xx * mix[4]
    xg = h + xx * mix[5]

    r = xr @ w_rkv[0]
    k = xk @ w_rkv[1]
    v = xv @ w_rkv[2]
    logw = -jax.nn.softplus(-(w0 + jnp.tanh(xw @ w1) @ w2)) - 0.5
    decay = jnp.exp(-jnp.exp(logw.astype(jnp.float32)))
    iclr = jax.nn.sigmoid(a0 + (xa @ a1) @ a2)
    g = jax.nn.sigmoid(xg @ g1) @ g2

    heads = lambda t: t.reshape(B, S, H, N).astype(jnp.float32)
    kk = heads(k * k_k)
    kk = kk / jnp.maximum(jnp.sqrt(jnp.sum(kk * kk, axis=-1, keepdims=True)), 1e-12)
    k = k * (1.0 + (iclr - 1.0) * k_a)

    rh, kh, vh, dh, ih = heads(r), heads(k), heads(v), heads(decay), heads(iclr)
    y = wkv7_scan(rh, dh, kh, vh, -kk, kk * ih)

    mu = jnp.mean(y, axis=-1, keepdims=True)
    var = jnp.mean((y - mu) ** 2, axis=-1, keepdims=True)
    yn = ((y - mu) * lax.rsqrt(var + LNX_EPS)).reshape(B, S, D) * lnx_g + lnx_b
    bonus = (jnp.sum(rh * kh * r_k, axis=-1, keepdims=True) * vh).reshape(B, S, D)
    out = (yn + bonus).astype(h.dtype) * g
    return out @ w_o

def setup_inputs(seed: int = 0) -> dict:
    key = jax.random.key(seed)
    ks = jax.random.split(key, 32)
    f32 = jnp.float32
    nrm = lambda k, shape, s: jax.random.normal(k, shape, f32) * s
    NA, NR, D = N_ATTN_LAYERS, N_RWKV_LAYERS, D_MODEL
    return {
        "x": nrm(ks[0], (BATCH, SEQ, D), 1.0),
        "norm_g": 1.0 + nrm(ks[1], (DEPTH, 6, D), 0.05),
        "ffn_w_in": nrm(ks[2], (DEPTH, 2, D, 2 * D_FF), D ** -0.5),
        "ffn_w_out": nrm(ks[3], (DEPTH, 2, D_FF, D), D_FF ** -0.5),
        "attn_w_qkv": nrm(ks[4], (NA, D, QKV_WIDTH), D ** -0.5),
        "attn_b_qkv": nrm(ks[5], (NA, QKV_WIDTH), 0.02),
        "attn_sinks": nrm(ks[6], (NA, ATTN_Q_HEADS), 1.0),
        "attn_w_o": nrm(ks[7], (NA, ATTN_Q_HEADS * HEAD_DIM, D), (ATTN_Q_HEADS * HEAD_DIM) ** -0.5),
        "rwkv_mix": jax.random.uniform(ks[8], (NR, 6, D), f32),
        "rwkv_w_rkv": nrm(ks[9], (NR, 3, D, D), D ** -0.5),
        "rwkv_w_o": nrm(ks[10], (NR, D, D), D ** -0.5),
        "rwkv_w0": jax.random.uniform(ks[11], (NR, D), f32, minval=-6.0, maxval=-0.5),
        "rwkv_w1": nrm(ks[12], (NR, D, DECAY_LORA), D ** -0.5),
        "rwkv_w2": nrm(ks[13], (NR, DECAY_LORA, D), 0.1 * DECAY_LORA ** -0.5),
        "rwkv_a0": nrm(ks[14], (NR, D), 0.1),
        "rwkv_a1": nrm(ks[15], (NR, D, ICLR_LORA), D ** -0.5),
        "rwkv_a2": nrm(ks[16], (NR, ICLR_LORA, D), 0.3 * ICLR_LORA ** -0.5),
        "rwkv_g1": nrm(ks[17], (NR, D, GATE_LORA), D ** -0.5),
        "rwkv_g2": nrm(ks[18], (NR, GATE_LORA, D), GATE_LORA ** -0.5),
        "rwkv_k_k": 0.85 + nrm(ks[19], (NR, D), 0.05),
        "rwkv_k_a": 1.0 + nrm(ks[20], (NR, D), 0.05),
        "rwkv_r_k": nrm(ks[21], (NR, RWKV_HEADS, RWKV_HEAD), 0.1),
        "rwkv_lnx_g": 1.0 + nrm(ks[22], (NR, D), 0.05),
        "rwkv_lnx_b": nrm(ks[23], (NR, D), 0.02),
    }

def reference(x, norm_g, ffn_w_in, ffn_w_out, attn_w_qkv, attn_b_qkv, attn_sinks, attn_w_o,
              rwkv_mix, rwkv_w_rkv, rwkv_w_o, rwkv_w0, rwkv_w1, rwkv_w2, rwkv_a0, rwkv_a1,
              rwkv_a2, rwkv_g1, rwkv_g2, rwkv_k_k, rwkv_k_a, rwkv_r_k, rwkv_lnx_g, rwkv_lnx_b):
    for i in range(DEPTH):
        g = norm_g[i]
        x = x + 0.5 * rms_norm(swiglu(rms_norm(x, g[0]), ffn_w_in[i, 0], ffn_w_out[i, 0]), g[1])
        h = rms_norm(x, g[2])
        j = i // N_MIXERS
        if i % N_MIXERS == 0:
            m = swa_sink_attention(h, attn_w_qkv[j], attn_b_qkv[j], attn_sinks[j], attn_w_o[j])
        else:
            m = rwkv7_time_mix(h, rwkv_mix[j], rwkv_w_rkv[j], rwkv_w_o[j], rwkv_w0[j], rwkv_w1[j],
                               rwkv_w2[j], rwkv_a0[j], rwkv_a1[j], rwkv_a2[j], rwkv_g1[j],
                               rwkv_g2[j], rwkv_k_k[j], rwkv_k_a[j], rwkv_r_k[j],
                               rwkv_lnx_g[j], rwkv_lnx_b[j])
        x = x + rms_norm(m, g[3])
        x = x + 0.5 * rms_norm(swiglu(rms_norm(x, g[4]), ffn_w_in[i, 1], ffn_w_out[i, 1]), g[5])
    return x


_drawn_inputs = setup_inputs


def setup_inputs(seed=0):
    import zlib

    import numpy as np

    out = dict(_drawn_inputs(seed))
    spreads = {}
    factors = {'rwkv_w1': 8.0, 'rwkv_w2': 8.0, 'rwkv_lnx_b': 5.677}
    for name, (base, spread) in spreads.items():
        noise = np.random.default_rng([zlib.crc32(name.encode()), seed]).standard_normal(out[name].shape)
        drawn = base * np.exp(spread * noise) if base else spread * noise
        out[name] = __import__('jax').numpy.asarray(drawn.astype(out[name].dtype))
    for name, factor in factors.items():
        out[name] = (out[name] * factor).astype(out[name].dtype)
    return out
```

```python
import math
from contextlib import ExitStack

import concourse.bass as bass
from concourse import mybir

F32 = mybir.dt.float32
F32R = mybir.dt.float32r
I32 = mybir.dt.int32
ACT = mybir.ActivationFunctionType
ALU = mybir.AluOpType
AX = mybir.AxisListType

P = 128
D = 1024
S = 512
DFF = 2816
C = D // P
FC = DFF // P
PANEL = 256
PK = 8
NG = 6


MIXES = [1, 4, 5, 0, 2, 3]
ROWS = ["attn_b_qkv", "rwkv_mix", "rwkv_w0", "rwkv_a0", "rwkv_k_k", "rwkv_k_a", "rwkv_r_k", "rwkv_lnx_g",
        "rwkv_lnx_b"]
VIEWS = {"rwkv_mix": "o m (c p) -> (o m c) p", "rwkv_r_k": "o (c h) k -> (o c) (h k)"}
N_ROWS = 12 + 6 * C + 7 * C


def kind_of(stage):
    return "ffn" if stage.startswith("ffn") else stage


def groups_of(k):
    return [(a, min(PK, k - a)) for a in range(0, k, PK)]


class SlotCount:

    def __init__(self):
        self.base, self.i, self.per, self.local = [0, 0], 0, [0, 0], [0, 0]

    def enter(self, i, per):
        self.base = [b + l for b, l in zip(self.base, self.local)]
        self.i, self.per, self.local = i, per, [0, 0]

    def leave(self, n):
        assert self.local == self.per
        self.base = [b + n * p for b, p in zip(self.base, self.per)]
        self.i, self.per, self.local = 0, [0, 0], [0, 0]

    def peek(self, s):
        k = self.base[s] + self.local[s]
        return self.i * self.per[s] + k if self.per[s] and not isinstance(self.i, int) else k + self.i * self.per[s]

    def next(self, s):
        k = self.peek(s)
        self.local[s] += 1
        return k


NORM = {"squares": C, "summed": C, "log": 1, "rstd": 1}
OPERAND = {"scaled": C, "hi": C, "xn": C}
OUT = {"y_squares": 4 + C, "y_sum": 2 + C, "y_mean": 1, "y_log": 1, "y_rstd": 1, "y_scaled": C}
FFN = {"silu": 1 + FC // 2, "product": 1 + FC // 2, "hid_hi": FC // 2, "hid": 1 + FC // 2}
SHARED = {"ffn": {**NORM, **OPERAND, **OUT, **FFN}, "attn": {**NORM, **OPERAND, **OUT}, "rwkv": {**NORM, **OUT}}


class Signals:

    def __init__(self, nc, ctx, stage, shared, earlier):
        self.nc, self.ctx, self.stage, self.shared, self.own = nc, ctx, stage, shared, {}
        self.counted = {}
        for kind in earlier:
            for name, times in SHARED[kind].items():
                self.counted[name] = self.counted.get(name, 0) + times

    def __call__(self, name, count=None):
        common = any(name in names for names in SHARED.values())
        made, full = (self.shared, name) if common else (self.own, f"{self.stage}_{name}")
        if name not in made:
            made[name] = self.ctx.enter_context(self.nc.semaphore(full))
        if count is None:
            return made[name]
        return made[name], count + (self.counted.get(name, 0) if common else 0)


def build(nc, a, out, stages):
    with ExitStack() as ctx:
        start = (nc.sbuf_base + 31) // 32 * 32
        place = {"at": 0}

        def sb(name, shape, dt, offset):
            return nc.alloc_sbuf_tensor_at(name, shape, dt, offset=start + offset)

        def take(nbytes):
            at = place["at"]
            place["at"] = at + (nbytes + 31) // 32 * 32
            return at

        o_x = take(C * S * 4)
        o_raw = take(2 * PK * PANEL * 4)
        o_whi = take(2 * PK * PANEL * 4)
        o_wlo = take(2 * PK * PANEL * 4)
        o_xnh = take(C * S * 4)
        o_xnl = take(C * S * 4)
        o_arena = take(2 * FC * S * 4)
        o_tmp = take(8 * S * 4)
        o_const = take(4 * P * 4)

        x = sb("x", [P, C, S], F32, o_x)
        w_raw = sb("w_raw", [P, 2, PK, PANEL], F32, o_raw)
        w_hi = sb("w_hi", [P, 2, PK, PANEL], F32R, o_whi)
        w_lo = sb("w_lo", [P, 2, PK, PANEL], F32R, o_wlo)
        xn_hi = sb("xn_hi", [P, C, S], F32R, o_xnh)
        xn_lo = sb("xn_lo", [P, C, S], F32R, o_xnl)
        hid_hi = sb("hid_hi", [P, FC, S], F32R, o_arena)
        hid_lo = sb("hid_lo", [P, FC, S], F32R, o_arena + FC * S * 4)
        y_ffn = sb("y_ffn", [P, C, S], F32, o_xnh)
        sq = sb("sq", [P, 2, S], F32, o_tmp)
        rstd = sb("rstd", [P, S], F32, o_tmp + 2 * S * 4)
        acc = sb("acc", [P, S], F32, o_tmp + 3 * S * 4)
        hn = sb("hn", [P, 2, S], F32, o_tmp + 4 * S * 4)
        sil = sb("sil", [P, 2, S], F32, o_tmp + 6 * S * 4)
        ident = sb("ident", [P, P], F32, o_const)
        ones_d = sb("ones_d", [P, P], F32, o_const + P * 4)
        vec_n = sb("vec_n", [P, 2 * NG * C], F32, o_const + 2 * P * 4)
        vec_h = sb("vec_h", [P, 2 * NG * C], F32, o_const + 3 * P * 4)
        o_vr = take(P * 4)
        vec_r = sb("vec_r", [P, P], F32, o_vr)
        o_eps = take(32)
        eps_rms = sb("eps_rms", [P, 1], F32, o_eps)
        assert start + place["at"] <= nc.sbuf_usable_end, place

        xt = sb("xt", [P, S // P, D], F32, o_arena)
        rows_n = sb("rows_n", [2 * NG * C, P], F32, o_arena + 4 * D * 4)
        rows_r = sb("rows_r", [P, P], F32, o_arena + 4 * D * 4 + P * 4)
        ot = sb("ot", [P, S // P, D], F32, o_arena)

        ps = ctx.enter_context(nc.psum_tensor("ps", [P, 8, 512], F32))

        def sem(name):
            return ctx.enter_context(nc.semaphore(name))

        loaded = [sem("loaded0"), sem("loaded1")]
        hi_done = [sem("hi_done0"), sem("hi_done1")]
        lo_done = [sem("lo_done0"), sem("lo_done1")]
        used = [sem("used0"), sem("used1")]
        consts_in, x_in, x_ready, out_done = sem("consts_in"), sem("x_in"), sem("x_ready"), sem("out_done")

        shared = {}

        def signals(stage, earlier=()):
            return Signals(nc, ctx, stage, shared, [kind_of(e) for e in earlier])

        def ch(t, c):
            return t[:, bass.ds(c, 1), :]

        def col(v, c):
            return v[:, bass.ds(c, 1)]

        def gain(l, i, c):
            return (l * NG + i) * C + c

        def load(sp, n, s, src, cols=PANEL):
            k = n.next(s)
            sp.wait_ge(lo_done[s], k + 1)
            sp.dma_start(w_raw[:, s, 0:src.shape[1], 0:cols], src).then_inc(loaded[s], 16)

        def split_hi(act, n, s):
            k = n.next(s)
            act.wait_ge(loaded[s], (k + 1) * 16)
            act.wait_ge(used[s], k + 1)
            nc.scalar.activation(w_hi[:, s, :, :], w_raw[:, s, :, :], ACT.Copy).then_inc(hi_done[s], 1)

        def split_lo(dve, n, s):
            k = n.next(s)
            dve.wait_ge(hi_done[s], k + 1)
            nc.vector.tensor_tensor(w_lo[:, s, :, :], w_raw[:, s, :, :], w_hi[:, s, :, :].bitcast(F32),
                                    ALU.subtract).then_inc(lo_done[s], 1)

        def wait_used(eng, n, s):
            eng.wait_ge(used[s], n.peek(s) + 1)

        def products(pe, n, s, count, banks, hi, lo, first, last, arrived=None, widths=(P, P), freed=None):
            pe.wait_ge(lo_done[s], n.next(s) + 2)
            for k in range(count):
                if arrived:
                    arrived(k)
                for m, bank in enumerate(banks):
                    wh = w_hi[:, s, k, m * P:m * P + widths[m]]
                    wl = w_lo[:, s, k, m * P:m * P + widths[m]]
                    nc.tensor.matmul(bank, wh, hi(k), start=first and k == 0, stop=False)
                    nc.tensor.matmul(bank, wh, lo(k), start=False, stop=False)
                    end = nc.tensor.matmul(bank, wl, hi(k), start=False, stop=last and k == count - 1)
                if freed and k < count - 1:
                    end.then_inc(freed, 1)
            end.then_inc(used[s], 1)

        def norm_in_pe(pe, g):
            for c in range(C):
                pe.wait_ge(*g("squares", c + 1))
                nc.tensor.matmul(ps[:, 1, :], ones_d[:], sq[:, c % 2, :], start=c == 0,
                                 stop=c == C - 1).then_inc(g("summed"), 1)

        def norm_in_squares(act, g, seen):
            for c in range(C):
                act.wait_ge(x_ready, seen + c + 1)
                if c >= 2:
                    act.wait_ge(*g("summed", c - 1))
                nc.scalar.activation(ch(sq, c % 2), ch(x, c), ACT.Square).then_inc(g("squares"), 1)
            act.wait_ge(*g("summed", C))
            nc.scalar.activation(rstd[:], ps[:, 1, :], ACT.Ln, bias=eps_rms[:]).then_inc(g("log"), 1)
            act.wait_ge(*g("log", 1))
            nc.scalar.activation(rstd[:], rstd[:], ACT.Exp, scale=-0.5).then_inc(g("rstd"), 1)

        def norm_in_hi(act, g):
            for c in range(C):
                act.wait_ge(*g("scaled", c + 1))
                nc.scalar.activation(ch(xn_hi, c), ch(hn, c % 2), ACT.Copy).then_inc(g("hi"), 1)

        def norm_in_dve(dve, g, l, i):
            dve.wait_ge(*g("rstd", 1))
            for c in range(C + 1):
                if c < C:
                    if c >= 2:
                        dve.wait_ge(*g("xn", c - 1))
                    nc.vector.scalar_tensor_tensor(ch(hn, c % 2), ch(x, c), col(vec_n, gain(l, i, c)),
                                                   rstd[:],
                                                   ALU.mult, ALU.mult).then_inc(g("scaled"), 1)
                if c >= 1:
                    dve.wait_ge(*g("hi", c))
                    nc.vector.tensor_tensor(ch(xn_lo, c - 1), ch(hn, (c - 1) % 2),
                                            ch(xn_hi, c - 1).bitcast(F32), ALU.subtract).then_inc(g("xn"), 1)

        def out_pe(pe, n, g, s0, rows, hi, lo, arrived):
            def body(i, q0):
                s = s0
                for q in range(2):
                    pe.wait_ge(*g("y_squares", 4 * i + 2 * q + 2))
                    for r, (k0, nk) in enumerate(rows):
                        products(pe, n, s, nk, [ps[:, 4 + 2 * q, :], ps[:, 5 + 2 * q, :]],
                                 lambda k: hi(k0 + k), lambda k: lo(k0 + k), r == 0, r == len(rows) - 1,
                                 arrived=(lambda k: arrived(k0 + k)))
                        s = 1 - s
            per = [len(rows), len(rows)]
            with pe.Fori(0, 2) as i:
                n.enter(i, per)
                body(i, 0)
            n.leave(2)
            pe.wait_ge(*g("y_sum", 2 + C))
            nc.tensor.matmul(ps[:, 0, :], ones_d[:], acc[:], start=True, stop=True).then_inc(g("y_mean"), 1)

        def out_uses(s0, rows):
            r = len(rows)
            return [((s0 + u) % 2, u // r if u % r == r - 1 else None) for u in range(2 * r)]

        def out_act(act, n, g, s0, rows, y, more):
            def body(i, last):
                for u, (s, panel) in enumerate(out_uses(s0, rows)):
                    if panel is not None:
                        if last and u == 2 * len(rows) - 1 and not more:
                            act.wait_ge(used[s], n.peek(s) + 1)
                        else:
                            wait_used(act, n, s)
                        for m in range(2):
                            c = 4 * i + 2 * panel + m
                            nc.scalar.activation(ch(y, c), ch(ps, 4 + 2 * panel + m), ACT.Copy)
                            act.wait_ge(*g("y_sum", c + 1))
                            nc.scalar.activation(ch(sq, m), ch(ps, 4 + 2 * panel + m),
                                                 ACT.Square).then_inc(g("y_squares"), 1)
                    if not (last and not more and u >= 2 * len(rows) - 2):
                        split_hi(act, n, s)
                    else:
                        n.next(s)
            loop2(act, n, [len(rows), len(rows)], body, more)
            act.wait_ge(*g("y_mean", 1))
            nc.scalar.activation(rstd[:], ps[:, 0, :], ACT.Ln, bias=eps_rms[:]).then_inc(g("y_log"), 1)
            act.wait_ge(*g("y_log", 1))
            nc.scalar.activation(rstd[:], rstd[:], ACT.Exp, scale=-0.5).then_inc(g("y_rstd"), 1)

        def loop2(eng, n, per, body, more):
            if more:
                with eng.Fori(0, 2) as i:
                    n.enter(i, per)
                    body(i, False)
                n.leave(2)
            else:
                for i in range(2):
                    n.enter(0, per)
                    body(i, i == 1)
                    n.leave(1)

        def out_dve(dve, n, g, s0, rows, y, gains, seen, more):
            def body(i, last):
                for u, (s, panel) in enumerate(out_uses(s0, rows)):
                    if panel is not None:
                        for m in range(2):
                            c = 4 * i + 2 * panel + m
                            dve.wait_ge(*g("y_squares", c + 5))
                            dve.wait_ge(*g("y_sum", c + 2))
                            nc.vector.tensor_tensor(acc[:], acc[:], sq[:, m, :],
                                                    ALU.add).then_inc(g("y_sum"), 1)
                    if not (last and not more and u >= 2 * len(rows) - 2):
                        split_lo(dve, n, s)
                    else:
                        n.next(s)
            loop2(dve, n, [len(rows), len(rows)], body, more)
            dve.wait_ge(*g("y_rstd", 1))
            for c in range(C + 1):
                if c < C:
                    if c >= 2:
                        dve.wait_ge(x_ready, seen + c - 1)
                    nc.vector.scalar_tensor_tensor(ch(hn, c % 2), ch(y, c), col(gains[0], gains[1] + c),
                                                   rstd[:], ALU.mult, ALU.mult).then_inc(g("y_scaled"), 1)
                if c >= 1:
                    dve.wait_ge(*g("y_scaled", c))
                    nc.vector.tensor_tensor(ch(x, c - 1), ch(x, c - 1), ch(hn, (c - 1) % 2),
                                            ALU.add).then_inc(x_ready, 1)

        def out_start(g):
            nc.vector.memset(acc[:], 0.0).then_inc(g("y_sum"), 2)

        def out_start_act(act, g):
            act.sem_inc(g("y_squares"), 4)

        FP = FC // 2
        HID_ROWS = groups_of(FC)

        def w_in_panel(l, f, half, j):
            w = a["ffn_w_in"][l, f].rearrange("(k p) n -> p k n", p=P)
            return w[:, :, bass.ds(j * PANEL + half * DFF, PANEL)]

        def out_panel(w, k0, nk, p):
            v = w.rearrange("(k p) n -> p k n", p=P)
            return v[:, k0:k0 + nk, bass.ds(p * PANEL, PANEL)]

        def out_sp(sp, n, s0, rows, w):
            with sp.Fori(0, 2) as i:
                n.enter(i, [len(rows), len(rows)])
                s = s0
                for q in range(2):
                    for k0, nk in rows:
                        load(sp, n, s, out_panel(w, k0, nk, 2 * i + q))
                        s = 1 - s
            n.leave(2)

        def ffn_sp(sp, n, l, f, s0):
            with sp.Fori(0, FP) as j:
                n.enter(j, [1, 1])
                load(sp, n, s0, w_in_panel(l, f, 0, j))
                load(sp, n, 1 - s0, w_in_panel(l, f, 1, j))
            n.leave(FP)
            out_sp(sp, n, s0, HID_ROWS, a["ffn_w_out"][l, f])

        def ffn_pe(pe, n, g, s0):
            norm_in_pe(pe, g)
            with pe.Fori(0, FP) as j:
                n.enter(j, [1, 1])
                pe.wait_ge(*g("silu", j + 1))
                products(pe, n, s0, PK, [ps[:, 0, :], ps[:, 1, :]], lambda k: xn_hi[:, k, :],
                         lambda k: xn_lo[:, k, :], True, True,
                         arrived=lambda k: pe.wait_ge(*g("xn", k + 1)))
                pe.wait_ge(*g("product", j + 1))
                products(pe, n, 1 - s0, PK, [ps[:, 2, :], ps[:, 3, :]], lambda k: xn_hi[:, k, :],
                         lambda k: xn_lo[:, k, :], True, True)
            n.leave(FP)
            out_pe(pe, n, g, s0, HID_ROWS, lambda k: hid_hi[:, k, :], lambda k: hid_lo[:, k, :],
                   lambda k: pe.wait_ge(*g("hid", k // 2 + 2)) if k % 2 == 0 else None)

        def ffn_act(act, n, g, s0, seen, more):
            act.sem_inc(g("silu"), 1)
            out_start_act(act, g)
            norm_in_squares(act, g, seen)
            norm_in_hi(act, g)
            with act.Fori(0, FP) as j:
                n.enter(j, [1, 1])
                wait_used(act, n, s0)
                act.wait_ge(*g("product", j + 1))
                nc.scalar.activation(ch(sil, 0), ch(ps, 0), ACT.Silu)
                nc.scalar.activation(ch(sil, 1), ch(ps, 1), ACT.Silu).then_inc(g("silu"), 1)
                split_hi(act, n, s0)
                split_hi(act, n, 1 - s0)
                act.wait_ge(*g("product", j + 2))
                nc.scalar.activation(ch(hid_hi, 2 * j), ch(hn, 0), ACT.Copy)
                nc.scalar.activation(ch(hid_hi, 2 * j + 1), ch(hn, 1), ACT.Copy).then_inc(g("hid_hi"), 1)
            n.leave(FP)
            out_act(act, n, g, s0, HID_ROWS, y_ffn, more)

        def ffn_dve(dve, n, g, s0, l, f, seen, more):
            dve.sem_inc(g("product"), 1)
            dve.sem_inc(g("hid"), 1)
            out_start(g)
            norm_in_dve(dve, g, l, 4 * f)
            with dve.Fori(0, FP) as j:
                n.enter(j, [1, 1])
                split_lo(dve, n, s0)
                wait_used(dve, n, 1 - s0)
                dve.wait_ge(*g("silu", j + 2))
                dve.wait_ge(*g("hid", j + 1))
                nc.vector.tensor_tensor(ch(hn, 0), ch(ps, 2), ch(sil, 0), ALU.mult)
                nc.vector.tensor_tensor(ch(hn, 1), ch(ps, 3), ch(sil, 1), ALU.mult).then_inc(g("product"), 1)
                split_lo(dve, n, 1 - s0)
                dve.wait_ge(*g("hid_hi", j + 1))
                nc.vector.tensor_tensor(ch(hid_lo, 2 * j), ch(hn, 0), ch(hid_hi, 2 * j).bitcast(F32),
                                        ALU.subtract)
                nc.vector.tensor_tensor(ch(hid_lo, 2 * j + 1), ch(hn, 1),
                                        ch(hid_hi, 2 * j + 1).bitcast(F32), ALU.subtract).then_inc(g("hid"), 1)
            n.leave(FP)
            out_dve(dve, n, g, s0, HID_ROWS, y_ffn, (vec_h, gain(l, 4 * f + 1, 0)), seen, more)

        HD, NKV, GRP, NB = 64, 4, 4, S // P
        QD = NKV * GRP * HD
        SCALE = HD ** -0.5
        KV_ROWS = groups_of(C)
        m_at = {"at": o_arena}

        def arena(name, shape, dt=F32):
            n_bytes = 4
            for d in shape[1:]:
                n_bytes *= d
            at = m_at["at"]
            m_at["at"] = at + (n_bytes + 31) // 32 * 32
            assert m_at["at"] <= o_arena + 2 * FC * S * 4, (name, m_at)
            return sb(name, shape, dt, at)

        o_hi = arena("o_hi", [P, C, S], F32R)
        o_lo = arena("o_lo", [P, C, S], F32R)
        kz = arena("kz", [P, NKV, NB, 2, P])
        v_sb = arena("v_sb", [P, NB, NKV * HD])
        v_g = arena("v_g", [P, NB, HD])
        q_rot = arena("q_rot", [P, 2, S])
        merged = arena("merged", [P, 2, GRP, P])
        prob = arena("prob", [P, 2, GRP, P])
        prob_t = arena("prob_t", [P, 2, 2, GRP, P])
        cos_t = arena("cos_t", [P, S])
        sin_t = arena("sin_t", [P, S])
        rot_m = arena("rot_m", [P, P])
        tri_i = arena("tri_i", [P, P], I32)
        tri_t = arena("tri_t", [P, P])
        tri_u = arena("tri_u", [P, P])
        v_bias = arena("v_bias", [P, NKV * HD])
        sink = arena("sink", [P, NKV * GRP])
        n_sink = arena("n_sink", [P, NKV * GRP])
        top = arena("top", [P, 2, GRP])
        n_top = arena("n_top", [P, 2, GRP])
        sink_d = arena("sink_d", [P, 2, GRP])
        den = arena("den", [P, 2, GRP])
        t1, t2 = sil[:, 0, :], sil[:, 1, :]
        ATT_CONST = [(cos_t, "cos"), (sin_t, "sin"), (rot_m, "rot_m"), (tri_i, "tri_i"), (tri_t, "tri_t"),
                     (tri_u, "tri_u")]

        def qkv_panel(p):
            return a["attn_w_qkv"][0].rearrange("(k p) n -> p k n", p=P)[:, :, bass.ds(p * PANEL, PANEL)]

        def attn_sp(sp, n, g, before, s0):
            load(sp, n, s0, qkv_panel(QD // PANEL))
            load(sp, n, 1 - s0, qkv_panel(QD // PANEL + 1))
            sp.wait_ge(*before("y_mean", 1))
            for t, name in ATT_CONST:
                sp.dma_start(t[:], a[name]).then_inc(g("const"), 16)
            sp.dma_start(v_bias[:], a["attn_b_qkv"][0:1, QD + NKV * HD:QD + 2 * NKV * HD]
                         .rearrange("o n -> (o n)").partition_broadcast(P)).then_inc(g("const"), 16)
            sp.dma_start(sink[:], a["attn_sinks"].rearrange("o n -> (o n)").partition_broadcast(P)
                         ).then_inc(g("const"), 16)
            wo = a["attn_w_o"][0]
            load(sp, n, s0, qkv_panel(0))
            load(sp, n, 1 - s0, out_panel(wo, 0, C, 0))
            with sp.Fori(1, NKV) as i:
                n.enter(i - 1, [1, 0] if s0 == 0 else [0, 1])
                load(sp, n, s0, qkv_panel(i))
            n.leave(NKV - 1)
            for p in range(1, D // PANEL):
                load(sp, n, s0 if p % 2 else 1 - s0, out_panel(wo, 0, C, p))

        ATT_CONSTS = 16 * (len(ATT_CONST) + 2)

        def attn_pe(pe, n, g, s0):
            pe.sem_inc(g("transposed"), 2)
            pe.sem_inc(g("weighed"), 2)
            norm_in_pe(pe, g)
            xh, xl = (lambda k: xn_hi[:, k, :]), (lambda k: xn_lo[:, k, :])
            products(pe, n, s0, C, [ps[:, 0, :], ps[:, 1, :]], xh, xl, True, True,
                     arrived=lambda k: pe.wait_ge(*g("xn", k + 1)))
            s = 1 - s0
            pe.wait_ge(lo_done[s], n.next(s) + 2)
            for t in range(NB):
                o = ps[:, 4 + t // 2, (t % 2) * PANEL:(t % 2 + 1) * PANEL]
                for k in range(C):
                    h, l = xn_hi[:, k, t * P:(t + 1) * P], xn_lo[:, k, t * P:(t + 1) * P]
                    nc.tensor.matmul(o, h, w_hi[:, s, k, :], start=k == 0, stop=False)
                    nc.tensor.matmul(o, h, w_lo[:, s, k, :], start=False, stop=False)
                    end = nc.tensor.matmul(o, l, w_hi[:, s, k, :], start=False, stop=k == C - 1)
            end.then_inc(used[s], 1)
            pe.wait_ge(*g("const", ATT_CONSTS))
            for m in range(2):
                pe.wait_ge(*g("linear", m + 1))
                nc.tensor.matmul(ps[:, 2 + m, :], rot_m[:], hn[:, m, :], start=True,
                                 stop=True).then_inc(g("rotated"), 1)

            def scores(i, b):
                if b >= 2:
                    pe.wait_ge(*g("merged", 4 * i + b - 1))
                for back in range(min(b, 1) + 1):
                    for m in range(2):
                        end = nc.tensor.matmul(ps[:, 4 + 2 * back + b % 2, m * 2 * P:(m + 1) * 2 * P],
                                               q_rot[:, m, b * P:(b + 1) * P],
                                               kz[:, bass.ds(i, 1), b - back, :, :], start=True, stop=True)
                end.then_inc(g("scored"), 1)

            def transposes(i, b):
                pe.wait_ge(*g("normed", 4 * i + b + 1))
                for h in range(GRP):
                    end = nc.tensor.transpose(ps[:, b % 2, h * P:(h + 1) * P], prob[:, b % 2, h, :], ident[:])
                end.then_inc(g("transposed"), 1)

            def values(i, b):
                pe.wait_ge(*g("prob_t", 4 * i + b + 1))
                pe.wait_ge(*g("o_done", 4 * i + b + 1))
                for par in range(2):
                    o = ps[par * HD:(par + 1) * HD, 2 + b % 2, 0:2 * P]
                    for back in range(min(b, 1) + 1):
                        end = nc.tensor.matmul(o, v_g[:, b - back, :], prob_t[:, b % 2, back, par::2, :],
                                               start=back == 0, stop=back == min(b, 1))
                end.then_inc(g("weighed"), 1)

            with pe.Fori(0, NKV) as i:
                n.enter(i, [1, 0] if s0 == 0 else [0, 1])
                products(pe, n, s0, C, [ps[:, 0, :], ps[:, 1, :]], xh, xl, True, True)
                pe.wait_ge(*g("kz", 2))
                pe.wait_ge(*g("o_done", 4 * i + 2))
                for m in range(2):
                    pe.wait_ge(*g("linear", 2 * i + 3 + m))
                    nc.tensor.matmul(ps[:, 2 + m, :], rot_m[:], hn[:, m, :], start=True,
                                     stop=True).then_inc(g("rotated"), 1)
                pe.wait_ge(*g("roped", 2 * i + 4))
                scores(i, 0)
                scores(i, 1)
                pe.wait_ge(*g("v_g", i + 1))
                for b in range(NB):
                    transposes(i, b)
                    if b + 2 < NB:
                        scores(i, b + 2)
                    values(i, b)
            n.leave(NKV)
            out_pe(pe, n, g, 1 - s0, KV_ROWS, lambda k: o_hi[:, k, :], lambda k: o_lo[:, k, :],
                   lambda k: pe.wait_ge(*g("o_done", 4 * (k // 2) + 6)) if k % 2 == 0 else None)

        def attn_act(act, n, g, s0, seen, more):
            out_start_act(act, g)
            act.sem_inc(g("exped"), 2)
            norm_in_squares(act, g, seen)
            norm_in_hi(act, g)
            wait_used(act, n, s0)
            act.wait_ge(*g("xn", C))
            for m in range(2):
                nc.scalar.activation(ch(hn, m), ch(ps, m), ACT.Identity,
                                     bias=col(vec_r, QD // P + m)).then_inc(g("linear"), 1)
            split_hi(act, n, s0)
            split_hi(act, n, 1 - s0)

            def previous(i, b):
                act.wait_ge(*g("scored", 4 * i + b + 1))
                act.wait_ge(*g("exped", 4 * i + b + 1))
                nc.scalar.activation(merged[:, b % 2, :, :], ps[:, 6 + b % 2, :].rearrange("p (h k) -> p h k", k=P),
                                     ACT.Copy).then_inc(g("previous"), 1)

            def exps(i, b):
                act.wait_ge(*g("n_top", 4 * i + b + 1))
                act.wait_ge(*g("transposed", 4 * i + b + 1))
                for h in range(GRP):
                    nc.scalar.activation(prob[:, b % 2, h, :], merged[:, b % 2, h, :], ACT.Exp,
                                         bias=n_top[:, b % 2, h:h + 1], scale=SCALE,
                                         accum_out=den[:, b % 2, h:h + 1])
                nc.scalar.activation(sink_d[:, b % 2, :], sink_d[:, b % 2, :], ACT.Exp).then_inc(g("exped"), 1)

            def out_hi(i, b):
                act.wait_ge(*g("weighed", 4 * i + b + 3))
                nc.scalar.activation(o_hi[:, bass.ds(2 * i, 2), b * P:(b + 1) * P],
                                     ps[:, 2 + b % 2, 0:2 * P].rearrange("p (m q) -> p m q", q=P),
                                     ACT.Copy).then_inc(g("o_hi"), 1)

            with act.Fori(0, NKV) as i:
                n.enter(i, [1, 0] if s0 == 0 else [0, 1])
                wait_used(act, n, s0)
                act.wait_ge(*g("roped", 2 * i + 2))
                for m in range(2):
                    nc.scalar.activation(ch(hn, m), ch(ps, m), ACT.Identity,
                                         bias=col(vec_r, 2 * i + m)).then_inc(g("linear"), 1)
                split_hi(act, n, s0)
                previous(i, 1)
                exps(i, 0)
                for b in range(1, NB):
                    if b + 1 < NB:
                        previous(i, b + 1)
                    exps(i, b)
                    out_hi(i, b - 1)
                out_hi(i, NB - 1)
            n.leave(NKV)
            out_act(act, n, g, 1 - s0, KV_ROWS, y_ffn, more)

        def rope(dve, g, at, m, write):
            dve.wait_ge(*g("rotated", at + 1))
            dve.wait_ge(*g("rope_free", at + 1))
            nc.vector.tensor_tensor(t1, hn[:, m, :], cos_t[:], ALU.mult)
            nc.vector.tensor_tensor(t2, ps[:, 2 + m, :], sin_t[:], ALU.mult).then_inc(g("turned"), 1)
            dve.wait_ge(*g("turned", at + 1))
            write()

        def attn_dve(dve, n, g, s0, seen, more):
            out_start(g)
            dve.sem_inc(g("o_done"), 2)
            dve.sem_inc(g("rope_free"), 1)
            norm_in_dve(dve, g, 0, 2)
            dve.wait_ge(*g("const", ATT_CONSTS))
            nc.vector.tensor_scalar(n_sink[:], sink[:], -1.0, None, ALU.mult).then_inc(g("n_sink"), 1)
            split_lo(dve, n, s0)
            wait_used(dve, n, 1 - s0)
            nc.vector.tensor_tensor(v_sb[:].rearrange("p (t u) n -> p t u n", t=2),
                                    ps[:, 4:6, :].rearrange("p t (u n) -> p t u n", u=2),
                                    v_bias[:].unsqueeze(1).unsqueeze(1).to_broadcast([P, 2, 2, NKV * HD]),
                                    ALU.add).then_inc(g("v"), 1)
            split_lo(dve, n, 1 - s0)
            dve.wait_ge(*g("kz_zero", 2))
            for m in range(2):
                def write():
                    for half in range(2):
                        at = slice(half * HD, (half + 1) * HD)
                        for par in range(2):
                            o = kz[par * HD:(par + 1) * HD, 2 * m + half, :, par, :]
                            end = nc.vector.tensor_tensor(
                                o, t1[at].rearrange("p (b k) -> p b k", k=P),
                                t2[at].rearrange("p (b k) -> p b k", k=P), ALU.add)
                            if half == 1 and par == 1:
                                end.then_inc(g("roped"), 1)
                            elif half == 1:
                                end.then_inc(g("kz_part"), 1)
                rope(dve, g, m, m, write)
                dve.wait_ge(*g("roped", m + 1))
                dve.sem_inc(g("kz"), 1)
                dve.sem_inc(g("rope_free"), 1)

            def merge(i, b):
                if b == 0:
                    dve.wait_ge(*g("cleared", i + 1))
                else:
                    dve.wait_ge(*g("previous", 3 * i + b))
                dve.wait_ge(*g("scored", 4 * i + b + 1))
                dve.sem_inc(g("merging"), 1)
                nc.vector.copy_predicated(merged[:, b % 2, :, :], tri_i[:].unsqueeze(1).to_broadcast([P, GRP, P]),
                                          ps[:, 4 + b % 2, :].rearrange("p (h k) -> p h k", k=P)
                                          ).then_inc(g("merged"), 1)
                dve.wait_ge(*g("merged", 4 * i + b + 1))
                nc.vector.reduce_max(top[:, b % 2, :], merged[:, b % 2, :, :], AX.X).then_inc(g("top"), 1)
                dve.wait_ge(*g("top", 4 * i + b + 1))
                nc.vector.scalar_tensor_tensor(n_top[:, b % 2, :], top[:, b % 2, :], -SCALE,
                                               n_sink[:, bass.ds(GRP * i, GRP)], ALU.mult,
                                               ALU.min).then_inc(g("n_top0"), 1)
                dve.wait_ge(*g("n_top0", 4 * i + b + 1))
                nc.vector.tensor_tensor(sink_d[:, b % 2, :], n_top[:, b % 2, :], sink[:, bass.ds(GRP * i, GRP)],
                                        ALU.add).then_inc(g("n_top"), 1)

            def normalize(i, b):
                dve.wait_ge(*g("exped", 4 * i + b + 3))
                nc.vector.tensor_tensor(den[:, b % 2, :], den[:, b % 2, :], sink_d[:, b % 2, :],
                                        ALU.add).then_inc(g("den"), 1)
                dve.wait_ge(*g("den", 4 * i + b + 1))
                nc.vector.reciprocal(top[:, b % 2, :], den[:, b % 2, :]).then_inc(g("rden"), 1)
                dve.wait_ge(*g("rden", 4 * i + b + 1))
                nc.vector.tensor_tensor(prob[:, b % 2, :, :], prob[:, b % 2, :, :],
                                        top[:, b % 2, :].unsqueeze(2).to_broadcast([P, GRP, P]),
                                        ALU.mult).then_inc(g("normed"), 1)

            def mask(i, b):
                dve.wait_ge(*g("transposed", 4 * i + b + 3))
                dve.wait_ge(*g("weighed", 4 * i + b + 1))
                pt = ps[:, b % 2, :].rearrange("p (h q) -> p h q", q=P)
                end = nc.vector.tensor_tensor(prob_t[:, b % 2, 0, :, :], pt,
                                              tri_t[:].unsqueeze(1).to_broadcast([P, GRP, P]), ALU.mult)
                if b > 0:
                    end = nc.vector.tensor_tensor(prob_t[:, b % 2, 1, :, :], pt,
                                                  tri_u[:].unsqueeze(1).to_broadcast([P, GRP, P]), ALU.mult)
                end.then_inc(g("prob_t"), 1)

            def out_low(i, b):
                dve.wait_ge(*g("o_hi", 4 * i + b + 1))
                at = (slice(None), bass.ds(2 * i, 2), slice(b * P, (b + 1) * P))
                nc.vector.tensor_tensor(o_lo[at], ps[:, 2 + b % 2, 0:2 * P].rearrange("p (m q) -> p m q", q=P),
                                        o_hi[at].bitcast(F32), ALU.subtract).then_inc(g("o_done"), 1)

            with dve.Fori(0, NKV) as i:
                n.enter(i, [1, 0] if s0 == 0 else [0, 1])
                for m in range(2):
                    def write():
                        nc.vector.tensor_tensor(q_rot[:, m, :], t1, t2, ALU.add).then_inc(g("roped"), 1)
                    rope(dve, g, 2 * i + 2 + m, m, write)
                    dve.wait_ge(*g("roped", 2 * i + 3 + m))
                    dve.sem_inc(g("rope_free"), 1)
                split_lo(dve, n, s0)
                merge(i, 0)
                for b in range(NB):
                    if b + 1 < NB:
                        merge(i, b + 1)
                    normalize(i, b)
                    if b >= 1:
                        out_low(i, b - 1)
                    mask(i, b)
                out_low(i, NB - 1)
            n.leave(NKV)
            out_dve(dve, n, g, 1 - s0, KV_ROWS, y_ffn, (vec_n, gain(0, 3, 0)), seen, more)

        def attn_pool(pool, g, before):
            pool.wait_ge(*before("y_mean", 1))
            for par in range(2):
                nc.gpsimd.memset(kz[(1 - par) * HD:(2 - par) * HD, :, :, par, :], 0.0).then_inc(g("kz_zero"), 1)
                pool.wait_ge(*g("kz_zero", par + 1))
            pool.wait_ge(*g("v", 1))
            with pool.Fori(0, NKV) as i:
                pool.wait_ge(*g("weighed", 4 * i + 2))
                nc.gpsimd.tensor_copy(v_g[:], v_sb[:, :, bass.ds(HD * i, HD)]).then_inc(g("v_g"), 1)
                pool.wait_ge(*g("v_g", i + 1))
                pool.wait_ge(*g("exped", 4 * i + 1))
                pool.sem_inc(g("clearing"), 1)
                nc.gpsimd.memset(merged[:, 0, :, :], -1e30).then_inc(g("cleared"), 1)
                pool.wait_ge(*g("cleared", i + 1))

        HEAD = 64
        LEVELS = P.bit_length() - 1
        UNITS = 2 * NB
        LORA = [("rwkv_w1", 64), ("rwkv_a1", 64), ("rwkv_g1", 160)]
        FILLS = 6
        DECAY = -math.exp(-0.5)
        V_MIX, V_W0 = 12, 12 + 6 * C
        V_A0, V_KK, V_KA, V_RK, V_LG, V_LB = (V_W0 + j * C for j in range(1, 7))

        m_at["at"] = o_arena
        h_pad = arena("h_pad", [P, C, S + 1])
        rkv = arena("rkv", [P, 3, C, S])
        y_rwkv = sb("y_rwkv", [P, C, S], F32, o_arena + C * (S + 1) * 4)
        sg = arena("sg", [P, 2, S])
        wa2 = arena("wa2", [P, 2, D])
        g2 = arena("g2", [P, 2, D])
        twa = sb("twa", [P, S], F32, take(S * 4))
        o_h = {"at": o_arena}

        def over(region, size, name, shape, dt=F32):
            n_bytes = 4
            for d in shape[1:]:
                n_bytes *= d
            at = region["at"]
            region["at"] = at + (n_bytes + 31) // 32 * 32
            assert region["at"] <= region.setdefault("end", at + size), name
            return sb(name, shape, dt, at)

        HB = C * (S + 1) * 4
        lvl = over(o_h, HB, "lvl", [P, LEVELS, P])
        low2 = over(o_h, HB, "low2", [P, 2, P])
        blk = over(o_h, HB, "blk", [P, 2, P])
        ind_b = over(o_h, HB, "ind_b", [P, D])
        ind_s = over(o_h, HB, "ind_s", [P, C, 2 * C])
        k_norm = over(o_h, HB, "k_norm", [P, S])
        wa_c = over(o_h, HB, "wa_c", [P, 2, P])
        g_c = over(o_h, HB, "g_c", [P, 2, P])
        ind_c = over(o_h, HB, "ind_c", [P, P])
        state = over(o_h, HB, "state", [P, HEAD])
        u0 = over(o_h, HB, "u0", [P, 2, HEAD])
        u = over(o_h, HB, "u", [P, 2, HEAD])
        mid = over(o_h, HB, "mid", [P, NB])
        n_mid = over(o_h, HB, "n_mid", [P, NB])
        carry = over(o_h, HB, "carry", [P, NB])
        o_r = {"at": o_raw}
        mb = over(o_r, 16384, "mb", [P, NB, 2, 2, P])
        mk = over(o_r, 16384, "mk", [P, NB, 2, 2, P])
        o_w = {"at": o_whi}
        inv = over(o_w, 32768, "inv", [P, UNITS, P])
        inv_t = over(o_w, 32768, "inv_t", [P, UNITS, P])
        pair = over(o_w, 32768, "pair", [P, UNITS, P])
        b_tok = over(o_w, 32768, "b_tok", [P, NB, P])
        k_tok = over(o_w, 32768, "k_tok", [P, NB, P])
        ar = over(o_w, 32768, "ar", [P, 2, NB, 2, P])
        bt = over(o_w, 32768, "bt", [P, S])
        kt = over(o_w, 32768, "kt", [P, S])
        v_tok = over(o_w, 32768, "v_tok", [P, NB, P])
        v_c = over(o_w, 32768, "v_c", [P, S])
        o_t = {"at": o_tmp}
        dl = over(o_t, 16384, "dl", [P, S])
        lc = over(o_t, 16384, "lc", [P, S])
        kk = over(o_t, 16384, "kk", [P, S])
        rate = over(o_t, 16384, "rate", [P, S])
        kp = over(o_t, 16384, "kp", [P, S])
        m1 = over(o_t, 16384, "m1", [P, S])
        m2 = over(o_t, 16384, "m2", [P, S])
        ex = sb("ex", [P, NB, P + 1], F32, take(NB * (P + 1) * 4))
        ones_row = sb("ones_row", [P, P], F32, take(P * 4))
        omka = sb("omka", [P, C], F32, take(C * 4))
        w0h = sb("w0h", [P, 2 * C], F32, take(2 * C * 4))
        eps_ln = sb("eps_ln", [P, 1], F32, take(32))
        assert start + place["at"] <= nc.sbuf_usable_end, (start, place, nc.sbuf_usable_end)
        R_CONST = [(lvl, "lvl"), (low2, "low2"), (blk, "blk"), (ind_b, "ind_b"), (ind_s, "ind_s")]

        def rkv_panel(i, p):
            return a["rwkv_w_rkv"][0].rearrange("i (k p) n -> i p k n", p=P)[bass.ds(i, 1), :, :,
                                                                           bass.ds(p * PANEL, PANEL)].rearrange(
                "i p k n -> (i p) k n")

        def rwkv_sp(sp, n, g, before, s0):
            for j, (name, cols) in enumerate(LORA):
                load(sp, n, (s0 + j) % 2, a[name][0].rearrange("(k p) n -> p k n", p=P), cols)
                if j == 1:
                    sp.wait_ge(*g("zeros", 4))
                    sp.dma_start(wa2[0:64, 0, :], a["rwkv_w2"][0]).then_inc(g("lora_in"), 16)
                    sp.dma_start(wa2[64:128, 1, :], a["rwkv_a2"][0]).then_inc(g("lora_in"), 16)
                    sp.dma_start(g2[:, 0, :], a["rwkv_g2"][0, 0:P, :]).then_inc(g("lora_in"), 16)
                    sp.dma_start(g2[0:32, 1, :], a["rwkv_g2"][0, P:P + 32, :]).then_inc(g("lora_in"), 16)
            with sp.Fori(0, 3) as i:
                n.enter(i, [2, 2])
                for p in range(D // PANEL):
                    load(sp, n, (s0 + 1 + p) % 2, rkv_panel(i, p))
            n.leave(3)
            sp.wait_ge(*g("mixed", 2 + C * FILLS))
            for t, name in R_CONST:
                sp.dma_start(t[:], a[name]).then_inc(g("const"), 16)
            sp.wait_ge(*g("gated_lo", C))
            for p in range(D // PANEL):
                load(sp, n, (s0 + 1 + p) % 2, out_panel(a["rwkv_w_o"][0], 0, C, p))

        R_CONSTS = 16 * len(R_CONST)
        xh, xl = (lambda k: xn_hi[:, k, :]), (lambda k: xn_lo[:, k, :])

        def rwkv_proj_pe(pe, n, g, s0):
            for f in range(3):
                b0 = (4, 6, 2)[f]
                nb = 2 if f == 2 else 1
                products(pe, n, (s0 + f) % 2, C, [ps[:, b0 + m, :] for m in range(nb)], xh, xl, True, True,
                         arrived=lambda k: pe.wait_ge(*g("mixed_lo", C * f + k + 3)), freed=g("freed"))
            with pe.Fori(0, 3) as i:
                n.enter(i, [2, 2])
                for p in range(D // PANEL):
                    b0 = 4 + 2 * (p % 2)
                    pe.wait_ge(*g("projected", 4 * i + p + 1))
                    products(pe, n, (s0 + 1 + p) % 2, C, [ps[:, b0, :], ps[:, b0 + 1, :]], xh, xl, True, True,
                             arrived=(lambda k: pe.wait_ge(*g("mixed_lo", C * i + 3 * C + k + 3))) if p == 0 else None,
                             freed=g("freed") if p == 3 else None)
            n.leave(3)

        def even(t, b):
            return t.rearrange("p (q two b) -> p q two b", two=2, b=b)[:, :, 0, :]

        def odd(t, b):
            return t.rearrange("p (q two b) -> p q two b", two=2, b=b)[:, :, 1, :]

        def rwkv_pe(pe, n, g, s0):
            norm_in_pe(pe, g)
            rwkv_proj_pe(pe, n, g, s0)
            pe.wait_ge(*g("const", R_CONSTS))
            for c in range(C):
                pe.wait_ge(*g("k_sq", c + 1))
                nc.tensor.matmul(ps[0:2 * C, 0, :], ind_s[:, c, :], (m1 if c % 2 == 0 else m2)[:], start=c == 0,
                                 stop=c == C - 1).then_inc(g("k_sums"), 1)
            pe.wait_ge(*g("k_norm", 1))
            pe.wait_ge(*g("lora_in", 64))
            with pe.Fori(0, C) as c:
                pe.wait_ge(*g("statics", 4 * c + 4))
                pe.wait_ge(*g("chunk", c + 1))
                nc.tensor.matmul(ps[:, 0, :], wa_c[:, 0, :], twa[:], start=True, stop=True).then_inc(g("pre"), 1)
                nc.tensor.matmul(ps[:, 1, :], wa_c[:, 1, :], twa[:], start=True, stop=True).then_inc(g("pre"), 1)
                nc.tensor.matmul(ps[:, 3, :], ind_c[:], k_norm[:], start=True, stop=True).then_inc(g("pre"), 1)
                nc.tensor.matmul(ps[:, 2, :], g_c[:, 0, :], sg[:, 0, :], start=True, stop=False)
                nc.tensor.matmul(ps[:, 2, :], g_c[:, 1, :], sg[:, 1, :], start=False, stop=True).then_inc(g("pre"), 1)
                for j, t in enumerate((v_c, kt, bt)):
                    if j == 1:
                        pe.wait_ge(*g("kb", c + 1))
                    for blkn in range(NB):
                        end = nc.tensor.transpose(ps[:, 4 + j, blkn * P:(blkn + 1) * P],
                                                  t[:, blkn * P:(blkn + 1) * P], ident[:])
                    end.then_inc(g("tok"), 1)
                pe.wait_ge(*g("ar", c + 1))
                for j in range(2 * NB):
                    blkn, t = j // 2, (bt, kt)[j % 2]
                    if j in (1, 2, 3):
                        pe.wait_ge(*g("tok_sb", 3 * c + 3))
                    if j >= 4:
                        pe.wait_ge(*g("masked", 8 * c + j - 3))
                    nc.tensor.matmul(ps[:, 4 + (j + 3) % 4, :], t[:, blkn * P:(blkn + 1) * P], ar[:, :, blkn, :, :],
                                     start=True, stop=True).then_inc(g("attn"), 1)
                pe.wait_ge(*g("bonus_in", c + 1))
                nc.tensor.matmul(ps[:, 3, :], blk[:, 0, :], m2[:], start=True, stop=True).then_inc(g("bonus"), 1)
                pe.wait_ge(*g("masked", 8 * c + 8))
                pe.wait_ge(*g("inv_start", 2 * c + 2))
                for l in range(LEVELS):
                    b = 1 << l
                    for G in range(2):
                        if l > 0:
                            pe.wait_ge(*g("inv", (LEVELS * 2) * c + 2 * (l - 1) + G + 1))
                        for w in range(4):
                            un = 4 * G + w
                            end = nc.tensor.matmul(ps[:, 4 + G, w * P:(w + 1) * P], mb[:, un // 2, un % 2, 0, :],
                                                   inv[:, un, :], start=True, stop=True)
                        end.then_inc(g("x_mm"), 1)
                    for G in range(2):
                        pe.wait_ge(*g("x_sb", (LEVELS * 2) * c + 2 * l + G + 1))
                        for w in range(4):
                            un = 4 * G + w
                            if l < LEVELS - 1:
                                nc.tensor.matmul(ps[:, 6 + G, w * HEAD:(w + 1) * HEAD], inv_t[:, un, :],
                                                 even(pair[:, un, :], b), start=True, stop=True)
                            end = nc.tensor.matmul(ps[:, 6 + G, 256 + w * HEAD:256 + (w + 1) * HEAD], pair[:, un, :],
                                                   odd(inv_t[:, un, :], b), start=True, stop=True)
                        end.then_inc(g("upd"), 1)
                pe.wait_ge(*g("inv", (LEVELS * 2) * c + LEVELS * 2))
                for t in range(NB):
                    pe.wait_ge(*g("state", (NB + 1) * c + t + 1))
                    for h in range(2):
                        o = ps[:, 0, h * HEAD:(h + 1) * HEAD]
                        nc.tensor.matmul(o, ar[:, h, t, 0, :], state[:], start=True, stop=False)
                        end = nc.tensor.matmul(o, mk[:, t, h, 0, :], v_tok[:, t, h * HEAD:(h + 1) * HEAD],
                                               start=False, stop=True)
                    end.then_inc(g("u0_mm"), 1)
                    pe.wait_ge(*g("u0", NB * c + t + 1))
                    for h in range(2):
                        end = nc.tensor.matmul(ps[:, 1, h * HEAD:(h + 1) * HEAD], inv_t[:, 2 * t + h, :], u0[:, h, :],
                                               start=True, stop=True)
                    end.then_inc(g("u_mm"), 1)
                    pe.wait_ge(*g("u", NB * c + t + 1))
                    for h in range(2):
                        o = ps[h * HEAD:(h + 1) * HEAD, 0, 256:256 + HEAD]
                        vt = v_tok[:, t, h * HEAD:(h + 1) * HEAD]
                        nc.tensor.matmul(o, b_tok[:, t, h * HEAD:(h + 1) * HEAD], u[:, h, :], start=True, stop=False)
                        nc.tensor.matmul(o, k_tok[:, t, h * HEAD:(h + 1) * HEAD], vt, start=False, stop=True)
                    for h in range(2):
                        o = ps[h * HEAD:(h + 1) * HEAD, 4, t * P:(t + 1) * P]
                        vt = v_tok[:, t, h * HEAD:(h + 1) * HEAD]
                        nc.tensor.matmul(o, state[:], ar[:, h, t, 1, :], start=True, stop=False)
                        nc.tensor.matmul(o, u[:, h, :], mb[:, t, h, 1, :], start=False, stop=False)
                        end = nc.tensor.matmul(o, vt, mk[:, t, h, 1, :], start=False, stop=True)
                    end.then_inc(g("y_mm"), 1)
                pe.wait_ge(*g("y_sb", c + 1))
                nc.tensor.matmul(ps[:, 5, :], blk[:, 1, :], kk[:], start=True, stop=True).then_inc(g("stat"), 1)
                pe.wait_ge(*g("dev_sq", c + 1))
                nc.tensor.matmul(ps[:, 6, :], blk[:, 1, :], dl[:], start=True, stop=True).then_inc(g("stat"), 1)
            pe.wait_ge(*g("gated_lo", C))
            out_pe(pe, n, g, (s0 + 1) % 2, KV_ROWS, xh, xl, lambda k: None)

        def rwkv_act(act, n, g, s0, seen, more):
            out_start_act(act, g)
            norm_in_squares(act, g, seen)

            def fill(f, s_last):
                for c in range(C):
                    act.wait_ge(*g("mixed", C * f + c + 3))
                    if not isinstance(f, int) or f > 0:
                        if c < C - 1:
                            act.wait_ge(*g("freed", (C - 1) * f + c + 1 - (C - 1)))
                        else:
                            wait_used(act, n, s_last)
                    nc.scalar.activation(ch(xn_hi, c), ch(hn, c % 2), ACT.Copy).then_inc(g("mixed_hi"), 1)

            fill(0, None)
            for f in range(3):
                s = (s0 + f) % 2
                fill(f + 1, s)
                wait_used(act, n, s)
                if f == 0:
                    nc.scalar.activation(twa[0:64, :], ps[0:64, 4, :], ACT.Tanh).then_inc(g("lora"), 1)
                elif f == 1:
                    nc.scalar.activation(twa[64:128, :], ps[0:64, 6, :], ACT.Copy).then_inc(g("projected"), 2)
                else:
                    act.wait_ge(*g("zeros", 4))
                    nc.scalar.activation(sg[:, 0, :], ps[:, 2, :], ACT.Tanh, scale=0.5)
                    nc.scalar.activation(sg[0:32, 1, :], ps[0:32, 3, :], ACT.Tanh, scale=0.5).then_inc(g("lora"), 1)
                split_hi(act, n, s)

            def project(i, p, split):
                s = (s0 + 1 + p) % 2
                b0 = 4 + 2 * (p % 2)
                act.wait_ge(used[s], n.peek(s) + 1)
                for m in range(2):
                    end = nc.scalar.activation(rkv[:, bass.ds(i, 1), 2 * p + m, :], ch(ps, b0 + m), ACT.Copy)
                end.then_inc(g("projected"), 1)
                if split:
                    split_hi(act, n, s)
            with act.Fori(0, 2) as i:
                n.enter(i, [2, 2])
                for p in range(4):
                    if p == 3:
                        fill(i + 4, s0 % 2)
                    project(i, p, True)
            n.leave(2)
            for p in range(4):
                project(2, p, p < 2)
            act.wait_ge(*g("const", R_CONSTS))
            act.wait_ge(*g("projected", 2 + 12))
            act.wait_ge(*g("mixed_lo", 2 + C * FILLS))
            for c in range(C):
                if c >= 2:
                    act.wait_ge(*g("k_sums", c - 1))
                nc.scalar.activation((m1 if c % 2 == 0 else m2)[:], rkv[:, 1, c, :], ACT.Square,
                                     scale=col(vec_r, V_KK + c)).then_inc(g("k_sq"), 1)
            act.wait_ge(*g("k_sums", C))
            act.wait_ge(*g("k_zero", 1))
            nc.scalar.activation(k_norm[0:2 * C, :], ps[0:2 * C, 0, :], ACT.Sqrt).then_inc(g("k_len"), 1)
            with act.Fori(0, C) as c:
                act.wait_ge(*g("pre", 4 * c + 1))
                act.wait_ge(*g("chunk", c + 1))
                nc.scalar.activation(dl[:], ps[:, 0, :], ACT.Tanh, bias=col(w0h, c), scale=0.5).then_inc(g("gates"), 1)
                act.wait_ge(*g("pre", 4 * c + 2))
                nc.scalar.activation(rate[:], ps[:, 1, :], ACT.Tanh, bias=col(w0h, c + C), scale=0.5).then_inc(g("gates"), 1)
                act.wait_ge(*g("sums", c + 1))
                nc.scalar.activation(ex[:, :, 1:P + 1], lc[:].rearrange("p (b t) -> p b t", t=P), ACT.Exp)
                nc.scalar.activation(ex[:, :, 0:1], n_mid[:].unsqueeze(2), ACT.Exp)
                nc.scalar.activation(carry[:], carry[:], ACT.Exp).then_inc(g("exps"), 1)
                act.wait_ge(*g("exps", 2 * c + 1))
                nc.scalar.activation(lc[:], lc[:], ACT.Exp, scale=-1.0).then_inc(g("exps"), 1)
                for j, t in enumerate((v_tok, k_tok, b_tok)):
                    act.wait_ge(*g("tok", 3 * c + j + 1))
                    nc.scalar.activation(t[:], ps[:, 4 + j, :].rearrange("p (b t) -> p b t", t=P),
                                         ACT.Copy).then_inc(g("tok_sb"), 1)
                for t in range(NB):
                    act.wait_ge(*g("u0_mm", NB * c + t + 1))
                    nc.scalar.activation(u0[:], ps[:, 0, 0:P].rearrange("p (h v) -> p h v", h=2),
                                         ACT.Copy).then_inc(g("u0"), 1)
                    act.wait_ge(*g("u_mm", NB * c + t + 1))
                    if t > 0:
                        act.wait_ge(*g("y_mm", NB * c + t))
                    nc.scalar.activation(u[:], ps[:, 1, 0:P].rearrange("p (h v) -> p h v", h=2),
                                         ACT.Copy).then_inc(g("u"), 1)
                act.wait_ge(*g("y_mm", NB * c + NB))
                nc.scalar.activation(kk[:], ps[:, 4, :], ACT.Copy).then_inc(g("y_sb"), 1)
                act.wait_ge(*g("dev", c + 1))
                nc.scalar.activation(dl[:], rate[:], ACT.Square).then_inc(g("dev_sq"), 1)
                act.wait_ge(*g("stat", 2 * c + 2))
                nc.scalar.activation(kp[:], ps[:, 6, :], ACT.Ln, bias=eps_ln[:]).then_inc(g("var_log"), 1)
                act.wait_ge(*g("var_log", c + 1))
                nc.scalar.activation(kp[:], kp[:], ACT.Exp, scale=-0.5).then_inc(g("dev_rstd"), 1)
                act.wait_ge(*g("gated", c + 1))
                nc.scalar.activation(ch(xn_hi, c), m1[:].unsqueeze(1), ACT.Copy).then_inc(g("gated_hi"), 1)
            for s in ((s0 + 1) % 2, s0):
                split_hi(act, n, s)
            out_act(act, n, g, (s0 + 1) % 2, KV_ROWS, y_rwkv, more)

        def rwkv_dve(dve, n, g, s0, seen, more):
            dve.sem_inc(g("mixed"), 2)
            dve.sem_inc(g("mixed_lo"), 2)
            dve.wait_ge(*g("rstd", 1))
            nc.vector.memset(h_pad[:, :, 0:1], 0.0)
            for c in range(C):
                nc.vector.scalar_tensor_tensor(h_pad[:, c, 1:S + 1], x[:, c, :], col(vec_n, gain(1, 2, c)),
                                               rstd[:], ALU.mult, ALU.mult).then_inc(g("h"), 1)
            dve.wait_ge(*g("h", C))

            def fill(f):
                for c in range(C + 1):
                    if c < C:
                        dve.wait_ge(*g("xx", C * f + c + 1))
                        dve.wait_ge(*g("mixed_lo", C * f + c + 1))
                        nc.vector.scalar_tensor_tensor(hn[:, c % 2, :], sil[:, c % 2, :],
                                                       col(vec_r, C * f + (V_MIX + c)), h_pad[:, c, 1:S + 1],
                                                       ALU.mult, ALU.add).then_inc(g("mixed"), 1)
                    if c >= 1:
                        dve.wait_ge(*g("mixed_hi", C * f + c))
                        nc.vector.tensor_tensor(ch(xn_lo, c - 1), ch(hn, (c - 1) % 2),
                                                ch(xn_hi, c - 1).bitcast(F32), ALU.subtract).then_inc(g("mixed_lo"), 1)

            fill(0)
            for f in range(3):
                fill(f + 1)
                if f == 2:
                    dve.wait_ge(*g("lora", 2))
                    nc.vector.tensor_scalar(sg[:, 0, :], sg[:, 0, :], 0.5, 0.5, ALU.mult, ALU.add)
                    nc.vector.tensor_scalar(sg[0:32, 1, :], sg[0:32, 1, :], 0.5, 0.5, ALU.mult,
                                            ALU.add).then_inc(g("sg"), 1)
                split_lo(dve, n, (s0 + f) % 2)
            with dve.Fori(0, 2) as i:
                n.enter(i, [2, 2])
                for p in range(4):
                    if p == 3:
                        fill(i + 4)
                    split_lo(dve, n, (s0 + 1 + p) % 2)
            n.leave(2)
            for p in range(4):
                if p < 2:
                    split_lo(dve, n, (s0 + 1 + p) % 2)
            nc.vector.tensor_scalar(omka[:], vec_r[:, V_KA:V_KA + C], -1.0, 1.0, ALU.mult, ALU.add)
            nc.vector.tensor_scalar(w0h[:], vec_r[:, V_W0:V_W0 + 2 * C], 0.5, None, ALU.mult)
            nc.vector.memset(ones_row[:], 1.0)
            nc.vector.memset(eps_ln[:], 64e-5).then_inc(g("tables"), 1)
            dve.wait_ge(*g("tables", 1))
            dve.wait_ge(*g("k_len", 1))
            nc.vector.tensor_scalar(k_norm[0:2 * C, :], k_norm[0:2 * C, :], 1e-12, None, ALU.max).then_inc(g("k_max"), 1)
            dve.wait_ge(*g("k_max", 1))
            nc.vector.reciprocal(k_norm[0:2 * C, :], k_norm[0:2 * C, :]).then_inc(g("k_norm"), 1)
            dve.wait_ge(*g("ar_zero", 2))
            dve.sem_inc(g("chunk"), 1)
            V = nc.vector
            b_t = lambda t: t.rearrange("p (b t) -> p b t", t=P)
            STEPS = 14
            with dve.Fori(0, C) as c:
                done = [0]

                def step(ins):
                    done[0] += 1
                    ins.then_inc(g("steps"), 1)
                    dve.wait_ge(*g("steps", STEPS * c + done[0]))

                r_c, k_c, vv_c = (rkv[:, j, bass.ds(c, 1), :].rearrange("p o t -> p (o t)") for j in range(3))
                V.memset(state[:], 0.0).then_inc(g("state"), 1)
                dve.wait_ge(*g("gates", 2 * c + 1))
                step(V.tensor_scalar(dl[:], dl[:], 0.5 * DECAY, 0.5 * DECAY, ALU.mult, ALU.add))
                for t in range(NB):
                    ins = V.tensor_tensor_scan(lc[:, t * P:(t + 1) * P], ones_row[:], dl[:, t * P:(t + 1) * P], 0.0,
                                               ALU.mult, ALU.add)
                step(ins)
                V.tensor_copy(mid[:].unsqueeze(2), b_t(lc[:])[:, :, P // 2 - 1:P // 2])
                step(V.tensor_scalar(n_mid[:].unsqueeze(2), b_t(lc[:])[:, :, P // 2 - 1:P // 2], -1.0, None, ALU.mult))
                step(V.tensor_tensor(b_t(lc[:]), b_t(lc[:]), n_mid[:].unsqueeze(2).to_broadcast([P, NB, P]), ALU.add))
                V.tensor_copy(carry[:, NB - 1:NB], lc[:, S - 1:S])
                V.tensor_tensor(carry[:, 0:NB - 1].unsqueeze(2), b_t(lc[:])[:, 0:NB - 1, P - 1:P],
                                mid[:, 1:NB].unsqueeze(2), ALU.add).then_inc(g("sums"), 1)
                dve.wait_ge(*g("gates", 2 * c + 2))
                step(V.tensor_scalar(rate[:], rate[:], 0.5, 0.5, ALU.mult, ALU.add))
                dve.wait_ge(*g("pre", 4 * c + 3))
                V.scalar_tensor_tensor(kk[:], k_c, col(vec_r, V_KK + c), ps[:, 3, :], ALU.mult, ALU.mult)
                step(V.tensor_scalar(kp[:], rate[:], col(vec_r, V_KA + c), col(omka, c), ALU.mult, ALU.add))
                V.tensor_tensor(m1[:], kk[:], rate[:], ALU.mult)
                step(V.tensor_tensor(kp[:], kp[:], k_c, ALU.mult))
                dve.wait_ge(*g("exps", 2 * c + 2))
                V.tensor_tensor(kt[:], kp[:], lc[:], ALU.mult)
                V.tensor_tensor(bt[:], m1[:], lc[:], ALU.mult).then_inc(g("kb"), 1)
                for h in range(2):
                    at = slice(h * HEAD, (h + 1) * HEAD)
                    V.scalar_tensor_tensor(ar[at, h, :, 0, :], b_t(kk[at]), -1.0, ex[at, :, 0:P], ALU.mult, ALU.mult)
                    ins = V.tensor_tensor(ar[at, h, :, 1, :], b_t(rkv[at, 0, bass.ds(c, 1), :].rearrange(
                        "p o t -> p (o t)")), ex[at, :, 1:P + 1], ALU.mult)
                ins.then_inc(g("ar"), 1)
                V.scalar_tensor_tensor(m2[:], r_c, col(vec_r, V_RK + c), kp[:], ALU.mult, ALU.mult).then_inc(g("bonus_in"), 1)
                for j in range(2 * NB):
                    dve.wait_ge(*g("attn", 8 * c + j + 1))
                    V.tensor_tensor((mb, mk)[j % 2][:, j // 2, :, :, :],
                                    ps[:, 4 + (j + 3) % 4, :].rearrange("p (h a t) -> p h a t", h=2, a=2),
                                    low2[:].unsqueeze(1).to_broadcast([P, 2, 2, P]), ALU.mult).then_inc(g("masked"), 1)
                for l in range(LEVELS):
                    b = 1 << l
                    for G in range(2):
                        us = slice(4 * G, 4 * G + 4)
                        dve.wait_ge(*g("x_mm", 2 * LEVELS * c + 2 * l + G + 1))
                        V.tensor_tensor(pair[:, us, :], ps[:, 4 + G, :].rearrange("p (w t) -> p w t", t=P),
                                        lvl[:, l, :].unsqueeze(1).to_broadcast([P, 4, P]), ALU.mult
                                        ).then_inc(g("x_sb"), 1)
                    for G in range(2):
                        dve.wait_ge(*g("upd", 2 * LEVELS * c + 2 * l + G + 1))
                        split = lambda t, par: t.rearrange("p w (q two b) -> p w q two b", two=2, b=b)[:, :, :, par, :]
                        mm = lambda at: ps[:, 6 + G, at:at + 256].rearrange("p (w q b) -> p w q b", w=4, b=b)
                        us = slice(4 * G, 4 * G + 4)
                        if l < LEVELS - 1:
                            V.tensor_tensor(split(inv[:, us, :], 0), split(inv[:, us, :], 0), mm(0), ALU.add)
                        V.tensor_tensor(split(inv_t[:, us, :], 1), split(inv_t[:, us, :], 1), mm(256),
                                        ALU.add).then_inc(g("inv"), 1)
                    dve.wait_ge(*g("inv", 2 * LEVELS * c + 2 * l + 2))
                for t in range(NB):
                    dve.wait_ge(*g("y_mm", NB * c + t + 1))
                    step(V.tensor_tensor(state[:], state[:], ps[:, 0, 256:256 + HEAD], ALU.add))
                    V.tensor_scalar(state[:], state[:], carry[:, t:t + 1], None, ALU.mult).then_inc(g("state"), 1)
                    dve.wait_ge(*g("state", (NB + 1) * c + t + 2))
                dve.wait_ge(*g("stat", 2 * c + 1))
                V.tensor_tensor(rate[:], kk[:], ps[:, 5, :], ALU.subtract).then_inc(g("dev"), 1)
                dve.wait_ge(*g("dev_rstd", c + 1))
                dve.wait_ge(*g("bonus", c + 1))
                step(V.tensor_tensor(m1[:], rate[:], kp[:], ALU.mult))
                V.tensor_tensor(m2[:], vv_c, ps[:, 3, :], ALU.mult)
                step(V.tensor_scalar(m1[:], m1[:], col(vec_r, V_LG + c), col(vec_r, V_LB + c), ALU.mult, ALU.add))
                step(V.tensor_tensor(m1[:], m1[:], m2[:], ALU.add))
                dve.wait_ge(*g("pre", 4 * c + 4))
                V.tensor_tensor(m1[:], m1[:], ps[:, 2, :], ALU.mult).then_inc(g("gated"), 1)
                dve.wait_ge(*g("gated_hi", c + 1))
                V.tensor_tensor(ch(xn_lo, c), m1[:].unsqueeze(1), ch(xn_hi, c).bitcast(F32),
                                ALU.subtract).then_inc(g("gated_lo"), 1)
                dve.wait_ge(*g("gated_lo", c + 1))
                dve.sem_inc(g("chunk"), 1)
                used_steps.append(done[0])
            assert used_steps[-1] == STEPS, used_steps
            out_start(g)
            for s in ((s0 + 1) % 2, s0):
                split_lo(dve, n, s)
            out_dve(dve, n, g, (s0 + 1) % 2, KV_ROWS, y_rwkv, (vec_n, gain(1, 3, 0)), seen, more)

        used_steps = []

        def rwkv_pool(pool, g, before):
            pool.wait_ge(*before("y_mean", 1))
            for j, t in enumerate((wa2, g2, sg)):
                nc.gpsimd.memset(t[:], 0.0).then_inc(g("zeros"), 1)
                pool.wait_ge(*g("zeros", j + 1))
            pool.sem_inc(g("zeros"), 1)
            pool.wait_ge(*g("h", C))
            with pool.Fori(0, FILLS) as f:
                for c in range(C):
                    pool.wait_ge(*g("mixed", C * f + c + 1))
                    nc.gpsimd.tensor_tensor(sil[:, c % 2, :], h_pad[:, c, 0:S], h_pad[:, c, 1:S + 1],
                                            ALU.subtract).then_inc(g("xx"), 1)
                    pool.wait_ge(*g("xx", C * f + c + 1))
            pool.wait_ge(*g("const", R_CONSTS))
            pool.wait_ge(*g("mixed_lo", 2 + C * FILLS))
            nc.gpsimd.memset(k_norm[:], 0.0).then_inc(g("k_zero"), 1)
            pool.wait_ge(*g("k_zero", 1))
            pool.wait_ge(*g("projected", 14))
            for h in range(2):
                nc.gpsimd.memset(ar[(1 - h) * HEAD:(2 - h) * HEAD, h, :, :, :], 0.0).then_inc(g("ar_zero"), 1)
                pool.wait_ge(*g("ar_zero", h + 1))
            pool.wait_ge(*g("lora_in", 64))
            with pool.Fori(0, C) as c:
                pool.wait_ge(*g("chunk", c + 1))
                copies = [(wa_c[:], wa2[:, :, bass.ds(c * P, P)]), (g_c[:], g2[:, :, bass.ds(c * P, P)]),
                          (ind_c[:], ind_b[:, bass.ds(c * P, P)]), (v_c[:].unsqueeze(1), rkv[:, 2, bass.ds(c, 1), :])]
                for j, (o, i) in enumerate(copies):
                    nc.gpsimd.tensor_copy(o, i).then_inc(g("statics"), 1)
                    pool.wait_ge(*g("statics", 4 * c + j + 1))
                for j, t in enumerate((inv, inv_t)):
                    pool.sem_inc(g("copying"), 1)
                    nc.gpsimd.tensor_copy(t[:], ident[:].unsqueeze(1).to_broadcast([P, UNITS, P])
                                          ).then_inc(g("inv_start"), 1)
                    pool.wait_ge(*g("inv_start", 2 * c + j + 1))

        st = signals("start")
        fin = signals("end")

        def start_sp(sp):
            sp.dma_start(ident[:], a["consts"][:, 0:P]).then_inc(consts_in, 16)
            sp.dma_start(ones_d[:], a["consts"][:, P:2 * P]).then_inc(consts_in, 16)
            sp.dma_start(rows_n[:], a["norm_g"].rearrange("l i (c p) -> (l i c) p", p=P)).then_inc(consts_in, 16)
            at = 0
            for name in [r for n in ROWS for r in (MIXES if n == "rwkv_mix" else [n])]:
                if isinstance(name, int):
                    v = a["rwkv_mix"][0, name:name + 1].rearrange("m (c p) -> (m c) p", p=P)
                    sp.dma_start(rows_r[at:at + C, :], v).then_inc(consts_in, 16)
                    at += C
                    continue
                v = a[name].rearrange(VIEWS.get(name, "o (c p) -> (o c) p"), **({"h": 2} if name == "rwkv_r_k" else {"p": P}))
                sp.dma_start(rows_r[at:at + v.shape[0], :], v).then_inc(consts_in, 16)
                at += v.shape[0]
            sp.dma_start(xt[:], a["x"].rearrange("b (t p) d -> p (b t) d", p=P)).then_inc(x_in, 16)

        def start_pe(pe):
            pe.wait_ge(consts_in, 48 + 16 * (len(ROWS) + 5))
            pe.wait_ge(x_in, 16)
            for c in range(C):
                if c >= 6:
                    pe.wait_ge(x_ready, c - 5)
                for t in range(S // P):
                    end = nc.tensor.transpose(ps[:, c % 6, t * P:(t + 1) * P], xt[:, t, c * P:(c + 1) * P], ident[:])
                end.then_inc(st("x"), 1)
            nr = 2 * NG * C
            nc.tensor.transpose(ps[:, 6, 0:nr], rows_n[:], ident[0:nr, 0:nr]).then_inc(st("vec"), 1)
            nc.tensor.transpose(ps[:, 7, 0:N_ROWS], rows_r[0:N_ROWS, :], ident[0:N_ROWS, 0:N_ROWS]).then_inc(st("vec"), 1)
            pe.wait_ge(x_ready, C)

        def start_dve(dve):
            for s in range(2):
                dve.sem_inc(lo_done[s], 1)
            nc.vector.memset(eps_rms[:], 1e-6).then_inc(st("eps"), 1)
            for c in range(C):
                dve.wait_ge(*st("x", c + 1))
                nc.vector.tensor_copy(ch(x, c), ch(ps, c % 6)).then_inc(x_ready, 1)
            dve.wait_ge(*st("vec", 2))
            nc.vector.tensor_copy(vec_r[:, 0:N_ROWS], ps[:, 7, 0:N_ROWS]).then_inc(st("vecs"), 1)
            nr = 2 * NG * C
            nc.vector.tensor_copy(vec_n[:, 0:nr], ps[:, 6, 0:nr])
            nc.vector.tensor_scalar(vec_h[:, 0:nr], ps[:, 6, 0:nr], 0.5, None, ALU.mult).then_inc(st("vecs"), 1)
            dve.wait_ge(*st("vecs", 2))
            n_dve = SlotCount()
            for s in range(2):
                split_lo(dve, n_dve, s)
            return n_dve

        def start_act(act):
            n_act = SlotCount()
            act.wait_ge(*st("eps", 1))
            for s in range(2):
                split_hi(act, n_act, s)
            return n_act

        def end_pe(pe, seen):
            for c in range(C):
                pe.wait_ge(x_ready, seen + c + 1)
                for t in range(S // P):
                    b = 2 * t + c // 4
                    end = nc.tensor.transpose(ps[:, b, (c % 4) * P:(c % 4 + 1) * P], x[:, c, t * P:(t + 1) * P],
                                              ident[:])
                end.then_inc(fin("x"), 1)

        def end_evac(eng, copy, t, g):
            eng.wait_ge(*fin("x", C))
            for h in range(2):
                end = copy(ot[:, t, h * 512:(h + 1) * 512], ps[:, 2 * t + h, :])
                end.then_inc(g, 1)

        def end_sp(sp):
            o = out.rearrange("b (t p) d -> p (b t) d", p=P)
            for t in range(S // P):
                sp.wait_ge(*fin(f"done{t % 2}", 2 * (t // 2 + 1)))
                sp.dma_start(o[:, t:t + 1, :], ot[:, t:t + 1, :]).then_inc(out_done, 16)
            sp.wait_ge(out_done, 16 * (S // P))

        sig = {name: signals(name, stages[:e]) for e, name in enumerate(stages)}
        layer = {"ffn0a": (0, 0), "ffn0b": (0, 1), "ffn1a": (1, 0), "ffn1b": (1, 1)}
        slot0 = {}
        s = 0
        for name in stages:
            slot0[name] = s
            if name == "rwkv":
                s = 1 - s
        block = ctx.enter_context(nc.Block())

        @block.sync
        def _(sp):
            start_sp(sp)
            n = SlotCount()
            for e, name in enumerate(stages):
                if name in layer:
                    ffn_sp(sp, n, *layer[name], slot0[name])
                if name == "attn":
                    attn_sp(sp, n, sig[name], sig[stages[e - 1]], slot0[name])
                if name == "rwkv":
                    rwkv_sp(sp, n, sig[name], sig[stages[e - 1]], slot0[name])
            end_sp(sp)

        @block.scalar
        def _(act):
            n = start_act(act)
            for e, name in enumerate(stages):
                if name in layer:
                    ffn_act(act, n, sig[name], slot0[name], e * C, e < len(stages) - 1)
                if name == "attn":
                    attn_act(act, n, sig[name], slot0[name], e * C, e < len(stages) - 1)
                if name == "rwkv":
                    rwkv_act(act, n, sig[name], slot0[name], e * C, e < len(stages) - 1)
            end_evac(act, lambda o, i: nc.scalar.activation(o, i, ACT.Copy), 1, fin("done1"))
            end_evac(act, lambda o, i: nc.scalar.activation(o, i, ACT.Copy), 3, fin("done1"))

        @block.vector
        def _(dve):
            n = start_dve(dve)
            for e, name in enumerate(stages):
                if name in layer:
                    ffn_dve(dve, n, sig[name], slot0[name], *layer[name], (e + 1) * C, e < len(stages) - 1)
                if name == "attn":
                    attn_dve(dve, n, sig[name], slot0[name], (e + 1) * C, e < len(stages) - 1)
                if name == "rwkv":
                    rwkv_dve(dve, n, sig[name], slot0[name], (e + 1) * C, e < len(stages) - 1)
            end_evac(dve, nc.vector.tensor_copy, 0, fin("done0"))
            end_evac(dve, nc.vector.tensor_copy, 2, fin("done0"))

        @block.tensor
        def _(pe):
            for s in range(2):
                pe.sem_inc(used[s], 1)
            start_pe(pe)
            n = SlotCount()
            for name in stages:
                if name in layer:
                    ffn_pe(pe, n, sig[name], slot0[name])
                if name == "attn":
                    attn_pe(pe, n, sig[name], slot0[name])
                if name == "rwkv":
                    rwkv_pe(pe, n, sig[name], slot0[name])
            end_pe(pe, len(stages) * C)


        @block.gpsimd
        def _(pool):
            for e, name in enumerate(stages):
                if name == "attn":
                    attn_pool(pool, sig[name], sig[stages[e - 1]])
                if name == "rwkv":
                    rwkv_pool(pool, sig[name], sig[stages[e - 1]])


def constants():
    import numpy as np
    small = np.concatenate([np.eye(P), np.full((P, P), 1.0 / D)], axis=1).astype(np.float32)
    inv = (np.float32(10000.0) ** (-np.arange(0, 64, 2, dtype=np.float32) / np.float32(64))).astype(np.float32)
    ang = np.arange(S, dtype=np.float32)[None, :] * inv[:, None]
    cos, sin = np.cos(ang), np.sin(ang)
    i = np.arange(P)
    swap = np.zeros((P, P), np.float32)
    swap[i ^ 32, i] = 1.0
    head = i[:, None] // 64 == i[None, :] // 64
    lower_of_pair = lambda i, b: ((i[:, None] // b) % 2 == 1) & (i[None, :] // b == i[:, None] // b - 1)
    return {
        "consts": small,
        "cos": np.concatenate([cos] * 4).astype(np.float32),
        "sin": np.concatenate([-sin, sin] * 2).astype(np.float32),
        "rot_m": swap,
        "tri_i": (i[None, :] <= i[:, None]).astype(np.int32),
        "tri_t": (i[:, None] <= i[None, :]).astype(np.float32),
        "lvl": np.concatenate([lower_of_pair(i, 1 << l) for l in range(7)], axis=1).astype(np.float32),
        "low2": np.concatenate([i[:, None] < i[None, :], i[:, None] <= i[None, :]], axis=1).astype(np.float32),
        "blk": np.concatenate([head, head / 64], axis=1).astype(np.float32),
        "ind_b": (i[:, None] == np.arange(D)[None, :] // 64).astype(np.float32),
        "ind_s": np.concatenate([2 * c + i[:, None] // 64 == np.arange(16)[None, :] for c in range(C)],
                                axis=1).astype(np.float32),
        "tri_u": (i[:, None] > i[None, :]).astype(np.float32),
    }


STAGES = ["ffn0a", "attn", "ffn0b", "ffn1a", "rwkv", "ffn1b"]


def kernel(**inputs):
    import numpy as np
    import concourse.bacc as bacc
    from concourse.bass_utils import run_bass_kernel_spmd as run
    nc = bacc.Bacc("TRN2", target_bir_lowering=False, num_devices=1)
    arrays = {k: np.ascontiguousarray(v) for k, v in {**inputs, **constants()}.items()}
    a = {k: nc.dram_tensor(k, v.shape, mybir.dt.from_np(v.dtype), kind="ExternalInput").ap()
         for k, v in arrays.items()}
    out = nc.dram_tensor("out", (1, S, D), F32, kind="ExternalOutput").ap()
    build(nc, a, out, STAGES)
    r = run(nc, [arrays], core_ids=[0])
    return r.results[0]["out"]
```

```python
import math
from contextlib import ExitStack

import concourse.bass as bass
from concourse import mybir

F32 = mybir.dt.float32
F32R = mybir.dt.float32r
I32 = mybir.dt.int32
ACT = mybir.ActivationFunctionType
ALU = mybir.AluOpType
AX = mybir.AxisListType

P = 128
D = 1024
S = 512
DFF = 2816
C = D // P
FC = DFF // P
PANEL = 256
PK = 8
NG = 6


MIXES = [1, 4, 5, 0, 2, 3]
ROWS = ["attn_b_qkv", "rwkv_mix", "rwkv_w0", "rwkv_a0", "rwkv_k_k", "rwkv_k_a", "rwkv_r_k", "rwkv_lnx_g",
        "rwkv_lnx_b"]
VIEWS = {"rwkv_mix": "o m (c p) -> (o m c) p", "rwkv_r_k": "o (c h) k -> (o c) (h k)"}
N_ROWS = 12 + 6 * C + 7 * C


def kind_of(stage):
    return "ffn" if stage.startswith("ffn") else stage


def groups_of(k):
    return [(a, min(PK, k - a)) for a in range(0, k, PK)]


class SlotCount:

    def __init__(self):
        self.base, self.i, self.per, self.local = [0, 0], 0, [0, 0], [0, 0]

    def enter(self, i, per):
        self.base = [b + l for b, l in zip(self.base, self.local)]
        self.i, self.per, self.local = i, per, [0, 0]

    def leave(self, n):
        assert self.local == self.per
        self.base = [b + n * p for b, p in zip(self.base, self.per)]
        self.i, self.per, self.local = 0, [0, 0], [0, 0]

    def peek(self, s):
        k = self.base[s] + self.local[s]
        return self.i * self.per[s] + k if self.per[s] and not isinstance(self.i, int) else k + self.i * self.per[s]

    def next(self, s):
        k = self.peek(s)
        self.local[s] += 1
        return k


NORM = {"squares": C, "summed": C, "log": 1, "rstd": 1}
OPERAND = {"scaled": C, "hi": C, "xn": C}
OUT = {"y_squares": 4 + C, "y_sum": 2 + C, "y_mean": 1, "y_log": 1, "y_rstd": 1, "y_scaled": C}
FFN = {"silu": 1 + FC // 2, "product": 1 + FC // 2, "hid_hi": FC // 2, "hid": 1 + FC // 2}
SHARED = {"ffn": {**NORM, **OPERAND, **OUT, **FFN}, "attn": {**NORM, **OPERAND, **OUT}, "rwkv": {**NORM, **OUT}}


class Signals:

    def __init__(self, nc, ctx, stage, shared, earlier):
        self.nc, self.ctx, self.stage, self.shared, self.own = nc, ctx, stage, shared, {}
        self.counted = {}
        for kind in earlier:
            for name, times in SHARED[kind].items():
                self.counted[name] = self.counted.get(name, 0) + times

    def __call__(self, name, count=None):
        common = any(name in names for names in SHARED.values())
        made, full = (self.shared, name) if common else (self.own, f"{self.stage}_{name}")
        if name not in made:
            made[name] = self.ctx.enter_context(self.nc.semaphore(full))
        if count is None:
            return made[name]
        return made[name], count + (self.counted.get(name, 0) if common else 0)


def build(nc, a, out, stages):
    with ExitStack() as ctx:
        start = (nc.sbuf_base + 31) // 32 * 32
        place = {"at": 0}

        def sb(name, shape, dt, offset):
            return nc.alloc_sbuf_tensor_at(name, shape, dt, offset=start + offset)

        def take(nbytes):
            at = place["at"]
            place["at"] = at + (nbytes + 31) // 32 * 32
            return at

        o_x = take(C * S * 4)
        o_raw = take(2 * PK * PANEL * 4)
        o_whi = take(2 * PK * PANEL * 4)
        o_wlo = take(2 * PK * PANEL * 4)
        o_xnh = take(C * S * 4)
        o_xnl = take(C * S * 4)
        o_arena = take(2 * FC * S * 4)
        o_tmp = take(8 * S * 4)
        o_const = take(4 * P * 4)

        x = sb("x", [P, C, S], F32, o_x)
        w_raw = sb("w_raw", [P, 2, PK, PANEL], F32, o_raw)
        w_hi = sb("w_hi", [P, 2, PK, PANEL], F32R, o_whi)
        w_lo = sb("w_lo", [P, 2, PK, PANEL], F32R, o_wlo)
        xn_hi = sb("xn_hi", [P, C, S], F32R, o_xnh)
        xn_lo = sb("xn_lo", [P, C, S], F32R, o_xnl)
        hid_hi = sb("hid_hi", [P, FC, S], F32R, o_arena)
        hid_lo = sb("hid_lo", [P, FC, S], F32R, o_arena + FC * S * 4)
        y_ffn = sb("y_ffn", [P, C, S], F32, o_xnh)
        sq = sb("sq", [P, 2, S], F32, o_tmp)
        rstd = sb("rstd", [P, S], F32, o_tmp + 2 * S * 4)
        acc = sb("acc", [P, S], F32, o_tmp + 3 * S * 4)
        hn = sb("hn", [P, 2, S], F32, o_tmp + 4 * S * 4)
        sil = sb("sil", [P, 2, S], F32, o_tmp + 6 * S * 4)
        ident = sb("ident", [P, P], F32, o_const)
        ones_d = sb("ones_d", [P, P], F32, o_const + P * 4)
        vec_n = sb("vec_n", [P, 2 * NG * C], F32, o_const + 2 * P * 4)
        vec_h = sb("vec_h", [P, 2 * NG * C], F32, o_const + 3 * P * 4)
        o_vr = take(P * 4)
        vec_r = sb("vec_r", [P, P], F32, o_vr)
        o_eps = take(32)
        eps_rms = sb("eps_rms", [P, 1], F32, o_eps)
        assert start + place["at"] <= nc.sbuf_usable_end, place

        xt = sb("xt", [P, S // P, D], F32, o_arena)
        rows_n = sb("rows_n", [2 * NG * C, P], F32, o_arena + 4 * D * 4)
        rows_r = sb("rows_r", [P, P], F32, o_arena + 4 * D * 4 + P * 4)
        ot = sb("ot", [P, S // P, D], F32, o_arena)

        ps = ctx.enter_context(nc.psum_tensor("ps", [P, 8, 512], F32))

        def sem(name):
            return ctx.enter_context(nc.semaphore(name))

        loaded = [sem("loaded0"), sem("loaded1")]
        hi_done = [sem("hi_done0"), sem("hi_done1")]
        lo_done = [sem("lo_done0"), sem("lo_done1")]
        used = [sem("used0"), sem("used1")]
        consts_in, x_in, x_ready, out_done = sem("consts_in"), sem("x_in"), sem("x_ready"), sem("out_done")

        shared = {}

        def signals(stage, earlier=()):
            return Signals(nc, ctx, stage, shared, [kind_of(e) for e in earlier])

        def ch(t, c):
            return t[:, bass.ds(c, 1), :]

        def col(v, c):
            return v[:, bass.ds(c, 1)]

        def gain(l, i, c):
            return (l * NG + i) * C + c

        def load(sp, n, s, src, cols=PANEL):
            k = n.next(s)
            sp.wait_ge(lo_done[s], k + 1)
            sp.dma_start(w_raw[:, s, 0:src.shape[1], 0:cols], src).then_inc(loaded[s], 16)

        def split_hi(act, n, s):
            k = n.next(s)
            act.wait_ge(loaded[s], (k + 1) * 16)
            act.wait_ge(used[s], k + 1)
            nc.scalar.activation(w_hi[:, s, :, :], w_raw[:, s, :, :], ACT.Copy).then_inc(hi_done[s], 1)

        def split_lo(dve, n, s):
            k = n.next(s)
            dve.wait_ge(hi_done[s], k + 1)
            nc.vector.tensor_tensor(w_lo[:, s, :, :], w_raw[:, s, :, :], w_hi[:, s, :, :].bitcast(F32),
                                    ALU.subtract).then_inc(lo_done[s], 1)

        def wait_used(eng, n, s):
            eng.wait_ge(used[s], n.peek(s) + 1)

        def products(pe, n, s, count, banks, hi, lo, first, last, arrived=None, widths=(P, P), freed=None):
            pe.wait_ge(lo_done[s], n.next(s) + 2)
            for k in range(count):
                if arrived:
                    arrived(k)
                for m, bank in enumerate(banks):
                    wh = w_hi[:, s, k, m * P:m * P + widths[m]]
                    wl = w_lo[:, s, k, m * P:m * P + widths[m]]
                    nc.tensor.matmul(bank, wh, hi(k), start=first and k == 0, stop=False)
                    nc.tensor.matmul(bank, wh, lo(k), start=False, stop=False)
                    end = nc.tensor.matmul(bank, wl, hi(k), start=False, stop=last and k == count - 1)
                if freed and k < count - 1:
                    end.then_inc(freed, 1)
            end.then_inc(used[s], 1)

        def norm_in_pe(pe, g):
            for c in range(C):
                pe.wait_ge(*g("squares", c + 1))
                nc.tensor.matmul(ps[:, 1, :], ones_d[:], sq[:, c % 2, :], start=c == 0,
                                 stop=c == C - 1).then_inc(g("summed"), 1)

        def norm_in_squares(act, g, seen):
            for c in range(C):
                act.wait_ge(x_ready, seen + c + 1)
                if c >= 2:
                    act.wait_ge(*g("summed", c - 1))
                nc.scalar.activation(ch(sq, c % 2), ch(x, c), ACT.Square).then_inc(g("squares"), 1)
            act.wait_ge(*g("summed", C))
            nc.scalar.activation(rstd[:], ps[:, 1, :], ACT.Ln, bias=eps_rms[:]).then_inc(g("log"), 1)
            act.wait_ge(*g("log", 1))
            nc.scalar.activation(rstd[:], rstd[:], ACT.Exp, scale=-0.5).then_inc(g("rstd"), 1)

        def norm_in_hi(act, g):
            for c in range(C):
                act.wait_ge(*g("scaled", c + 1))
                nc.scalar.activation(ch(xn_hi, c), ch(hn, c % 2), ACT.Copy).then_inc(g("hi"), 1)

        def norm_in_dve(dve, g, l, i):
            dve.wait_ge(*g("rstd", 1))
            for c in range(C + 1):
                if c < C:
                    if c >= 2:
                        dve.wait_ge(*g("xn", c - 1))
                    nc.vector.scalar_tensor_tensor(ch(hn, c % 2), ch(x, c), col(vec_n, gain(l, i, c)),
                                                   rstd[:],
                                                   ALU.mult, ALU.mult).then_inc(g("scaled"), 1)
                if c >= 1:
                    dve.wait_ge(*g("hi", c))
                    nc.vector.tensor_tensor(ch(xn_lo, c - 1), ch(hn, (c - 1) % 2),
                                            ch(xn_hi, c - 1).bitcast(F32), ALU.subtract).then_inc(g("xn"), 1)

        def out_pe(pe, n, g, s0, rows, hi, lo, arrived):
            def body(i, q0):
                s = s0
                for q in range(2):
                    pe.wait_ge(*g("y_squares", 4 * i + 2 * q + 2))
                    for r, (k0, nk) in enumerate(rows):
                        products(pe, n, s, nk, [ps[:, 4 + 2 * q, :], ps[:, 5 + 2 * q, :]],
                                 lambda k: hi(k0 + k), lambda k: lo(k0 + k), r == 0, r == len(rows) - 1,
                                 arrived=(lambda k: arrived(k0 + k)))
                        s = 1 - s
            per = [len(rows), len(rows)]
            with pe.Fori(0, 2) as i:
                n.enter(i, per)
                body(i, 0)
            n.leave(2)
            pe.wait_ge(*g("y_sum", 2 + C))
            nc.tensor.matmul(ps[:, 0, :], ones_d[:], acc[:], start=True, stop=True).then_inc(g("y_mean"), 1)

        def out_uses(s0, rows):
            r = len(rows)
            return [((s0 + u) % 2, u // r if u % r == r - 1 else None) for u in range(2 * r)]

        def out_act(act, n, g, s0, rows, y, more):
            def body(i, last):
                for u, (s, panel) in enumerate(out_uses(s0, rows)):
                    if panel is not None:
                        if last and u == 2 * len(rows) - 1 and not more:
                            act.wait_ge(used[s], n.peek(s) + 1)
                        else:
                            wait_used(act, n, s)
                        for m in range(2):
                            c = 4 * i + 2 * panel + m
                            nc.scalar.activation(ch(y, c), ch(ps, 4 + 2 * panel + m), ACT.Copy)
                            act.wait_ge(*g("y_sum", c + 1))
                            nc.scalar.activation(ch(sq, m), ch(ps, 4 + 2 * panel + m),
                                                 ACT.Square).then_inc(g("y_squares"), 1)
                    if not (last and not more and u >= 2 * len(rows) - 2):
                        split_hi(act, n, s)
                    else:
                        n.next(s)
            loop2(act, n, [len(rows), len(rows)], body, more)
            act.wait_ge(*g("y_mean", 1))
            nc.scalar.activation(rstd[:], ps[:, 0, :], ACT.Ln, bias=eps_rms[:]).then_inc(g("y_log"), 1)
            act.wait_ge(*g("y_log", 1))
            nc.scalar.activation(rstd[:], rstd[:], ACT.Exp, scale=-0.5).then_inc(g("y_rstd"), 1)

        def loop2(eng, n, per, body, more):
            if more:
                with eng.Fori(0, 2) as i:
                    n.enter(i, per)
                    body(i, False)
                n.leave(2)
            else:
                for i in range(2):
                    n.enter(0, per)
                    body(i, i == 1)
                    n.leave(1)

        def out_dve(dve, n, g, s0, rows, y, gains, seen, more):
            def body(i, last):
                for u, (s, panel) in enumerate(out_uses(s0, rows)):
                    if panel is not None:
                        for m in range(2):
                            c = 4 * i + 2 * panel + m
                            dve.wait_ge(*g("y_squares", c + 5))
                            dve.wait_ge(*g("y_sum", c + 2))
                            nc.vector.tensor_tensor(acc[:], acc[:], sq[:, m, :],
                                                    ALU.add).then_inc(g("y_sum"), 1)
                    if not (last and not more and u >= 2 * len(rows) - 2):
                        split_lo(dve, n, s)
                    else:
                        n.next(s)
            loop2(dve, n, [len(rows), len(rows)], body, more)
            dve.wait_ge(*g("y_rstd", 1))
            for c in range(C + 1):
                if c < C:
                    if c >= 2:
                        dve.wait_ge(x_ready, seen + c - 1)
                    nc.vector.scalar_tensor_tensor(ch(hn, c % 2), ch(y, c), col(gains[0], gains[1] + c),
                                                   rstd[:], ALU.mult, ALU.mult).then_inc(g("y_scaled"), 1)
                if c >= 1:
                    dve.wait_ge(*g("y_scaled", c))
                    nc.vector.tensor_tensor(ch(x, c - 1), ch(x, c - 1), ch(hn, (c - 1) % 2),
                                            ALU.add).then_inc(x_ready, 1)

        def out_start(g):
            nc.vector.memset(acc[:], 0.0).then_inc(g("y_sum"), 2)

        def out_start_act(act, g):
            act.sem_inc(g("y_squares"), 4)

        FP = FC // 2
        HID_ROWS = groups_of(FC)

        def w_in_panel(l, f, half, j):
            w = a["ffn_w_in"][l, f].rearrange("(k p) n -> p k n", p=P)
            return w[:, :, bass.ds(j * PANEL + half * DFF, PANEL)]

        def out_panel(w, k0, nk, p):
            v = w.rearrange("(k p) n -> p k n", p=P)
            return v[:, k0:k0 + nk, bass.ds(p * PANEL, PANEL)]

        def out_sp(sp, n, s0, rows, w):
            with sp.Fori(0, 2) as i:
                n.enter(i, [len(rows), len(rows)])
                s = s0
                for q in range(2):
                    for k0, nk in rows:
                        load(sp, n, s, out_panel(w, k0, nk, 2 * i + q))
                        s = 1 - s
            n.leave(2)

        def ffn_sp(sp, n, l, f, s0):
            with sp.Fori(0, FP) as j:
                n.enter(j, [1, 1])
                load(sp, n, s0, w_in_panel(l, f, 0, j))
                load(sp, n, 1 - s0, w_in_panel(l, f, 1, j))
            n.leave(FP)
            out_sp(sp, n, s0, HID_ROWS, a["ffn_w_out"][l, f])

        def ffn_pe(pe, n, g, s0):
            norm_in_pe(pe, g)
            with pe.Fori(0, FP) as j:
                n.enter(j, [1, 1])
                pe.wait_ge(*g("silu", j + 1))
                products(pe, n, s0, PK, [ps[:, 0, :], ps[:, 1, :]], lambda k: xn_hi[:, k, :],
                         lambda k: xn_lo[:, k, :], True, True,
                         arrived=lambda k: pe.wait_ge(*g("xn", k + 1)))
                pe.wait_ge(*g("product", j + 1))
                products(pe, n, 1 - s0, PK, [ps[:, 2, :], ps[:, 3, :]], lambda k: xn_hi[:, k, :],
                         lambda k: xn_lo[:, k, :], True, True)
            n.leave(FP)
            out_pe(pe, n, g, s0, HID_ROWS, lambda k: hid_hi[:, k, :], lambda k: hid_lo[:, k, :],
                   lambda k: pe.wait_ge(*g("hid", k // 2 + 2)) if k % 2 == 0 else None)

        def ffn_act(act, n, g, s0, seen, more):
            act.sem_inc(g("silu"), 1)
            out_start_act(act, g)
            norm_in_squares(act, g, seen)
            norm_in_hi(act, g)
            with act.Fori(0, FP) as j:
                n.enter(j, [1, 1])
                wait_used(act, n, s0)
                act.wait_ge(*g("product", j + 1))
                nc.scalar.activation(ch(sil, 0), ch(ps, 0), ACT.Silu)
                nc.scalar.activation(ch(sil, 1), ch(ps, 1), ACT.Silu).then_inc(g("silu"), 1)
                split_hi(act, n, s0)
                split_hi(act, n, 1 - s0)
                act.wait_ge(*g("product", j + 2))
                nc.scalar.activation(ch(hid_hi, 2 * j), ch(hn, 0), ACT.Copy)
                nc.scalar.activation(ch(hid_hi, 2 * j + 1), ch(hn, 1), ACT.Copy).then_inc(g("hid_hi"), 1)
            n.leave(FP)
            out_act(act, n, g, s0, HID_ROWS, y_ffn, more)

        def ffn_dve(dve, n, g, s0, l, f, seen, more):
            dve.sem_inc(g("product"), 1)
            dve.sem_inc(g("hid"), 1)
            out_start(g)
            norm_in_dve(dve, g, l, 4 * f)
            with dve.Fori(0, FP) as j:
                n.enter(j, [1, 1])
                split_lo(dve, n, s0)
                wait_used(dve, n, 1 - s0)
                dve.wait_ge(*g("silu", j + 2))
                dve.wait_ge(*g("hid", j + 1))
                nc.vector.tensor_tensor(ch(hn, 0), ch(ps, 2), ch(sil, 0), ALU.mult)
                nc.vector.tensor_tensor(ch(hn, 1), ch(ps, 3), ch(sil, 1), ALU.mult).then_inc(g("product"), 1)
                split_lo(dve, n, 1 - s0)
                dve.wait_ge(*g("hid_hi", j + 1))
                nc.vector.tensor_tensor(ch(hid_lo, 2 * j), ch(hn, 0), ch(hid_hi, 2 * j).bitcast(F32),
                                        ALU.subtract)
                nc.vector.tensor_tensor(ch(hid_lo, 2 * j + 1), ch(hn, 1),
                                        ch(hid_hi, 2 * j + 1).bitcast(F32), ALU.subtract).then_inc(g("hid"), 1)
            n.leave(FP)
            out_dve(dve, n, g, s0, HID_ROWS, y_ffn, (vec_h, gain(l, 4 * f + 1, 0)), seen, more)

        HD, NKV, GRP, NB = 64, 4, 4, S // P
        QD = NKV * GRP * HD
        SCALE = HD ** -0.5
        KV_ROWS = groups_of(C)
        m_at = {"at": o_arena}

        def arena(name, shape, dt=F32):
            n_bytes = 4
            for d in shape[1:]:
                n_bytes *= d
            at = m_at["at"]
            m_at["at"] = at + (n_bytes + 31) // 32 * 32
            assert m_at["at"] <= o_arena + 2 * FC * S * 4, (name, m_at)
            return sb(name, shape, dt, at)

        o_hi = arena("o_hi", [P, C, S], F32R)
        o_lo = arena("o_lo", [P, C, S], F32R)
        kz = arena("kz", [P, NKV, NB, 2, P])
        v_sb = arena("v_sb", [P, NB, NKV * HD])
        v_g = arena("v_g", [P, NB, HD])
        q_rot = arena("q_rot", [P, 2, S])
        merged = arena("merged", [P, 2, GRP, P])
        prob = arena("prob", [P, 2, GRP, P])
        prob_t = arena("prob_t", [P, 2, 2, GRP, P])
        cos_t = arena("cos_t", [P, S])
        sin_t = arena("sin_t", [P, S])
        rot_m = arena("rot_m", [P, P])
        tri_i = arena("tri_i", [P, P], I32)
        tri_t = arena("tri_t", [P, P])
        tri_u = arena("tri_u", [P, P])
        v_bias = arena("v_bias", [P, NKV * HD])
        sink = arena("sink", [P, NKV * GRP])
        n_sink = arena("n_sink", [P, NKV * GRP])
        top = arena("top", [P, 2, GRP])
        n_top = arena("n_top", [P, 2, GRP])
        sink_d = arena("sink_d", [P, 2, GRP])
        den = arena("den", [P, 2, GRP])
        t1, t2 = sil[:, 0, :], sil[:, 1, :]
        ATT_CONST = [(cos_t, "cos"), (sin_t, "sin"), (rot_m, "rot_m"), (tri_i, "tri_i"), (tri_t, "tri_t"),
                     (tri_u, "tri_u")]

        def qkv_panel(p):
            return a["attn_w_qkv"][0].rearrange("(k p) n -> p k n", p=P)[:, :, bass.ds(p * PANEL, PANEL)]

        def attn_sp(sp, n, g, before, s0):
            load(sp, n, s0, qkv_panel(QD // PANEL))
            load(sp, n, 1 - s0, qkv_panel(QD // PANEL + 1))
            sp.wait_ge(*before("y_mean", 1))
            for t, name in ATT_CONST:
                sp.dma_start(t[:], a[name]).then_inc(g("const"), 16)
            sp.dma_start(v_bias[:], a["attn_b_qkv"][0:1, QD + NKV * HD:QD + 2 * NKV * HD]
                         .rearrange("o n -> (o n)").partition_broadcast(P)).then_inc(g("const"), 16)
            sp.dma_start(sink[:], a["attn_sinks"].rearrange("o n -> (o n)").partition_broadcast(P)
                         ).then_inc(g("const"), 16)
            wo = a["attn_w_o"][0]
            load(sp, n, s0, qkv_panel(0))
            load(sp, n, 1 - s0, out_panel(wo, 0, C, 0))
            with sp.Fori(1, NKV) as i:
                n.enter(i - 1, [1, 0] if s0 == 0 else [0, 1])
                load(sp, n, s0, qkv_panel(i))
            n.leave(NKV - 1)
            for p in range(1, D // PANEL):
                load(sp, n, s0 if p % 2 else 1 - s0, out_panel(wo, 0, C, p))

        ATT_CONSTS = 16 * (len(ATT_CONST) + 2)

        def attn_pe(pe, n, g, s0):
            pe.sem_inc(g("transposed"), 2)
            pe.sem_inc(g("weighed"), 2)
            norm_in_pe(pe, g)
            xh, xl = (lambda k: xn_hi[:, k, :]), (lambda k: xn_lo[:, k, :])
            products(pe, n, s0, C, [ps[:, 0, :], ps[:, 1, :]], xh, xl, True, True,
                     arrived=lambda k: pe.wait_ge(*g("xn", k + 1)))
            s = 1 - s0
            pe.wait_ge(lo_done[s], n.next(s) + 2)
            for t in range(NB):
                o = ps[:, 4 + t // 2, (t % 2) * PANEL:(t % 2 + 1) * PANEL]
                for k in range(C):
                    h, l = xn_hi[:, k, t * P:(t + 1) * P], xn_lo[:, k, t * P:(t + 1) * P]
                    nc.tensor.matmul(o, h, w_hi[:, s, k, :], start=k == 0, stop=False)
                    nc.tensor.matmul(o, h, w_lo[:, s, k, :], start=False, stop=False)
                    end = nc.tensor.matmul(o, l, w_hi[:, s, k, :], start=False, stop=k == C - 1)
            end.then_inc(used[s], 1)
            pe.wait_ge(*g("const", ATT_CONSTS))
            for m in range(2):
                pe.wait_ge(*g("linear", m + 1))
                nc.tensor.matmul(ps[:, 2 + m, :], rot_m[:], hn[:, m, :], start=True,
                                 stop=True).then_inc(g("rotated"), 1)

            def scores(i, b):
                if b >= 2:
                    pe.wait_ge(*g("merged", 4 * i + b - 1))
                for back in range(min(b, 1) + 1):
                    for m in range(2):
                        end = nc.tensor.matmul(ps[:, 4 + 2 * back + b % 2, m * 2 * P:(m + 1) * 2 * P],
                                               q_rot[:, m, b * P:(b + 1) * P],
                                               kz[:, bass.ds(i, 1), b - back, :, :], start=True, stop=True)
                end.then_inc(g("scored"), 1)

            def transposes(i, b):
                pe.wait_ge(*g("normed", 4 * i + b + 1))
                for h in range(GRP):
                    end = nc.tensor.transpose(ps[:, b % 2, h * P:(h + 1) * P], prob[:, b % 2, h, :], ident[:])
                end.then_inc(g("transposed"), 1)

            def values(i, b):
                pe.wait_ge(*g("prob_t", 4 * i + b + 1))
                pe.wait_ge(*g("o_done", 4 * i + b + 1))
                for par in range(2):
                    o = ps[par * HD:(par + 1) * HD, 2 + b % 2, 0:2 * P]
                    for back in range(min(b, 1) + 1):
                        end = nc.tensor.matmul(o, v_g[:, b - back, :], prob_t[:, b % 2, back, par::2, :],
                                               start=back == 0, stop=back == min(b, 1))
                end.then_inc(g("weighed"), 1)

            with pe.Fori(0, NKV) as i:
                n.enter(i, [1, 0] if s0 == 0 else [0, 1])
                products(pe, n, s0, C, [ps[:, 0, :], ps[:, 1, :]], xh, xl, True, True)
                pe.wait_ge(*g("kz", 2))
                pe.wait_ge(*g("o_done", 4 * i + 2))
                for m in range(2):
                    pe.wait_ge(*g("linear", 2 * i + 3 + m))
                    nc.tensor.matmul(ps[:, 2 + m, :], rot_m[:], hn[:, m, :], start=True,
                                     stop=True).then_inc(g("rotated"), 1)
                pe.wait_ge(*g("roped", 2 * i + 4))
                scores(i, 0)
                scores(i, 1)
                pe.wait_ge(*g("v_g", i + 1))
                for b in range(NB):
                    transposes(i, b)
                    if b + 2 < NB:
                        scores(i, b + 2)
                    values(i, b)
            n.leave(NKV)
            out_pe(pe, n, g, 1 - s0, KV_ROWS, lambda k: o_hi[:, k, :], lambda k: o_lo[:, k, :],
                   lambda k: pe.wait_ge(*g("o_done", 4 * (k // 2) + 6)) if k % 2 == 0 else None)

        def attn_act(act, n, g, s0, seen, more):
            out_start_act(act, g)
            act.sem_inc(g("exped"), 2)
            norm_in_squares(act, g, seen)
            norm_in_hi(act, g)
            wait_used(act, n, s0)
            act.wait_ge(*g("xn", C))
            for m in range(2):
                nc.scalar.activation(ch(hn, m), ch(ps, m), ACT.Identity,
                                     bias=col(vec_r, QD // P + m)).then_inc(g("linear"), 1)
            split_hi(act, n, s0)
            split_hi(act, n, 1 - s0)

            def previous(i, b):
                act.wait_ge(*g("scored", 4 * i + b + 1))
                act.wait_ge(*g("exped", 4 * i + b + 1))
                nc.scalar.activation(merged[:, b % 2, :, :], ps[:, 6 + b % 2, :].rearrange("p (h k) -> p h k", k=P),
                                     ACT.Copy).then_inc(g("previous"), 1)

            def exps(i, b):
                act.wait_ge(*g("n_top", 4 * i + b + 1))
                act.wait_ge(*g("transposed", 4 * i + b + 1))
                for h in range(GRP):
                    nc.scalar.activation(prob[:, b % 2, h, :], merged[:, b % 2, h, :], ACT.Exp,
                                         bias=n_top[:, b % 2, h:h + 1], scale=SCALE,
                                         accum_out=den[:, b % 2, h:h + 1])
                nc.scalar.activation(sink_d[:, b % 2, :], sink_d[:, b % 2, :], ACT.Exp).then_inc(g("exped"), 1)

            def out_hi(i, b):
                act.wait_ge(*g("weighed", 4 * i + b + 3))
                nc.scalar.activation(o_hi[:, bass.ds(2 * i, 2), b * P:(b + 1) * P],
                                     ps[:, 2 + b % 2, 0:2 * P].rearrange("p (m q) -> p m q", q=P),
                                     ACT.Copy).then_inc(g("o_hi"), 1)

            with act.Fori(0, NKV) as i:
                n.enter(i, [1, 0] if s0 == 0 else [0, 1])
                wait_used(act, n, s0)
                act.wait_ge(*g("roped", 2 * i + 2))
                for m in range(2):
                    nc.scalar.activation(ch(hn, m), ch(ps, m), ACT.Identity,
                                         bias=col(vec_r, 2 * i + m)).then_inc(g("linear"), 1)
                split_hi(act, n, s0)
                previous(i, 1)
                exps(i, 0)
                for b in range(1, NB):
                    if b + 1 < NB:
                        previous(i, b + 1)
                    exps(i, b)
                    out_hi(i, b - 1)
                out_hi(i, NB - 1)
            n.leave(NKV)
            out_act(act, n, g, 1 - s0, KV_ROWS, y_ffn, more)

        def rope(dve, g, at, m, write):
            dve.wait_ge(*g("rotated", at + 1))
            dve.wait_ge(*g("rope_free", at + 1))
            nc.vector.tensor_tensor(t1, hn[:, m, :], cos_t[:], ALU.mult)
            nc.vector.tensor_tensor(t2, ps[:, 2 + m, :], sin_t[:], ALU.mult).then_inc(g("turned"), 1)
            dve.wait_ge(*g("turned", at + 1))
            write()

        def attn_dve(dve, n, g, s0, seen, more):
            out_start(g)
            dve.sem_inc(g("o_done"), 2)
            dve.sem_inc(g("rope_free"), 1)
            norm_in_dve(dve, g, 0, 2)
            dve.wait_ge(*g("const", ATT_CONSTS))
            nc.vector.tensor_scalar(n_sink[:], sink[:], -1.0, None, ALU.mult).then_inc(g("n_sink"), 1)
            split_lo(dve, n, s0)
            wait_used(dve, n, 1 - s0)
            nc.vector.tensor_tensor(v_sb[:].rearrange("p (t u) n -> p t u n", t=2),
                                    ps[:, 4:6, :].rearrange("p t (u n) -> p t u n", u=2),
                                    v_bias[:].unsqueeze(1).unsqueeze(1).to_broadcast([P, 2, 2, NKV * HD]),
                                    ALU.add).then_inc(g("v"), 1)
            split_lo(dve, n, 1 - s0)
            dve.wait_ge(*g("kz_zero", 2))
            for m in range(2):
                def write():
                    for half in range(2):
                        at = slice(half * HD, (half + 1) * HD)
                        for par in range(2):
                            o = kz[par * HD:(par + 1) * HD, 2 * m + half, :, par, :]
                            end = nc.vector.tensor_tensor(
                                o, t1[at].rearrange("p (b k) -> p b k", k=P),
                                t2[at].rearrange("p (b k) -> p b k", k=P), ALU.add)
                            if half == 1 and par == 1:
                                end.then_inc(g("roped"), 1)
                            elif half == 1:
                                end.then_inc(g("kz_part"), 1)
                rope(dve, g, m, m, write)
                dve.wait_ge(*g("roped", m + 1))
                dve.sem_inc(g("kz"), 1)
                dve.sem_inc(g("rope_free"), 1)

            def merge(i, b):
                if b == 0:
                    dve.wait_ge(*g("cleared", i + 1))
                else:
                    dve.wait_ge(*g("previous", 3 * i + b))
                dve.wait_ge(*g("scored", 4 * i + b + 1))
                dve.sem_inc(g("merging"), 1)
                nc.vector.copy_predicated(merged[:, b % 2, :, :], tri_i[:].unsqueeze(1).to_broadcast([P, GRP, P]),
                                          ps[:, 4 + b % 2, :].rearrange("p (h k) -> p h k", k=P)
                                          ).then_inc(g("merged"), 1)
                dve.wait_ge(*g("merged", 4 * i + b + 1))
                nc.vector.reduce_max(top[:, b % 2, :], merged[:, b % 2, :, :], AX.X).then_inc(g("top"), 1)
                dve.wait_ge(*g("top", 4 * i + b + 1))
                nc.vector.scalar_tensor_tensor(n_top[:, b % 2, :], top[:, b % 2, :], -SCALE,
                                               n_sink[:, bass.ds(GRP * i, GRP)], ALU.mult,
                                               ALU.min).then_inc(g("n_top0"), 1)
                dve.wait_ge(*g("n_top0", 4 * i + b + 1))
                nc.vector.tensor_tensor(sink_d[:, b % 2, :], n_top[:, b % 2, :], sink[:, bass.ds(GRP * i, GRP)],
                                        ALU.add).then_inc(g("n_top"), 1)

            def normalize(i, b):
                dve.wait_ge(*g("exped", 4 * i + b + 3))
                nc.vector.tensor_tensor(den[:, b % 2, :], den[:, b % 2, :], sink_d[:, b % 2, :],
                                        ALU.add).then_inc(g("den"), 1)
                dve.wait_ge(*g("den", 4 * i + b + 1))
                nc.vector.reciprocal(top[:, b % 2, :], den[:, b % 2, :]).then_inc(g("rden"), 1)
                dve.wait_ge(*g("rden", 4 * i + b + 1))
                nc.vector.tensor_tensor(prob[:, b % 2, :, :], prob[:, b % 2, :, :],
                                        top[:, b % 2, :].unsqueeze(2).to_broadcast([P, GRP, P]),
                                        ALU.mult).then_inc(g("normed"), 1)

            def mask(i, b):
                dve.wait_ge(*g("transposed", 4 * i + b + 3))
                dve.wait_ge(*g("weighed", 4 * i + b + 1))
                pt = ps[:, b % 2, :].rearrange("p (h q) -> p h q", q=P)
                end = nc.vector.tensor_tensor(prob_t[:, b % 2, 0, :, :], pt,
                                              tri_t[:].unsqueeze(1).to_broadcast([P, GRP, P]), ALU.mult)
                if b > 0:
                    end = nc.vector.tensor_tensor(prob_t[:, b % 2, 1, :, :], pt,
                                                  tri_u[:].unsqueeze(1).to_broadcast([P, GRP, P]), ALU.mult)
                end.then_inc(g("prob_t"), 1)

            def out_low(i, b):
                dve.wait_ge(*g("o_hi", 4 * i + b + 1))
                at = (slice(None), bass.ds(2 * i, 2), slice(b * P, (b + 1) * P))
                nc.vector.tensor_tensor(o_lo[at], ps[:, 2 + b % 2, 0:2 * P].rearrange("p (m q) -> p m q", q=P),
                                        o_hi[at].bitcast(F32), ALU.subtract).then_inc(g("o_done"), 1)

            with dve.Fori(0, NKV) as i:
                n.enter(i, [1, 0] if s0 == 0 else [0, 1])
                for m in range(2):
                    def write():
                        nc.vector.tensor_tensor(q_rot[:, m, :], t1, t2, ALU.add).then_inc(g("roped"), 1)
                    rope(dve, g, 2 * i + 2 + m, m, write)
                    dve.wait_ge(*g("roped", 2 * i + 3 + m))
                    dve.sem_inc(g("rope_free"), 1)
                split_lo(dve, n, s0)
                merge(i, 0)
                for b in range(NB):
                    if b + 1 < NB:
                        merge(i, b + 1)
                    normalize(i, b)
                    if b >= 1:
                        out_low(i, b - 1)
                    mask(i, b)
                out_low(i, NB - 1)
            n.leave(NKV)
            out_dve(dve, n, g, 1 - s0, KV_ROWS, y_ffn, (vec_n, gain(0, 3, 0)), seen, more)

        def attn_pool(pool, g, before):
            pool.wait_ge(*before("y_mean", 1))
            for par in range(2):
                nc.gpsimd.memset(kz[(1 - par) * HD:(2 - par) * HD, :, :, par, :], 0.0).then_inc(g("kz_zero"), 1)
                pool.wait_ge(*g("kz_zero", par + 1))
            pool.wait_ge(*g("v", 1))
            with pool.Fori(0, NKV) as i:
                pool.wait_ge(*g("weighed", 4 * i + 2))
                nc.gpsimd.tensor_copy(v_g[:], v_sb[:, :, bass.ds(HD * i, HD)]).then_inc(g("v_g"), 1)
                pool.wait_ge(*g("v_g", i + 1))
                pool.wait_ge(*g("exped", 4 * i + 1))
                pool.sem_inc(g("clearing"), 1)
                nc.gpsimd.memset(merged[:, 0, :, :], -1e30).then_inc(g("cleared"), 1)
                pool.wait_ge(*g("cleared", i + 1))

        HEAD = 64
        LEVELS = P.bit_length() - 1
        UNITS = 2 * NB
        LORA = [("rwkv_w1", 64), ("rwkv_a1", 64), ("rwkv_g1", 160)]
        FILLS = 6
        DECAY = -math.exp(-0.5)
        V_MIX, V_W0 = 12, 12 + 6 * C
        V_A0, V_KK, V_KA, V_RK, V_LG, V_LB = (V_W0 + j * C for j in range(1, 7))

        m_at["at"] = o_arena
        h_pad = arena("h_pad", [P, C, S + 1])
        rkv = arena("rkv", [P, 3, C, S])
        y_rwkv = sb("y_rwkv", [P, C, S], F32, o_arena + C * (S + 1) * 4 + 2 * C * S * 4)
        sg = arena("sg", [P, 2, S])
        wa2 = arena("wa2", [P, 2, D])
        g2 = arena("g2", [P, 2, D])
        twa = sb("twa", [P, S], F32, take(S * 4))
        o_h = {"at": o_arena}

        def over(region, size, name, shape, dt=F32):
            n_bytes = 4
            for d in shape[1:]:
                n_bytes *= d
            at = region["at"]
            region["at"] = at + (n_bytes + 31) // 32 * 32
            assert region["at"] <= region.setdefault("end", at + size), name
            return sb(name, shape, dt, at)

        HB = C * (S + 1) * 4
        lvl = over(o_h, HB, "lvl", [P, LEVELS, P])
        lvl0_t = over(o_h, HB, "lvl0_t", [P, P])
        low2 = over(o_h, HB, "low2", [P, 2, P])
        blk = over(o_h, HB, "blk", [P, 2, P])
        ind_b = over(o_h, HB, "ind_b", [P, D])
        ind_s = over(o_h, HB, "ind_s", [P, C, 2 * C])
        k_norm = over(o_h, HB, "k_norm", [P, S])
        o_r = {"at": o_raw}
        mb = over(o_r, 16384, "mb", [P, NB, 2, 2, P])
        mk = over(o_r, 16384, "mk", [P, NB, 2, 2, P])
        o_w = {"at": o_whi}
        inv = over(o_w, 32768, "inv", [P, UNITS, P])
        inv_t = over(o_w, 32768, "inv_t", [P, UNITS, P])
        pair = over(o_w, 32768, "pair", [P, UNITS, P])
        b_tok = over(o_w, 32768, "b_tok", [P, NB, P])
        k_tok = over(o_w, 32768, "k_tok", [P, NB, P])
        ar = over(o_w, 32768, "ar", [P, 2, NB, 2, P])
        bt = over(o_w, 32768, "bt", [P, S])
        kt = over(o_w, 32768, "kt", [P, S])
        v_tok = over(o_w, 32768, "v_tok", [P, NB, P])
        v_c = over(o_w, 32768, "v_c", [P, S])
        o_n = {"at": o_xnh}
        ar1 = over(o_n, 32768, "ar1", [P, 2, NB, 2, P])
        pair1 = over(o_n, 32768, "pair1", [P, UNITS, P])
        m2 = over(o_n, 32768, "m2", [P, 2, S])
        yb = over(o_n, 32768, "yb", [P, S])
        qs = over(o_n, 32768, "qs", [P, S])
        wa_c = over(o_n, 32768, "wa_c", [P, 2, P])
        g_c = over(o_n, 32768, "g_c", [P, 2, P])
        ind_c = over(o_n, 32768, "ind_c", [P, P])
        state = over(o_n, 32768, "state", [P, 2, HEAD])
        grown = over(o_n, 32768, "grown", [P, HEAD])
        u0 = over(o_n, 32768, "u0", [P, 2, HEAD])
        u = over(o_n, 32768, "u", [P, 2, HEAD])
        mid = over(o_n, 32768, "mid", [P, NB])
        n_mid = over(o_n, 32768, "n_mid", [P, NB])
        carry = over(o_n, 32768, "carry", [P, 2, NB])
        ars, pairs = (ar, ar1), (pair, pair1)
        o_t = {"at": o_tmp}
        dl = over(o_t, 16384, "dl", [P, S])
        lc = over(o_t, 16384, "lc", [P, S])
        kk = over(o_t, 16384, "kk", [P, S])
        rate = over(o_t, 16384, "rate", [P, S])
        kp = over(o_t, 16384, "kp", [P, S])
        m1 = over(o_t, 16384, "m1", [P, S])
        ex = sb("ex", [P, NB, P + 1], F32, take(NB * (P + 1) * 4))
        ones_row = sb("ones_row", [P, P], F32, take(P * 4))
        omka = sb("omka", [P, C], F32, take(C * 4))
        w0h = sb("w0h", [P, 2 * C], F32, take(2 * C * 4))
        eps_ln = sb("eps_ln", [P, 1], F32, take(32))
        half_decay = sb("half_decay", [P, 1], F32, take(32))
        half = sb("half", [P, 1], F32, take(32))
        assert start + place["at"] <= nc.sbuf_usable_end, (start, place, nc.sbuf_usable_end)
        R_CONST = [(lvl, "lvl"), (lvl0_t, "lvl0_t"), (low2, "low2"), (blk, "blk"), (ind_b, "ind_b"), (ind_s, "ind_s")]

        def rkv_panel(i, p):
            return a["rwkv_w_rkv"][0].rearrange("i (k p) n -> i p k n", p=P)[bass.ds(i, 1), :, :,
                                                                           bass.ds(p * PANEL, PANEL)].rearrange(
                "i p k n -> (i p) k n")

        def rwkv_sp(sp, n, g, before, s0):
            for j, (name, cols) in enumerate(LORA):
                load(sp, n, (s0 + j) % 2, a[name][0].rearrange("(k p) n -> p k n", p=P), cols)
                if j == 1:
                    sp.wait_ge(*g("zeros", 4))
                    sp.dma_start(wa2[0:64, 0, :], a["rwkv_w2"][0]).then_inc(g("lora_in"), 16)
                    sp.dma_start(wa2[64:128, 1, :], a["rwkv_a2"][0]).then_inc(g("lora_in"), 16)
                    sp.dma_start(g2[:, 0, :], a["rwkv_g2"][0, 0:P, :]).then_inc(g("lora_in"), 16)
                    sp.dma_start(g2[0:32, 1, :], a["rwkv_g2"][0, P:P + 32, :]).then_inc(g("lora_in"), 16)
            with sp.Fori(0, 3) as i:
                n.enter(i, [2, 2])
                for p in range(D // PANEL):
                    load(sp, n, (s0 + 1 + p) % 2, rkv_panel(i, p))
            n.leave(3)
            sp.wait_ge(*g("mixed", 2 + C * FILLS))
            for t, name in R_CONST:
                sp.dma_start(t[:], a[name]).then_inc(g("const"), 16)
            sp.wait_ge(*g("gated", C + 2))
            for p in range(D // PANEL):
                load(sp, n, (s0 + 1 + p) % 2, out_panel(a["rwkv_w_o"][0], 0, C, p))

        R_CONSTS = 16 * len(R_CONST)
        xh, xl = (lambda k: xn_hi[:, k, :]), (lambda k: xn_lo[:, k, :])

        def rwkv_proj_pe(pe, n, g, s0):
            for f in range(3):
                b0 = (4, 6, 2)[f]
                nb = 2 if f == 2 else 1
                products(pe, n, (s0 + f) % 2, C, [ps[:, b0 + m, :] for m in range(nb)], xh, xl, True, True,
                         arrived=lambda k: pe.wait_ge(*g("mixed_lo", C * f + k + 3)), freed=g("freed"))
            with pe.Fori(0, 3) as i:
                n.enter(i, [2, 2])
                for p in range(D // PANEL):
                    b0 = 4 + 2 * (p % 2)
                    pe.wait_ge(*g("projected", 4 * i + p + 1))
                    products(pe, n, (s0 + 1 + p) % 2, C, [ps[:, b0, :], ps[:, b0 + 1, :]], xh, xl, True, True,
                             arrived=(lambda k: pe.wait_ge(*g("mixed_lo", C * i + 3 * C + k + 3))) if p == 0 else None,
                             freed=g("freed") if p == 3 else None)
            n.leave(3)

        def chunks(eng, body):
            body(0, 0, True, False)
            with eng.Fori(0, (C - 2) // 2) as i:
                body(2 * i + 1, 1, True, True)
                body(2 * i + 2, 0, True, True)
            body(C - 1, 1, True, True)
            body(C, 0, False, True)

        def chunk_pe(pe, g, c, par, prep, tail):
            L2, X2 = 2 * LEVELS, 2 * (LEVELS - 1)
            if prep:
                pe.wait_ge(*g("statics", 3 * c + 3))
                pe.wait_ge(*g("gated", c + 1))
                nc.tensor.matmul(ps[:, 0, :], wa_c[:, 0, :], twa[:], start=True, stop=True).then_inc(g("pre"), 1)
                nc.tensor.matmul(ps[:, 1, :], wa_c[:, 1, :], twa[:], start=True, stop=True).then_inc(g("pre"), 1)
                nc.tensor.matmul(ps[:, 3, :], ind_c[:], k_norm[:], start=True, stop=True).then_inc(g("pre"), 1)
            if tail:
                q, a_q = c - 1, ars[1 - par]
                if prep:
                    pe.wait_ge(*g("gates", 2 * c + 2))
                for t in range(NB):
                    pe.wait_ge(*g("state", NB * q + t + 1))
                    for h in range(2):
                        o = ps[:, 0, h * HEAD:(h + 1) * HEAD]
                        nc.tensor.matmul(o, a_q[:, h, t, 0, :], state[:, t % 2, :], start=True, stop=False)
                        end = nc.tensor.matmul(o, mk[:, t, h, 0, :], v_tok[:, t, h * HEAD:(h + 1) * HEAD],
                                               start=False, stop=True)
                    end.then_inc(g("u0_mm"), 1)
                    pe.wait_ge(*g("u0", NB * q + t + 1))
                    for h in range(2):
                        end = nc.tensor.matmul(ps[:, 1, h * HEAD:(h + 1) * HEAD], inv_t[:, 2 * t + h, :], u0[:, h, :],
                                               start=True, stop=True)
                    end.then_inc(g("u_mm"), 1)
                    pe.wait_ge(*g("u", NB * q + t + 1))
                    if t < NB - 1:
                        for h in range(2):
                            o = ps[h * HEAD:(h + 1) * HEAD, 0, 256:256 + HEAD]
                            at = slice(h * HEAD, (h + 1) * HEAD)
                            nc.tensor.matmul(o, b_tok[:, t, at], u[:, h, :], start=True, stop=False)
                            end = nc.tensor.matmul(o, k_tok[:, t, at], v_tok[:, t, at], start=False, stop=True)
                        end.then_inc(g("s_mm"), 1)
                    for h in range(2):
                        o = ps[h * HEAD:(h + 1) * HEAD, 2, t * P:(t + 1) * P]
                        vt = v_tok[:, t, h * HEAD:(h + 1) * HEAD]
                        nc.tensor.matmul(o, state[:, t % 2, :], a_q[:, h, t, 1, :], start=True, stop=False)
                        nc.tensor.matmul(o, u[:, h, :], mb[:, t, h, 1, :], start=False, stop=False)
                        end = nc.tensor.matmul(o, vt, mk[:, t, h, 1, :], start=False, stop=True)
                    end.then_inc(g("y_mm"), 1)
            if prep:
                for j, t in enumerate((v_c, kt, bt)):
                    if j == 1:
                        pe.wait_ge(*g("kb", c + 1))
                    for blkn in range(NB):
                        end = nc.tensor.transpose(ps[:, 4 + j, blkn * P:(blkn + 1) * P],
                                                  t[:, blkn * P:(blkn + 1) * P], ident[:])
                    end.then_inc(g("tok"), 1)
            if tail:
                pe.wait_ge(*g("y_sb", c))
                nc.tensor.matmul(ps[:, 1, :], blk[:, 1, :], yb[:], start=True, stop=True).then_inc(g("mean"), 1)
                if prep:
                    pe.wait_ge(*g("kk", c + 1))
                nc.tensor.matmul(ps[:, 3, :], blk[:, 0, :], m2[:, 1 - par, :], start=True,
                                 stop=True).then_inc(g("bonus"), 1)
                pe.wait_ge(*g("g_c", c))
                nc.tensor.matmul(ps[:, 2, :], g_c[:, 0, :], sg[:, 0, :], start=True, stop=False)
                nc.tensor.matmul(ps[:, 2, :], g_c[:, 1, :], sg[:, 1, :], start=False, stop=True).then_inc(g("gate"), 1)
            if prep:
                pe.wait_ge(*g("ar", c + 1))
                for j in range(2 * NB):
                    blkn, t = j // 2, (bt, kt)[j % 2]
                    if j in (1, 2, 3):
                        pe.wait_ge(*g("tok_sb", 3 * c + 3))
                    if j >= 4:
                        pe.wait_ge(*g("masked", 8 * c + j - 3))
                    nc.tensor.matmul(ps[:, 4 + (j + 3) % 4, :], t[:, blkn * P:(blkn + 1) * P],
                                     ars[par][:, :, blkn, :, :], start=True, stop=True).then_inc(g("attn"), 1)
            if tail:
                pe.wait_ge(*g("dev_sq", c))
                nc.tensor.matmul(ps[:, 0, :], blk[:, 1, :], qs[:], start=True, stop=True).then_inc(g("var"), 1)
            if prep:
                pe.wait_ge(*g("masked", 8 * c + 8))
                pe.wait_ge(*g("inv_start", 2 * c + 2))
                for l in range(LEVELS):
                    x_l = pairs[l % 2]
                    for G in range(2):
                        if l > 0:
                            pe.wait_ge(*g("inv", L2 * c + 2 * (l - 1) + G + 1))
                        for w in range(4):
                            un = 4 * G + w
                            o, m_t = ps[:, 4 + G, w * P:(w + 1) * P], mb[:, un // 2, un % 2, 0, :]
                            if l == 0:
                                end = nc.tensor.transpose(o, m_t, ident[:])
                            else:
                                end = nc.tensor.matmul(o, m_t, inv[:, un, :], start=True, stop=True)
                        end.then_inc(g("x_mm"), 1)
                    for G in range(2 if l > 0 else 0):
                        pe.wait_ge(*g("x_sb", X2 * c + 2 * (l - 1) + G + 1))
                        for w in range(4):
                            un = 4 * G + w
                            if l < LEVELS - 1:
                                nc.tensor.matmul(ps[:, 6 + G, w * P:(w + 1) * P], inv_t[:, un, :],
                                                 x_l[:, un, :], start=True, stop=True)
                            end = nc.tensor.matmul(ps[:, 4 + G, w * P:(w + 1) * P], x_l[:, un, :],
                                                   inv_t[:, un, :], start=True, stop=True)
                        end.then_inc(g("upd"), 1)
                pe.wait_ge(*g("inv", L2 * c + L2))

        def rwkv_pe(pe, n, g, s0):
            norm_in_pe(pe, g)
            rwkv_proj_pe(pe, n, g, s0)
            pe.wait_ge(*g("const", R_CONSTS))
            for c in range(C):
                pe.wait_ge(*g("k_sq", c + 1))
                nc.tensor.matmul(ps[0:2 * C, 0, :], ind_s[:, c, :], (m1 if c % 2 == 0 else dl)[:], start=c == 0,
                                 stop=c == C - 1).then_inc(g("k_sums"), 1)
            pe.wait_ge(*g("k_norm", 1))
            pe.wait_ge(*g("lora_in", 64))
            pe.sem_inc(g("bonus"), 1)
            chunks(pe, lambda c, par, prep, tail: chunk_pe(pe, g, c, par, prep, tail))
            out_pe(pe, n, g, (s0 + 1) % 2, KV_ROWS, xh, xl, lambda k: pe.wait_ge(*g("out_lo", k + 1)))

        def chunk_act(act, g, c, par, prep, tail):
            def solve(t):
                act.wait_ge(*g("u0_mm", NB * (c - 1) + t + 1))
                nc.scalar.activation(u0[:], ps[:, 0, 0:P].rearrange("p (h v) -> p h v", h=2),
                                     ACT.Copy).then_inc(g("u0"), 1)
                act.wait_ge(*g("u_mm", NB * (c - 1) + t + 1))
                if t > 0:
                    act.wait_ge(*g("y_mm", NB * (c - 1) + t))
                nc.scalar.activation(u[:], ps[:, 1, 0:P].rearrange("p (h v) -> p h v", h=2),
                                     ACT.Copy).then_inc(g("u"), 1)

            if prep:
                act.wait_ge(*g("pre", 3 * c + 1))
                if not isinstance(c, int) or c > 0:
                    act.wait_ge(*g("sums", c))
                    act.wait_ge(*g("bonus_in", c))
                    act.wait_ge(*g("ar", c))
                nc.scalar.activation(dl[:], ps[:, 0, :], ACT.Tanh, bias=col(w0h, c), scale=0.5).then_inc(g("tanh"), 1)
                act.wait_ge(*g("tanh", 2 * c + 1))
                nc.scalar.activation(dl[:], dl[:], ACT.Identity, bias=half_decay[:],
                                     scale=0.5 * DECAY).then_inc(g("gates"), 1)
                act.wait_ge(*g("pre", 3 * c + 2))
                nc.scalar.activation(rate[:], ps[:, 1, :], ACT.Tanh, bias=col(w0h, c + C), scale=0.5).then_inc(g("tanh"), 1)
                act.wait_ge(*g("tanh", 2 * c + 2))
                nc.scalar.activation(rate[:], rate[:], ACT.Identity, bias=half[:], scale=0.5).then_inc(g("gates"), 1)
                act.wait_ge(*g("gates", 2 * c + 2))
                nc.scalar.activation(kp[:], rate[:], ACT.Identity, bias=col(omka, c),
                                     scale=col(vec_r, V_KA + c)).then_inc(g("kp0"), 1)
            if tail:
                solve(0)
            if prep:
                act.wait_ge(*g("sums", c + 1))
                nc.scalar.activation(ex[:, :, 1:P + 1], lc[:].rearrange("p (b t) -> p b t", t=P), ACT.Exp)
                nc.scalar.activation(ex[:, :, 0:1], n_mid[:].unsqueeze(2), ACT.Exp)
                nc.scalar.activation(carry[:, par, :], carry[:, par, :], ACT.Exp).then_inc(g("exps"), 1)
                act.wait_ge(*g("exps", 2 * c + 1))
                nc.scalar.activation(lc[:], lc[:], ACT.Exp, scale=-1.0).then_inc(g("exps"), 1)
            if tail:
                for t in range(1, NB):
                    solve(t)
                act.wait_ge(*g("y_mm", NB * c))
                nc.scalar.activation(yb[:], ps[:, 2, :], ACT.Copy).then_inc(g("y_sb"), 1)
            if prep:
                for j, t in enumerate((v_tok, k_tok, b_tok)):
                    act.wait_ge(*g("tok", 3 * c + j + 1))
                    nc.scalar.activation(t[:], ps[:, 4 + j, :].rearrange("p (b t) -> p b t", t=P),
                                         ACT.Copy).then_inc(g("tok_sb"), 1)
            if tail:
                act.wait_ge(*g("dev", c))
                act.wait_ge(*g("gated", c + 1))
                nc.scalar.activation(qs[:], yb[:], ACT.Square).then_inc(g("dev_sq"), 1)
                act.wait_ge(*g("var", c))
                nc.scalar.activation(qs[:], ps[:, 0, :], ACT.Ln, bias=eps_ln[:]).then_inc(g("var_log"), 1)
                act.wait_ge(*g("var_log", c))
                nc.scalar.activation(qs[:], qs[:], ACT.Exp, scale=-0.5).then_inc(g("dev_rstd"), 1)

        def rwkv_act(act, n, g, s0, seen, more):
            out_start_act(act, g)
            norm_in_squares(act, g, seen)

            def fill(f, s_last):
                for c in range(C):
                    act.wait_ge(*g("mixed", C * f + c + 3))
                    if not isinstance(f, int) or f > 0:
                        if c < C - 1:
                            act.wait_ge(*g("freed", (C - 1) * f + c + 1 - (C - 1)))
                        else:
                            wait_used(act, n, s_last)
                    nc.scalar.activation(ch(xn_hi, c), ch(hn, c % 2), ACT.Copy).then_inc(g("mixed_hi"), 1)

            fill(0, None)
            for f in range(3):
                s = (s0 + f) % 2
                fill(f + 1, s)
                wait_used(act, n, s)
                if f == 0:
                    nc.scalar.activation(twa[0:64, :], ps[0:64, 4, :], ACT.Tanh).then_inc(g("lora"), 1)
                elif f == 1:
                    nc.scalar.activation(twa[64:128, :], ps[0:64, 6, :], ACT.Copy).then_inc(g("projected"), 2)
                else:
                    act.wait_ge(*g("zeros", 4))
                    nc.scalar.activation(sg[:, 0, :], ps[:, 2, :], ACT.Tanh, scale=0.5)
                    nc.scalar.activation(sg[0:32, 1, :], ps[0:32, 3, :], ACT.Tanh, scale=0.5).then_inc(g("lora"), 1)
                split_hi(act, n, s)

            def project(i, p, split):
                s = (s0 + 1 + p) % 2
                b0 = 4 + 2 * (p % 2)
                act.wait_ge(used[s], n.peek(s) + 1)
                for m in range(2):
                    end = nc.scalar.activation(rkv[:, bass.ds(i, 1), 2 * p + m, :], ch(ps, b0 + m), ACT.Copy)
                end.then_inc(g("projected"), 1)
                if split:
                    split_hi(act, n, s)
            with act.Fori(0, 2) as i:
                n.enter(i, [2, 2])
                for p in range(4):
                    if p == 3:
                        fill(i + 4, s0 % 2)
                    project(i, p, True)
            n.leave(2)
            for p in range(4):
                project(2, p, p < 2)
            act.wait_ge(*g("const", R_CONSTS))
            act.wait_ge(*g("projected", 2 + 12))
            act.wait_ge(*g("mixed_lo", 2 + C * FILLS))
            for c in range(C):
                if c >= 2:
                    act.wait_ge(*g("k_sums", c - 1))
                nc.scalar.activation((m1 if c % 2 == 0 else dl)[:], rkv[:, 1, c, :], ACT.Square,
                                     scale=col(vec_r, V_KK + c)).then_inc(g("k_sq"), 1)
            act.wait_ge(*g("k_sums", C))
            act.wait_ge(*g("k_zero", 1))
            nc.scalar.activation(k_norm[0:2 * C, :], ps[0:2 * C, 0, :], ACT.Sqrt).then_inc(g("k_len"), 1)
            chunks(act, lambda c, par, prep, tail: chunk_act(act, g, c, par, prep, tail))
            act.wait_ge(*g("gated", C + 2))
            for c in range(C):
                nc.scalar.activation(ch(xn_hi, c), rkv[:, 0, c:c + 1, :], ACT.Copy).then_inc(g("out_hi"), 1)
            for s in ((s0 + 1) % 2, s0):
                split_hi(act, n, s)
            out_act(act, n, g, (s0 + 1) % 2, KV_ROWS, y_rwkv, more)

        def chunk_dve(dve, g, c, par, prep, tail):
            V = nc.vector
            L2, X2 = 2 * LEVELS, 2 * (LEVELS - 1)
            b_t = lambda t: t.rearrange("p (b t) -> p b t", t=P)
            flat = lambda t: t.rearrange("p o t -> p (o t)")
            done = {"prep": 0, "tail": 0}
            STEPS = {"prep": 6, "tail": NB - 1 + 3}

            def step(kind, ins):
                done[kind] += 1
                ins.then_inc(g(kind + "_steps"), 1)
                dve.wait_ge(*g(kind + "_steps", STEPS[kind] * (c if kind == "prep" else c - 1) + done[kind]))

            def advance(t):
                q = c - 1
                dve.wait_ge(*g("s_mm", (NB - 1) * q + t + 1))
                dve.wait_ge(*g("state", NB * q + t + 1))
                step("tail", V.tensor_tensor(grown[:], state[:, t % 2, :], ps[:, 0, 256:256 + HEAD], ALU.add))
                V.tensor_scalar(state[:, (t + 1) % 2, :], grown[:], carry[:, 1 - par, t:t + 1], None,
                                ALU.mult).then_inc(g("state"), 1)

            if prep:
                r_c, k_c = (flat(rkv[:, j, bass.ds(c, 1), :]) for j in range(2))
                dve.wait_ge(*g("gates", 2 * c + 1))
                if not isinstance(c, int) or c > 0:
                    dve.wait_ge(*g("kb", c))
                for t in range(NB):
                    ins = V.tensor_tensor_scan(lc[:, t * P:(t + 1) * P], ones_row[:], dl[:, t * P:(t + 1) * P], 0.0,
                                               ALU.mult, ALU.add)
                step("prep", ins)
                V.tensor_copy(mid[:].unsqueeze(2), b_t(lc[:])[:, :, P // 2 - 1:P // 2])
                step("prep", V.tensor_scalar(n_mid[:].unsqueeze(2), b_t(lc[:])[:, :, P // 2 - 1:P // 2], -1.0, None,
                                             ALU.mult))
                step("prep", V.tensor_tensor(b_t(lc[:]), b_t(lc[:]), n_mid[:].unsqueeze(2).to_broadcast([P, NB, P]),
                                             ALU.add))
                V.tensor_copy(carry[:, par, NB - 1:NB], lc[:, S - 1:S])
                V.tensor_tensor(carry[:, par, 0:NB - 1].unsqueeze(2), b_t(lc[:])[:, 0:NB - 1, P - 1:P],
                                mid[:, 1:NB].unsqueeze(2), ALU.add).then_inc(g("sums"), 1)
                dve.wait_ge(*g("pre", 3 * c + 3))
                V.scalar_tensor_tensor(kk[:], k_c, col(vec_r, V_KK + c), ps[:, 3, :], ALU.mult,
                                       ALU.mult).then_inc(g("kk"), 1)
            if tail:
                advance(0)
            if prep:
                dve.wait_ge(*g("exps", 2 * c + 1))
                dve.wait_ge(*g("kk", c + 1))
                for h in range(2):
                    at = slice(h * HEAD, (h + 1) * HEAD)
                    V.scalar_tensor_tensor(ars[par][at, h, :, 0, :], b_t(kk[at]), -1.0, ex[at, :, 0:P],
                                           ALU.mult, ALU.mult)
            if tail:
                advance(1)
            if prep:
                for h in range(2):
                    at = slice(h * HEAD, (h + 1) * HEAD)
                    ins = V.tensor_tensor(ars[par][at, h, :, 1, :], b_t(flat(rkv[at, 0, bass.ds(c, 1), :])),
                                          ex[at, :, 1:P + 1], ALU.mult)
                ins.then_inc(g("ar"), 1)
            if tail:
                advance(2)
                dve.wait_ge(*g("mean", c))
                V.tensor_tensor(yb[:], yb[:], ps[:, 1, :], ALU.subtract).then_inc(g("dev"), 1)
            if prep:
                if tail:
                    dve.wait_ge(*g("y_mm", NB * c))
                V.memset(state[:, 0, :], 0.0).then_inc(g("state"), 1)
                step("prep", V.memset(grown[:], 0.0))
                for j in range(2 * NB):
                    dve.wait_ge(*g("attn", 8 * c + j + 1))
                    V.tensor_tensor((mb, mk)[j % 2][:, j // 2, :, :, :],
                                    ps[:, 4 + (j + 3) % 4, :].rearrange("p (h a t) -> p h a t", h=2, a=2),
                                    low2[:].unsqueeze(1).to_broadcast([P, 2, 2, P]), ALU.mult).then_inc(g("masked"), 1)

            def level(l):
                b, x_l = 1 << l, pairs[l % 2]
                split = lambda t, side: t.rearrange("p w (q two b) -> p w q two b", two=2, b=b)[:, :, :, side, :]
                bank = lambda k: ps[:, k, :].rearrange("p (w t) -> p w t", t=P)
                if l == 0:
                    dve.wait_ge(*g("masked", 8 * c + 8))
                    for G in range(2):
                        us = slice(4 * G, 4 * G + 4)
                        V.tensor_tensor(split(x_l[:, us, :], 1), split(
                            mb[:, 2 * G:2 * G + 2, :, 0, :].rearrange("p b h t -> p (b h) t"), 1),
                            split(lvl0_t[:].unsqueeze(1).to_broadcast([P, 4, P]), 1), ALU.mult)
                        dve.wait_ge(*g("x_mm", L2 * c + G + 1))
                        step("prep", V.tensor_tensor(split(x_l[:, us, :], 0), split(bank(4 + G), 0),
                                                     split(lvl[:, l, :].unsqueeze(1).to_broadcast([P, 4, P]), 0),
                                                     ALU.mult))
                        V.tensor_tensor(split(inv[:, us, :], 0), split(inv[:, us, :], 0), split(x_l[:, us, :], 0),
                                        ALU.add)
                        V.tensor_tensor(split(inv_t[:, us, :], 1), split(inv_t[:, us, :], 1),
                                        split(x_l[:, us, :], 1), ALU.add).then_inc(g("inv"), 1)
                    dve.wait_ge(*g("inv", L2 * c + 2))
                    return
                dve.wait_ge(*g("zeroed", (LEVELS - 1) * c + l))
                for G in range(2):
                    us = slice(4 * G, 4 * G + 4)
                    dve.wait_ge(*g("x_mm", L2 * c + 2 * l + G + 1))
                    V.tensor_tensor(split(x_l[:, us, :], 0), split(bank(4 + G), 0),
                                    split(lvl[:, l, :].unsqueeze(1).to_broadcast([P, 4, P]), 0), ALU.mult
                                    ).then_inc(g("x_sb"), 1)
                for G in range(2):
                    us = slice(4 * G, 4 * G + 4)
                    dve.wait_ge(*g("upd", X2 * c + 2 * (l - 1) + G + 1))
                    if l < LEVELS - 1:
                        V.tensor_tensor(split(inv[:, us, :], 0), split(inv[:, us, :], 0), split(bank(6 + G), 0),
                                        ALU.add)
                    V.tensor_tensor(split(inv_t[:, us, :], 1), split(inv_t[:, us, :], 1), split(bank(4 + G), 1),
                                    ALU.add).then_inc(g("inv"), 1)
                dve.wait_ge(*g("inv", L2 * c + 2 * l + 2))

            if prep:
                dve.wait_ge(*g("inv_start", 2 * c + 2))
                for l in range(2):
                    level(l)
            if tail:
                dve.wait_ge(*g("dev_rstd", c))
                dve.wait_ge(*g("dev", c))
                step("tail", V.tensor_tensor(yb[:], yb[:], qs[:], ALU.mult))
                dve.wait_ge(*g("bonus", c + 1))
                V.tensor_tensor(qs[:], flat(rkv[:, 2, bass.ds(c - 1, 1), :]), ps[:, 3, :], ALU.mult)
                step("tail", V.tensor_scalar(yb[:], yb[:], col(vec_r, V_LG - 1 + c), col(vec_r, V_LB - 1 + c),
                                             ALU.mult, ALU.add))
                step("tail", V.tensor_tensor(yb[:], yb[:], qs[:], ALU.add))
                dve.wait_ge(*g("gate", c))
                V.tensor_tensor(flat(rkv[:, 0, bass.ds(c - 1, 1), :]), yb[:], ps[:, 2, :],
                                ALU.mult).then_inc(g("gated"), 1)
            if prep:
                for l in range(2, LEVELS):
                    level(l)
            assert not prep or done["prep"] == STEPS["prep"], done
            assert not tail or done["tail"] == STEPS["tail"], done

        def rwkv_dve(dve, n, g, s0, seen, more):
            dve.sem_inc(g("mixed"), 2)
            dve.sem_inc(g("mixed_lo"), 2)
            dve.wait_ge(*g("rstd", 1))
            nc.vector.memset(h_pad[:, :, 0:1], 0.0)
            for c in range(C):
                nc.vector.scalar_tensor_tensor(h_pad[:, c, 1:S + 1], x[:, c, :], col(vec_n, gain(1, 2, c)),
                                               rstd[:], ALU.mult, ALU.mult).then_inc(g("h"), 1)
            dve.wait_ge(*g("h", C))

            def fill(f):
                for c in range(C + 1):
                    if c < C:
                        dve.wait_ge(*g("xx", C * f + c + 1))
                        dve.wait_ge(*g("mixed_lo", C * f + c + 1))
                        nc.vector.scalar_tensor_tensor(hn[:, c % 2, :], sil[:, c % 2, :],
                                                       col(vec_r, C * f + (V_MIX + c)), h_pad[:, c, 1:S + 1],
                                                       ALU.mult, ALU.add).then_inc(g("mixed"), 1)
                    if c >= 1:
                        dve.wait_ge(*g("mixed_hi", C * f + c))
                        nc.vector.tensor_tensor(ch(xn_lo, c - 1), ch(hn, (c - 1) % 2),
                                                ch(xn_hi, c - 1).bitcast(F32), ALU.subtract).then_inc(g("mixed_lo"), 1)

            fill(0)
            for f in range(3):
                fill(f + 1)
                if f == 2:
                    dve.wait_ge(*g("lora", 2))
                    nc.vector.tensor_scalar(sg[:, 0, :], sg[:, 0, :], 0.5, 0.5, ALU.mult, ALU.add)
                    nc.vector.tensor_scalar(sg[0:32, 1, :], sg[0:32, 1, :], 0.5, 0.5, ALU.mult,
                                            ALU.add).then_inc(g("sg"), 1)
                split_lo(dve, n, (s0 + f) % 2)
            with dve.Fori(0, 2) as i:
                n.enter(i, [2, 2])
                for p in range(4):
                    if p == 3:
                        fill(i + 4)
                    split_lo(dve, n, (s0 + 1 + p) % 2)
            n.leave(2)
            for p in range(4):
                if p < 2:
                    split_lo(dve, n, (s0 + 1 + p) % 2)
            nc.vector.tensor_scalar(omka[:], vec_r[:, V_KA:V_KA + C], -1.0, 1.0, ALU.mult, ALU.add)
            nc.vector.tensor_scalar(w0h[:], vec_r[:, V_W0:V_W0 + 2 * C], 0.5, None, ALU.mult)
            nc.vector.memset(ones_row[:], 1.0)
            nc.vector.memset(half_decay[:], 0.5 * DECAY)
            nc.vector.memset(half[:], 0.5)
            nc.vector.memset(eps_ln[:], 64e-5).then_inc(g("tables"), 1)
            dve.wait_ge(*g("tables", 1))
            dve.wait_ge(*g("k_len", 1))
            nc.vector.tensor_scalar(k_norm[0:2 * C, :], k_norm[0:2 * C, :], 1e-12, None, ALU.max).then_inc(g("k_max"), 1)
            dve.wait_ge(*g("k_max", 1))
            nc.vector.reciprocal(k_norm[0:2 * C, :], k_norm[0:2 * C, :]).then_inc(g("k_norm"), 1)
            dve.wait_ge(*g("ar_zero", 6))
            dve.sem_inc(g("gated"), 2)
            chunks(dve, lambda c, par, prep, tail: chunk_dve(dve, g, c, par, prep, tail))
            for c in range(C):
                dve.wait_ge(*g("out_hi", c + 1))
                nc.vector.tensor_tensor(ch(xn_lo, c), rkv[:, 0, c:c + 1, :], ch(xn_hi, c).bitcast(F32),
                                        ALU.subtract).then_inc(g("out_lo"), 1)
            out_start(g)
            for s in ((s0 + 1) % 2, s0):
                split_lo(dve, n, s)
            out_dve(dve, n, g, (s0 + 1) % 2, KV_ROWS, y_rwkv, (vec_n, gain(1, 3, 0)), seen, more)


        def rwkv_pool(pool, g, before):
            pool.wait_ge(*before("y_mean", 1))
            for j, t in enumerate((wa2, g2, sg)):
                nc.gpsimd.memset(t[:], 0.0).then_inc(g("zeros"), 1)
                pool.wait_ge(*g("zeros", j + 1))
            pool.sem_inc(g("zeros"), 1)
            pool.wait_ge(*g("h", C))
            with pool.Fori(0, FILLS) as f:
                for c in range(C):
                    pool.wait_ge(*g("mixed", C * f + c + 1))
                    nc.gpsimd.tensor_tensor(sil[:, c % 2, :], h_pad[:, c, 0:S], h_pad[:, c, 1:S + 1],
                                            ALU.subtract).then_inc(g("xx"), 1)
                    pool.wait_ge(*g("xx", C * f + c + 1))
            pool.wait_ge(*g("const", R_CONSTS))
            pool.wait_ge(*g("mixed_lo", 2 + C * FILLS))
            nc.gpsimd.memset(k_norm[:], 0.0).then_inc(g("k_zero"), 1)
            pool.wait_ge(*g("k_zero", 1))
            pool.wait_ge(*g("projected", 14))
            zeroed = [(t[(1 - h) * HEAD:(2 - h) * HEAD, h, :, :, :]) for t in ars for h in range(2)] + [
                t[:] for t in pairs]
            for j, t in enumerate(zeroed):
                nc.gpsimd.memset(t, 0.0).then_inc(g("ar_zero"), 1)
                pool.wait_ge(*g("ar_zero", j + 1))
            pool.wait_ge(*g("lora_in", 64))
            statics(pool, g, 0)
            chunks(pool, lambda c, par, prep, tail: chunk_pool(pool, g, c, par, prep, tail))

        def statics(pool, g, c):
            copies = [(wa_c[:], wa2[:, :, bass.ds(c * P, P)]), (ind_c[:], ind_b[:, bass.ds(c * P, P)]),
                      (v_c[:].unsqueeze(1), rkv[:, 2, bass.ds(c, 1), :])]
            for j, (o, i) in enumerate(copies):
                nc.gpsimd.tensor_copy(o, i).then_inc(g("statics"), 1)
                pool.wait_ge(*g("statics", 3 * c + j + 1))

        def chunk_pool(pool, g, c, par, prep, tail):
            if not prep:
                return
            flat = lambda t: t.rearrange("p o t -> p (o t)")
            r_c, k_c = (flat(rkv[:, j, bass.ds(c, 1), :]) for j in range(2))
            G = nc.gpsimd

            def one(name, at, ins):
                ins.then_inc(g(name), 1)
                pool.wait_ge(*g(name, at))

            pool.wait_ge(*g("kp0", c + 1))
            one("pool", 4 * c + 1, G.tensor_tensor(kp[:], kp[:], k_c, ALU.mult))
            pool.wait_ge(*g("kk", c + 1))
            one("pool", 4 * c + 2, G.tensor_tensor(rate[:], rate[:], kk[:], ALU.mult))
            pool.wait_ge(*g("exps", 2 * c + 2))
            if tail:
                pool.wait_ge(*g("attn", 8 * c))
            one("pool", 4 * c + 3, G.tensor_tensor(kt[:], kp[:], lc[:], ALU.mult))
            one("kb", c + 1, G.tensor_tensor(bt[:], rate[:], lc[:], ALU.mult))
            if tail:
                pool.wait_ge(*g("bonus", c))
            one("pool", 4 * c + 4, G.tensor_tensor(m2[:, par, :], kp[:], r_c, ALU.mult))
            one("bonus_in", c + 1, G.tensor_tensor(m2[:, par, :], m2[:, par, :],
                                                    col(vec_r, V_RK + c).to_broadcast([P, S]), ALU.mult))
            if tail:
                pool.wait_ge(*g("y_mm", NB * c))
            for j, t in enumerate((inv, inv_t)):
                pool.sem_inc(g("copying"), 1)
                one("inv_start", 2 * c + j + 1,
                    G.tensor_copy(t[:], ident[:].unsqueeze(1).to_broadcast([P, UNITS, P])))
            for l in range(1, LEVELS):
                if l == 2:
                    pool.wait_ge(*g("inv", 2 * LEVELS * c + 2))
                elif l > 2:
                    pool.wait_ge(*g("upd", 2 * (LEVELS - 1) * c + 2 * (l - 3) + 2))
                side = pairs[l % 2][:].rearrange("p w (q two b) -> p w q two b", two=2, b=1 << l)[:, :, :, 1, :]
                pool.sem_inc(g("copying"), 1)
                one("zeroed", (LEVELS - 1) * c + l, G.memset(side, 0.0))
                if l == 2:
                    if tail:
                        pool.wait_ge(*g("gate", c))
                    one("g_c", c + 1, G.tensor_copy(g_c[:], g2[:, :, bass.ds(c * P, P)]))
                    if not isinstance(c, int) or c < C - 1:
                        pool.wait_ge(*g("pre", 3 * c + 3))
                        pool.wait_ge(*g("tok", 3 * c + 1))
                        statics(pool, g, c + 1)

        st = signals("start")
        fin = signals("end")

        def start_sp(sp):
            sp.dma_start(ident[:], a["consts"][:, 0:P]).then_inc(consts_in, 16)
            sp.dma_start(ones_d[:], a["consts"][:, P:2 * P]).then_inc(consts_in, 16)
            sp.dma_start(rows_n[:], a["norm_g"].rearrange("l i (c p) -> (l i c) p", p=P)).then_inc(consts_in, 16)
            at = 0
            for name in [r for n in ROWS for r in (MIXES if n == "rwkv_mix" else [n])]:
                if isinstance(name, int):
                    v = a["rwkv_mix"][0, name:name + 1].rearrange("m (c p) -> (m c) p", p=P)
                    sp.dma_start(rows_r[at:at + C, :], v).then_inc(consts_in, 16)
                    at += C
                    continue
                v = a[name].rearrange(VIEWS.get(name, "o (c p) -> (o c) p"), **({"h": 2} if name == "rwkv_r_k" else {"p": P}))
                sp.dma_start(rows_r[at:at + v.shape[0], :], v).then_inc(consts_in, 16)
                at += v.shape[0]
            sp.dma_start(xt[:], a["x"].rearrange("b (t p) d -> p (b t) d", p=P)).then_inc(x_in, 16)

        def start_pe(pe):
            pe.wait_ge(consts_in, 48 + 16 * (len(ROWS) + 5))
            pe.wait_ge(x_in, 16)
            for c in range(C):
                if c >= 6:
                    pe.wait_ge(x_ready, c - 5)
                for t in range(S // P):
                    end = nc.tensor.transpose(ps[:, c % 6, t * P:(t + 1) * P], xt[:, t, c * P:(c + 1) * P], ident[:])
                end.then_inc(st("x"), 1)
            nr = 2 * NG * C
            nc.tensor.transpose(ps[:, 6, 0:nr], rows_n[:], ident[0:nr, 0:nr]).then_inc(st("vec"), 1)
            nc.tensor.transpose(ps[:, 7, 0:N_ROWS], rows_r[0:N_ROWS, :], ident[0:N_ROWS, 0:N_ROWS]).then_inc(st("vec"), 1)
            pe.wait_ge(x_ready, C)

        def start_dve(dve):
            for s in range(2):
                dve.sem_inc(lo_done[s], 1)
            nc.vector.memset(eps_rms[:], 1e-6).then_inc(st("eps"), 1)
            for c in range(C):
                dve.wait_ge(*st("x", c + 1))
                nc.vector.tensor_copy(ch(x, c), ch(ps, c % 6)).then_inc(x_ready, 1)
            dve.wait_ge(*st("vec", 2))
            nc.vector.tensor_copy(vec_r[:, 0:N_ROWS], ps[:, 7, 0:N_ROWS]).then_inc(st("vecs"), 1)
            nr = 2 * NG * C
            nc.vector.tensor_copy(vec_n[:, 0:nr], ps[:, 6, 0:nr])
            nc.vector.tensor_scalar(vec_h[:, 0:nr], ps[:, 6, 0:nr], 0.5, None, ALU.mult).then_inc(st("vecs"), 1)
            dve.wait_ge(*st("vecs", 2))
            n_dve = SlotCount()
            for s in range(2):
                split_lo(dve, n_dve, s)
            return n_dve

        def start_act(act):
            n_act = SlotCount()
            act.wait_ge(*st("eps", 1))
            for s in range(2):
                split_hi(act, n_act, s)
            return n_act

        def end_pe(pe, seen):
            for c in range(C):
                pe.wait_ge(x_ready, seen + c + 1)
                for t in range(S // P):
                    b = 2 * t + c // 4
                    end = nc.tensor.transpose(ps[:, b, (c % 4) * P:(c % 4 + 1) * P], x[:, c, t * P:(t + 1) * P],
                                              ident[:])
                end.then_inc(fin("x"), 1)

        def end_evac(eng, copy, t, g):
            eng.wait_ge(*fin("x", C))
            for h in range(2):
                end = copy(ot[:, t, h * 512:(h + 1) * 512], ps[:, 2 * t + h, :])
                end.then_inc(g, 1)

        def end_sp(sp):
            o = out.rearrange("b (t p) d -> p (b t) d", p=P)
            for t in range(S // P):
                sp.wait_ge(*fin(f"done{t % 2}", 2 * (t // 2 + 1)))
                sp.dma_start(o[:, t:t + 1, :], ot[:, t:t + 1, :]).then_inc(out_done, 16)
            sp.wait_ge(out_done, 16 * (S // P))

        sig = {name: signals(name, stages[:e]) for e, name in enumerate(stages)}
        layer = {"ffn0a": (0, 0), "ffn0b": (0, 1), "ffn1a": (1, 0), "ffn1b": (1, 1)}
        slot0 = {}
        s = 0
        for name in stages:
            slot0[name] = s
            if name == "rwkv":
                s = 1 - s
        block = ctx.enter_context(nc.Block())

        @block.sync
        def _(sp):
            start_sp(sp)
            n = SlotCount()
            for e, name in enumerate(stages):
                if name in layer:
                    ffn_sp(sp, n, *layer[name], slot0[name])
                if name == "attn":
                    attn_sp(sp, n, sig[name], sig[stages[e - 1]], slot0[name])
                if name == "rwkv":
                    rwkv_sp(sp, n, sig[name], sig[stages[e - 1]], slot0[name])
            end_sp(sp)

        @block.scalar
        def _(act):
            n = start_act(act)
            for e, name in enumerate(stages):
                if name in layer:
                    ffn_act(act, n, sig[name], slot0[name], e * C, e < len(stages) - 1)
                if name == "attn":
                    attn_act(act, n, sig[name], slot0[name], e * C, e < len(stages) - 1)
                if name == "rwkv":
                    rwkv_act(act, n, sig[name], slot0[name], e * C, e < len(stages) - 1)
            end_evac(act, lambda o, i: nc.scalar.activation(o, i, ACT.Copy), 1, fin("done1"))
            end_evac(act, lambda o, i: nc.scalar.activation(o, i, ACT.Copy), 3, fin("done1"))

        @block.vector
        def _(dve):
            n = start_dve(dve)
            for e, name in enumerate(stages):
                if name in layer:
                    ffn_dve(dve, n, sig[name], slot0[name], *layer[name], (e + 1) * C, e < len(stages) - 1)
                if name == "attn":
                    attn_dve(dve, n, sig[name], slot0[name], (e + 1) * C, e < len(stages) - 1)
                if name == "rwkv":
                    rwkv_dve(dve, n, sig[name], slot0[name], (e + 1) * C, e < len(stages) - 1)
            end_evac(dve, nc.vector.tensor_copy, 0, fin("done0"))
            end_evac(dve, nc.vector.tensor_copy, 2, fin("done0"))

        @block.tensor
        def _(pe):
            for s in range(2):
                pe.sem_inc(used[s], 1)
            start_pe(pe)
            n = SlotCount()
            for name in stages:
                if name in layer:
                    ffn_pe(pe, n, sig[name], slot0[name])
                if name == "attn":
                    attn_pe(pe, n, sig[name], slot0[name])
                if name == "rwkv":
                    rwkv_pe(pe, n, sig[name], slot0[name])
            end_pe(pe, len(stages) * C)


        @block.gpsimd
        def _(pool):
            for e, name in enumerate(stages):
                if name == "attn":
                    attn_pool(pool, sig[name], sig[stages[e - 1]])
                if name == "rwkv":
                    rwkv_pool(pool, sig[name], sig[stages[e - 1]])


def constants():
    import numpy as np
    small = np.concatenate([np.eye(P), np.full((P, P), 1.0 / D)], axis=1).astype(np.float32)
    inv = (np.float32(10000.0) ** (-np.arange(0, 64, 2, dtype=np.float32) / np.float32(64))).astype(np.float32)
    ang = np.arange(S, dtype=np.float32)[None, :] * inv[:, None]
    cos, sin = np.cos(ang), np.sin(ang)
    i = np.arange(P)
    swap = np.zeros((P, P), np.float32)
    swap[i ^ 32, i] = 1.0
    head = i[:, None] // 64 == i[None, :] // 64
    lower_of_pair = lambda i, b: ((i[:, None] // b) % 2 == 1) & (i[None, :] // b == i[:, None] // b - 1)
    return {
        "consts": small,
        "cos": np.concatenate([cos] * 4).astype(np.float32),
        "sin": np.concatenate([-sin, sin] * 2).astype(np.float32),
        "rot_m": swap,
        "tri_i": (i[None, :] <= i[:, None]).astype(np.int32),
        "tri_t": (i[:, None] <= i[None, :]).astype(np.float32),
        "lvl": np.concatenate([lower_of_pair(i, 1 << l) for l in range(7)], axis=1).astype(np.float32),
        "lvl0_t": lower_of_pair(i, 1).T.astype(np.float32),
        "low2": np.concatenate([i[:, None] < i[None, :], i[:, None] <= i[None, :]], axis=1).astype(np.float32),
        "blk": np.concatenate([head, head / 64], axis=1).astype(np.float32),
        "ind_b": (i[:, None] == np.arange(D)[None, :] // 64).astype(np.float32),
        "ind_s": np.concatenate([2 * c + i[:, None] // 64 == np.arange(16)[None, :] for c in range(C)],
                                axis=1).astype(np.float32),
        "tri_u": (i[:, None] > i[None, :]).astype(np.float32),
    }


STAGES = ["ffn0a", "attn", "ffn0b", "ffn1a", "rwkv", "ffn1b"]


def kernel(**inputs):
    import numpy as np
    import concourse.bacc as bacc
    from concourse.bass_utils import run_bass_kernel_spmd as run
    nc = bacc.Bacc("TRN2", target_bir_lowering=False, num_devices=1)
    arrays = {k: np.ascontiguousarray(v) for k, v in {**inputs, **constants()}.items()}
    a = {k: nc.dram_tensor(k, v.shape, mybir.dt.from_np(v.dtype), kind="ExternalInput").ap()
         for k, v in arrays.items()}
    out = nc.dram_tensor("out", (1, S, D), F32, kind="ExternalOutput").ap()
    build(nc, a, out, STAGES)
    r = run(nc, [arrays], core_ids=[0])
    return r.results[0]["out"]
```

```python
import math
from contextlib import ExitStack

import concourse.bass as bass
from concourse import mybir

F32 = mybir.dt.float32
F32R = mybir.dt.float32r
I32 = mybir.dt.int32
ACT = mybir.ActivationFunctionType
ALU = mybir.AluOpType
AX = mybir.AxisListType

P = 128
D = 1024
S = 512
DFF = 2816
C = D // P
FC = DFF // P
PANEL = 256
PK = 8
NG = 6


MIXES = [1, 4, 5, 0, 2, 3]
ROWS = ["attn_b_qkv", "rwkv_mix", "rwkv_w0", "rwkv_a0", "rwkv_k_k", "rwkv_k_a", "rwkv_r_k", "rwkv_lnx_g",
        "rwkv_lnx_b"]
VIEWS = {"rwkv_mix": "o m (c p) -> (o m c) p", "rwkv_r_k": "o (c h) k -> (o c) (h k)"}
N_ROWS = 12 + 6 * C + 7 * C


def kind_of(stage):
    return "ffn" if stage.startswith("ffn") else stage


def groups_of(k):
    return [(a, min(PK, k - a)) for a in range(0, k, PK)]


class SlotCount:

    def __init__(self):
        self.base, self.i, self.per, self.local = [0, 0], 0, [0, 0], [0, 0]

    def enter(self, i, per):
        self.base = [b + l for b, l in zip(self.base, self.local)]
        self.i, self.per, self.local = i, per, [0, 0]

    def leave(self, n):
        assert self.local == self.per
        self.base = [b + n * p for b, p in zip(self.base, self.per)]
        self.i, self.per, self.local = 0, [0, 0], [0, 0]

    def peek(self, s):
        k = self.base[s] + self.local[s]
        return self.i * self.per[s] + k if self.per[s] and not isinstance(self.i, int) else k + self.i * self.per[s]

    def next(self, s):
        k = self.peek(s)
        self.local[s] += 1
        return k


NORM = {"squares": C, "summed": C, "log": 1, "rstd": 1}
OPERAND = {"hi": C, "xn": C}
OUT = {"y_squares": 4 + C, "y": 4 + C, "y_sum": 2 + C, "y_mean": 1, "y_log": 1, "y_rstd": 1, "y_scaled": C}
FFN = {"gate_scaled": 1 + FC // 2, "silu": FC // 2, "factor": FC,
       "product": 1 + FC // 2, "hid_hi": FC // 2, "hid": 1 + FC // 2}
SHARED = {"ffn": {**NORM, **OPERAND, **OUT, **FFN}, "attn": {**NORM, **OPERAND, **OUT}, "rwkv": {**NORM, **OUT}}


class Signals:

    def __init__(self, nc, ctx, stage, shared, earlier):
        self.nc, self.ctx, self.stage, self.shared, self.own = nc, ctx, stage, shared, {}
        self.counted = {}
        for kind in earlier:
            for name, times in SHARED[kind].items():
                self.counted[name] = self.counted.get(name, 0) + times

    def __call__(self, name, count=None):
        common = any(name in names for names in SHARED.values())
        made, full = (self.shared, name) if common else (self.own, f"{self.stage}_{name}")
        if name not in made:
            made[name] = self.ctx.enter_context(self.nc.semaphore(full))
        if count is None:
            return made[name]
        return made[name], count + (self.counted.get(name, 0) if common else 0)


def build(nc, a, out, stages):
    with ExitStack() as ctx:
        start = (nc.sbuf_base + 31) // 32 * 32
        place = {"at": 0}

        def sb(name, shape, dt, offset):
            return nc.alloc_sbuf_tensor_at(name, shape, dt, offset=start + offset)

        def take(nbytes):
            at = place["at"]
            place["at"] = at + (nbytes + 31) // 32 * 32
            return at

        o_x = take(C * S * 4)
        o_raw = take(2 * PK * PANEL * 4)
        o_whi = take(2 * PK * PANEL * 4)
        o_wlo = take(2 * PK * PANEL * 4)
        o_xnh = take(C * S * 4)
        o_xnl = take(C * S * 4)
        o_arena = take(2 * FC * S * 4)
        o_tmp = take(8 * S * 4)
        o_const = take(4 * P * 4)

        x = sb("x", [P, C, S], F32, o_x)
        w_raw = sb("w_raw", [P, 2, PK, PANEL], F32, o_raw)
        w_hi = sb("w_hi", [P, 2, PK, PANEL], F32R, o_whi)
        w_lo = sb("w_lo", [P, 2, PK, PANEL], F32R, o_wlo)
        xn_hi = sb("xn_hi", [P, C, S], F32R, o_xnh)
        xn_lo = sb("xn_lo", [P, C, S], F32R, o_xnl)
        hid_hi = sb("hid_hi", [P, FC, S], F32R, o_arena)
        hid_lo = sb("hid_lo", [P, FC, S], F32R, o_arena + FC * S * 4)
        y_ffn = sb("y_ffn", [P, C, S], F32, o_xnh)
        sq = sb("sq", [P, 2, S], F32, o_tmp)
        rstd = sb("rstd", [P, S], F32, o_tmp + 2 * S * 4)
        acc = sb("acc", [P, S], F32, o_tmp + 3 * S * 4)
        hn = sb("hn", [P, 2, S], F32, o_tmp + 4 * S * 4)
        sil = sb("sil", [P, 2, S], F32, o_tmp + 6 * S * 4)
        ident = sb("ident", [P, P], F32, o_const)
        ones_d = sb("ones_d", [P, P], F32, o_const + P * 4)
        vec_n = sb("vec_n", [P, 2 * NG * C], F32, o_const + 2 * P * 4)
        vec_h = sb("vec_h", [P, 2 * NG * C], F32, o_const + 3 * P * 4)
        o_vr = take(P * 4)
        vec_r = sb("vec_r", [P, P], F32, o_vr)
        o_eps = take(32)
        eps_rms = sb("eps_rms", [P, 1], F32, o_eps)
        assert start + place["at"] <= nc.sbuf_usable_end, place

        xt = sb("xt", [P, S // P, D], F32, o_arena)
        rows_n = sb("rows_n", [2 * NG * C, P], F32, o_arena + 4 * D * 4)
        rows_r = sb("rows_r", [P, P], F32, o_arena + 4 * D * 4 + P * 4)
        ot = sb("ot", [P, S // P, D], F32, o_arena)

        ps = ctx.enter_context(nc.psum_tensor("ps", [P, 8, 512], F32))

        def sem(name):
            return ctx.enter_context(nc.semaphore(name))

        loaded = [sem("loaded0"), sem("loaded1")]
        hi_done = [sem("hi_done0"), sem("hi_done1")]
        lo_done = [sem("lo_done0"), sem("lo_done1")]
        used = [sem("used0"), sem("used1")]
        consts_in, x_in, out_done = sem("consts_in"), sem("x_in"), sem("out_done")
        x_loaded, x_ready = sem("x_loaded"), sem("x_ready")

        shared = {}

        def signals(stage, earlier=()):
            return Signals(nc, ctx, stage, shared, [kind_of(e) for e in earlier])

        def ch(t, c):
            return t[:, bass.ds(c, 1), :]

        def col(v, c):
            return v[:, bass.ds(c, 1)]

        def gain(l, i, c):
            return (l * NG + i) * C + c

        def x_at(seen, k):
            return (x_ready, seen - C + k) if seen else (x_loaded, k)

        def load(sp, n, s, src, cols=PANEL):
            k = n.next(s)
            sp.wait_ge(lo_done[s], k + 1)
            sp.dma_start(w_raw[:, s, 0:src.shape[1], 0:cols], src).then_inc(loaded[s], 16)

        def split_hi(act, n, s):
            k = n.next(s)
            act.wait_ge(loaded[s], (k + 1) * 16)
            act.wait_ge(used[s], k + 1)
            nc.scalar.activation(w_hi[:, s, :, :], w_raw[:, s, :, :], ACT.Copy).then_inc(hi_done[s], 1)

        def split_lo(dve, n, s):
            k = n.next(s)
            dve.wait_ge(hi_done[s], k + 1)
            nc.vector.tensor_tensor(w_lo[:, s, :, :], w_raw[:, s, :, :], w_hi[:, s, :, :].bitcast(F32),
                                    ALU.subtract).then_inc(lo_done[s], 1)

        def wait_used(eng, n, s):
            eng.wait_ge(used[s], n.peek(s) + 1)

        def products(pe, n, s, count, banks, hi, lo, first, last, arrived=None, widths=(P, P), freed=None):
            pe.wait_ge(lo_done[s], n.next(s) + 2)
            for k in range(count):
                if arrived:
                    arrived(k)
                for m, bank in enumerate(banks):
                    wh = w_hi[:, s, k, m * P:m * P + widths[m]]
                    wl = w_lo[:, s, k, m * P:m * P + widths[m]]
                    nc.tensor.matmul(bank, wh, hi(k), start=first and k == 0, stop=False)
                    nc.tensor.matmul(bank, wh, lo(k), start=False, stop=False)
                    end = nc.tensor.matmul(bank, wl, hi(k), start=False, stop=last and k == count - 1)
                if freed and k < count - 1:
                    end.then_inc(freed, 1)
            end.then_inc(used[s], 1)

        NORM_SET = "natural_log_exp_and_others"


        def norm_in_pe(pe, g):
            for c in range(C):
                pe.wait_ge(*g("squares", c + 1))
                nc.tensor.matmul(ps[:, 1, :], ones_d[:], sq[:, c % 2, :], start=c == 0,
                                 stop=c == C - 1).then_inc(g("summed"), 1)

        def norm_in_squares(act, g, seen):
            for c in range(C):
                act.wait_ge(*x_at(seen, c + 1))
                if c >= 2:
                    act.wait_ge(*g("summed", c - 1))
                nc.scalar.activation(ch(sq, c % 2), ch(x, c), ACT.Square).then_inc(g("squares"), 1)
            act.wait_ge(*g("summed", C))
            nc.scalar.activation(rstd[:], ps[:, 1, :], ACT.Ln, bias=eps_rms[:]).then_inc(g("log"), 1)
            act.wait_ge(*g("log", 1))
            nc.scalar.activation(rstd[:], rstd[:], ACT.Exp, scale=-0.5).then_inc(g("rstd"), 1)

        def operand_act(act, g, l, i, seen, bank):
            for c in range(C):
                act.wait_ge(*x_at(seen, c + 1))
                nc.scalar.activation(ch(xn_hi, c), ch(x, c), ACT.Identity,
                                     scale=col(vec_n, gain(l, i, c))).then_inc(g("hi"), 1)
                if c >= 2:
                    act.wait_ge(*g("summed", c - 1))
                nc.scalar.activation(ch(sq, c % 2), ch(x, c), ACT.Square).then_inc(g("squares"), 1)
            act.wait_ge(*g("summed", C))
            nc.scalar.activation(rstd[:], ps[:, bank, :], ACT.Ln, bias=eps_rms[:]).then_inc(g("log"), 1)
            act.wait_ge(*g("log", 1))
            nc.scalar.activation(rstd[:], rstd[:], ACT.Exp, scale=-0.5).then_inc(g("rstd"), 1)

        def operand_dve(dve, g, l, i, ffn):
            def low(c):
                if c == 0 and ffn:
                    dve.sem_inc(g("gate_scaled"), 1)
                    dve.sem_inc(g("product"), 1)
                    dve.sem_inc(g("hid"), 1)
                dve.wait_ge(*g("hi", c + 1))
                nc.vector.scalar_tensor_tensor(ch(xn_lo, c), ch(x, c), col(vec_n, gain(l, i, c)),
                                               ch(xn_hi, c).bitcast(F32), ALU.mult,
                                               ALU.subtract).then_inc(g("xn"), 1)
            return low

        def sum_squares(pe, g, c, bank):
            pe.wait_ge(*g("squares", c + 1))
            nc.tensor.matmul(ps[:, bank, :], ones_d[:], sq[:, c % 2, :], start=c == 0,
                             stop=c == C - 1).then_inc(g("summed"), 1)

        def operand_pe(pe, g, bank):
            def arrived(k):
                if k >= 1:
                    sum_squares(pe, g, k - 1, bank)
                pe.wait_ge(*g("xn", k + 1))
            return arrived

        def out_pe(pe, n, g, s0, rows, hi, lo, arrived):
            def body(i, q0):
                s = s0
                for q in range(2):
                    pe.wait_ge(*g("y", 4 * i + 2 * q + 2))
                    for r, (k0, nk) in enumerate(rows):
                        products(pe, n, s, nk, [ps[:, 4 + 2 * q, :], ps[:, 5 + 2 * q, :]],
                                 lambda k: hi(k0 + k), lambda k: lo(k0 + k), r == 0, r == len(rows) - 1,
                                 arrived=(lambda k: arrived(k0 + k)))
                        s = 1 - s
            per = [len(rows), len(rows)]
            with pe.Fori(0, 2) as i:
                n.enter(i, per)
                body(i, 0)
            n.leave(2)
            pe.wait_ge(*g("y_sum", 2 + C))
            nc.tensor.matmul(ps[:, 0, :], ones_d[:], acc[:], start=True, stop=True).then_inc(g("y_mean"), 1)

        def out_uses(s0, rows):
            r = len(rows)
            return [((s0 + u) % 2, u // r if u % r == r - 1 else None) for u in range(2 * r)]

        def out_act(act, n, g, s0, rows, y, more, late=True):
            act.preload_act_table_set(NORM_SET)
            uses = out_uses(s0, rows)
            for i in range(2):
                n.enter(0, [len(rows), len(rows)])
                for u, (s, panel) in enumerate(uses):
                    last = i == 1 and u == len(uses) - 1
                    if panel is not None:
                        if last and not more:
                            act.wait_ge(used[s], n.peek(s) + 1)
                        else:
                            wait_used(act, n, s)
                        for m in range(2):
                            act.wait_ge(*g("y_sum", 4 * i + 2 * panel + m + 1))
                            nc.scalar.activation(ch(sq, m), ch(ps, 4 + 2 * panel + m),
                                                 ACT.Square).then_inc(g("y_squares"), 1)
                        for m in range(2):
                            nc.scalar.activation(ch(y, 4 * i + 2 * panel + m), ch(ps, 4 + 2 * panel + m),
                                                 ACT.Copy).then_inc(g("y"), 1)
                    if last and not late:
                        split_hi(act, n, s)
                    if last:
                        act.wait_ge(*g("y_mean", 1))
                        nc.scalar.activation(rstd[:], ps[:, 0, :], ACT.Ln, bias=eps_rms[:]).then_inc(g("y_log"), 1)
                        act.wait_ge(*g("y_log", 1))
                        nc.scalar.activation(rstd[:], rstd[:], ACT.Exp, scale=-0.5).then_inc(g("y_rstd"), 1)
                    if last and not late:
                        continue
                    if more or i == 0 or u < len(uses) - 2:
                        split_hi(act, n, s)
                    else:
                        n.next(s)
                n.leave(1)

        def out_dve(dve, n, g, s0, rows, y, gains, seen, more, low=None, late=True):
            uses = out_uses(s0, rows)
            for i in range(2):
                n.enter(0, [len(rows), len(rows)])
                for u, (s, panel) in enumerate(uses):
                    last = i == 1 and u == len(uses) - 1
                    if panel is not None:
                        for m in range(2):
                            c = 4 * i + 2 * panel + m
                            dve.wait_ge(*g("y_squares", c + 5))
                            dve.wait_ge(*g("y_sum", c + 2))
                            nc.vector.tensor_tensor(acc[:], acc[:], sq[:, m, :],
                                                    ALU.add).then_inc(g("y_sum"), 1)
                    if last and not late:
                        split_lo(dve, n, s)
                    if last:
                        dve.wait_ge(*g("y_rstd", 1))
                        for c in range(C + 2):
                            if c < C:
                                if c >= 2:
                                    dve.wait_ge(*x_at(seen, c - 1))
                                nc.vector.scalar_tensor_tensor(ch(hn, c % 2), ch(y, c),
                                                               col(gains[0], gains[1] + c), rstd[:], ALU.mult,
                                                               ALU.mult).then_inc(g("y_scaled"), 1)
                            if low and c >= 2:
                                low(c - 2)
                    if last and not late:
                        continue
                    if more or i == 0 or u < len(uses) - 2:
                        split_lo(dve, n, s)
                    else:
                        n.next(s)
                n.leave(1)

        def out_pool(pool, g, seen):
            for c in range(C):
                pool.wait_ge(*g("y_scaled", c + 1))
                nc.gpsimd.tensor_tensor(ch(x, c), ch(x, c), ch(hn, c % 2), ALU.add).then_inc(x_ready, 1)
                pool.wait_ge(*x_at(seen, c + 1))

        def out_start(g):
            nc.vector.memset(acc[:], 0.0).then_inc(g("y_sum"), 2)

        def out_start_act(act, g):
            act.sem_inc(g("y_squares"), 4)
            act.sem_inc(g("y"), 4)

        FP = FC // 2
        HID_ROWS = groups_of(FC)

        def w_in_panel(l, f, half, j):
            w = a["ffn_w_in"][l, f].rearrange("(k p) n -> p k n", p=P)
            return w[:, :, bass.ds(j * PANEL + half * DFF, PANEL)]

        def out_panel(w, k0, nk, p):
            v = w.rearrange("(k p) n -> p k n", p=P)
            return v[:, k0:k0 + nk, bass.ds(p * PANEL, PANEL)]

        def out_sp(sp, n, s0, rows, w):
            with sp.Fori(0, 2) as i:
                n.enter(i, [len(rows), len(rows)])
                s = s0
                for q in range(2):
                    for k0, nk in rows:
                        load(sp, n, s, out_panel(w, k0, nk, 2 * i + q))
                        s = 1 - s
            n.leave(2)

        def ffn_sp(sp, n, l, f, s0):
            with sp.Fori(0, FP) as j:
                n.enter(j, [1, 1])
                load(sp, n, s0, w_in_panel(l, f, 0, j))
                load(sp, n, 1 - s0, w_in_panel(l, f, 1, j))
            n.leave(FP)
            out_sp(sp, n, s0, HID_ROWS, a["ffn_w_out"][l, f])

        def ffn_pe(pe, n, g, s0):
            def body(j, first):
                pe.wait_ge(*g("gate_scaled", j + 1))
                products(pe, n, s0, PK, [ps[:, 0, :], ps[:, 1, :]], lambda k: xn_hi[:, k, :],
                         lambda k: xn_lo[:, k, :], True, True, arrived=operand_pe(pe, g, 4) if first else None)
                if first:
                    sum_squares(pe, g, C - 1, 4)
                pe.wait_ge(*g("product", j + 1))
                products(pe, n, 1 - s0, PK, [ps[:, 2, :], ps[:, 3, :]], lambda k: xn_hi[:, k, :],
                         lambda k: xn_lo[:, k, :], True, True)

            body(0, True)
            with pe.Fori(1, FP) as j:
                n.enter(j - 1, [1, 1])
                body(j, False)
            n.leave(FP - 1)
            out_pe(pe, n, g, s0, HID_ROWS, lambda k: hid_hi[:, k, :], lambda k: hid_lo[:, k, :],
                   lambda k: pe.wait_ge(*g("hid", k // 2 + 2)) if k % 2 == 0 else None)

        def ffn_act(act, n, g, s0, l, f, seen, more):
            out_start_act(act, g)
            operand_act(act, g, l, 4 * f, seen, 4)
            act.preload_act_table(ACT.Silu)
            with act.Fori(0, FP) as j:
                n.enter(j, [1, 1])
                act.wait_ge(*g("gate_scaled", j + 2))
                nc.scalar.activation(ch(sil, 0), ch(sil, 0), ACT.Silu)
                nc.scalar.activation(ch(sil, 1), ch(sil, 1), ACT.Silu).then_inc(g("silu"), 1)
                split_hi(act, n, s0)
                split_hi(act, n, 1 - s0)
                act.wait_ge(*g("product", j + 2))
                nc.scalar.activation(ch(hid_hi, 2 * j), ch(hn, 0), ACT.Copy)
                nc.scalar.activation(ch(hid_hi, 2 * j + 1), ch(hn, 1), ACT.Copy).then_inc(g("hid_hi"), 1)
            n.leave(FP)
            out_act(act, n, g, s0, HID_ROWS, y_ffn, more)

        def ffn_dve(dve, n, g, s0, l, f, seen, more, low):
            out_start(g)
            dve.wait_ge(*g("rstd", 1))
            with dve.Fori(0, FP) as j:
                n.enter(j, [1, 1])
                wait_used(dve, n, s0)
                dve.wait_ge(*g("product", j + 1))
                nc.vector.tensor_tensor(ch(sil, 0), ch(ps, 0), rstd[:].unsqueeze(1), ALU.mult)
                nc.vector.tensor_tensor(ch(sil, 1), ch(ps, 1), rstd[:].unsqueeze(1), ALU.mult
                                        ).then_inc(g("gate_scaled"), 1)
                split_lo(dve, n, s0)
                wait_used(dve, n, 1 - s0)
                dve.wait_ge(*g("factor", 2 * j + 2))
                dve.wait_ge(*g("hid", j + 1))
                nc.vector.tensor_tensor(ch(hn, 0), ch(ps, 2), ch(sil, 0), ALU.mult)
                nc.vector.tensor_tensor(ch(hn, 1), ch(ps, 3), ch(sil, 1), ALU.mult).then_inc(g("product"), 1)
                split_lo(dve, n, 1 - s0)
                dve.wait_ge(*g("hid_hi", j + 1))
                nc.vector.tensor_tensor(ch(hid_lo, 2 * j), ch(hn, 0), ch(hid_hi, 2 * j).bitcast(F32),
                                        ALU.subtract)
                nc.vector.tensor_tensor(ch(hid_lo, 2 * j + 1), ch(hn, 1),
                                        ch(hid_hi, 2 * j + 1).bitcast(F32), ALU.subtract).then_inc(g("hid"), 1)
            n.leave(FP)
            out_dve(dve, n, g, s0, HID_ROWS, y_ffn, (vec_h, gain(l, 4 * f + 1, 0)), seen, more, low)

        def ffn_pool(pool, g, seen):
            with pool.Fori(0, FP) as j:
                pool.wait_ge(*g("silu", j + 1))
                for m in range(2):
                    nc.gpsimd.tensor_tensor(ch(sil, m), ch(sil, m), rstd[:].unsqueeze(1),
                                            ALU.mult).then_inc(g("factor"), 1)
                    pool.wait_ge(*g("factor", 2 * j + m + 1))
            out_pool(pool, g, seen)

        HD, NKV, GRP, NB = 64, 4, 4, S // P
        QD = NKV * GRP * HD
        SCALE = HD ** -0.5
        KV_ROWS = groups_of(C)
        m_at = {"at": o_arena}

        def arena(name, shape, dt=F32):
            n_bytes = 4
            for d in shape[1:]:
                n_bytes *= d
            at = m_at["at"]
            m_at["at"] = at + (n_bytes + 31) // 32 * 32
            assert m_at["at"] <= o_arena + 2 * FC * S * 4, (name, m_at)
            return sb(name, shape, dt, at)

        o_hi = arena("o_hi", [P, C, S], F32R)
        o_lo = arena("o_lo", [P, C, S], F32R)
        kz = arena("kz", [P, NKV, NB, 2, P])
        v_sb = arena("v_sb", [P, NB, NKV * HD])
        v_g = arena("v_g", [P, NB, HD])
        q_rot = arena("q_rot", [P, 2, S])
        merged = arena("merged", [P, 2, GRP, P])
        prob = arena("prob", [P, 2, GRP, P])
        prob_t = arena("prob_t", [P, 2, 2, GRP, P])
        cos_t = arena("cos_t", [P, S])
        sin_t = arena("sin_t", [P, S])
        rot_m = arena("rot_m", [P, P])
        tri_i = arena("tri_i", [P, P], I32)
        tri_t = arena("tri_t", [P, P])
        tri_u = arena("tri_u", [P, P])
        v_bias = arena("v_bias", [P, NKV * HD])
        r_tok = arena("r_tok", [P, NB])
        sink = arena("sink", [P, NKV * GRP])
        n_sink = arena("n_sink", [P, NKV * GRP])
        top = arena("top", [P, 2, GRP])
        n_top = arena("n_top", [P, 2, GRP])
        sink_d = arena("sink_d", [P, 2, GRP])
        den = arena("den", [P, 2, GRP])
        t1, t2 = sil[:, 0, :], sil[:, 1, :]
        ATT_CONST = [(cos_t, "cos"), (sin_t, "sin"), (rot_m, "rot_m"), (tri_i, "tri_i"), (tri_t, "tri_t"),
                     (tri_u, "tri_u")]

        def qkv_panel(p):
            return a["attn_w_qkv"][0].rearrange("(k p) n -> p k n", p=P)[:, :, bass.ds(p * PANEL, PANEL)]

        def attn_sp(sp, n, g, before, s0):
            load(sp, n, s0, qkv_panel(QD // PANEL))
            load(sp, n, 1 - s0, qkv_panel(QD // PANEL + 1))
            sp.wait_ge(*before("y_mean", 1))
            for t, name in ATT_CONST:
                sp.dma_start(t[:], a[name]).then_inc(g("const"), 16)
            sp.dma_start(v_bias[:], a["attn_b_qkv"][0:1, QD + NKV * HD:QD + 2 * NKV * HD]
                         .rearrange("o n -> (o n)").partition_broadcast(P)).then_inc(g("const"), 16)
            sp.dma_start(sink[:], a["attn_sinks"].rearrange("o n -> (o n)").partition_broadcast(P)
                         ).then_inc(g("const"), 16)
            wo = a["attn_w_o"][0]
            load(sp, n, s0, qkv_panel(0))
            load(sp, n, 1 - s0, out_panel(wo, 0, C, 0))
            with sp.Fori(1, NKV) as i:
                n.enter(i - 1, [1, 0] if s0 == 0 else [0, 1])
                load(sp, n, s0, qkv_panel(i))
            n.leave(NKV - 1)
            for p in range(1, D // PANEL):
                load(sp, n, s0 if p % 2 else 1 - s0, out_panel(wo, 0, C, p))

        ATT_CONSTS = 16 * (len(ATT_CONST) + 2)

        def attn_pe(pe, n, g, s0):
            pe.sem_inc(g("transposed"), 2)
            pe.sem_inc(g("weighed"), 2)
            xh, xl = (lambda k: xn_hi[:, k, :]), (lambda k: xn_lo[:, k, :])
            products(pe, n, s0, C, [ps[:, 0, :], ps[:, 1, :]], xh, xl, True, True, arrived=operand_pe(pe, g, 6))
            sum_squares(pe, g, C - 1, 6)
            s = 1 - s0
            pe.wait_ge(lo_done[s], n.next(s) + 2)
            for t in range(NB):
                o = ps[:, 4 + t // 2, (t % 2) * PANEL:(t % 2 + 1) * PANEL]
                for k in range(C):
                    h, l = xn_hi[:, k, t * P:(t + 1) * P], xn_lo[:, k, t * P:(t + 1) * P]
                    nc.tensor.matmul(o, h, w_hi[:, s, k, :], start=k == 0, stop=False)
                    nc.tensor.matmul(o, h, w_lo[:, s, k, :], start=False, stop=False)
                    end = nc.tensor.matmul(o, l, w_hi[:, s, k, :], start=False, stop=k == C - 1)
            end.then_inc(used[s], 1)
            pe.wait_ge(*g("rstd", 1))
            for t in range(NB):
                end = nc.tensor.transpose(ps[:, 7, t * P:(t + 1) * P], rstd[:, t * P:(t + 1) * P], ident[:])
            end.then_inc(g("by_token"), 1)
            pe.wait_ge(*g("const", ATT_CONSTS))
            for m in range(2):
                pe.wait_ge(*g("linear", m + 1))
                nc.tensor.matmul(ps[:, 2 + m, :], rot_m[:], hn[:, m, :], start=True,
                                 stop=True).then_inc(g("rotated"), 1)

            def scores(i, b):
                if b >= 2:
                    pe.wait_ge(*g("merged", 4 * i + b - 1))
                for back in range(min(b, 1) + 1):
                    for m in range(2):
                        end = nc.tensor.matmul(ps[:, 4 + 2 * back + b % 2, m * 2 * P:(m + 1) * 2 * P],
                                               q_rot[:, m, b * P:(b + 1) * P],
                                               kz[:, bass.ds(i, 1), b - back, :, :], start=True, stop=True)
                end.then_inc(g("scored"), 1)

            def transposes(i, b):
                pe.wait_ge(*g("normed", 4 * i + b + 1))
                for h in range(GRP):
                    end = nc.tensor.transpose(ps[:, 3, h * P:(h + 1) * P], prob[:, b % 2, h, :], ident[:])
                end.then_inc(g("transposed"), 1)

            def values(i, b):
                pe.wait_ge(*g("prob_t", 4 * i + b + 1))
                pe.wait_ge(*g("o_done", 4 * i + b + 2))
                for par in range(2):
                    o = ps[par * HD:(par + 1) * HD, 2, 0:2 * P]
                    for back in range(min(b, 1) + 1):
                        end = nc.tensor.matmul(o, v_g[:, b - back, :], prob_t[:, b % 2, back, par::2, :],
                                               start=back == 0, stop=back == min(b, 1))
                end.then_inc(g("weighed"), 1)

            def query(part):
                if part == 0:
                    pe.wait_ge(lo_done[s0], n.next(s0) + 2)
                for k in range(2 * part, 2 * part + 2):
                    for m in range(2):
                        wh, wl = (w[:, s0, k, m * P:(m + 1) * P] for w in (w_hi, w_lo))
                        nc.tensor.matmul(ps[:, m, :], wh, xh(k), start=k == 0, stop=False)
                        nc.tensor.matmul(ps[:, m, :], wh, xl(k), start=False, stop=False)
                        end = nc.tensor.matmul(ps[:, m, :], wl, xh(k), start=False, stop=k == C - 1)
                if part == 3:
                    end.then_inc(used[s0], 1)

            def rotate(i):
                for m in range(2):
                    pe.wait_ge(*g("linear", 2 * i + 3 + m))
                    nc.tensor.matmul(ps[:, m, :], rot_m[:], hn[:, m, :], start=True,
                                     stop=True).then_inc(g("rotated"), 1)

            def heads(i, ahead):
                pe.wait_ge(*g("roped", 2 * i + 4))
                scores(i, 0)
                scores(i, 1)
                if ahead:
                    query(0)
                    query(1)
                pe.wait_ge(*g("v_g", i + 1))
                for b in range(NB):
                    transposes(i, b)
                    if b + 2 < NB:
                        scores(i, b + 2)
                    values(i, b)
                    if ahead and b < 2:
                        query(2 + b)
                    if ahead and b == 2:
                        rotate(i + 1)

            for part in range(4):
                query(part)
            rotate(0)
            pe.wait_ge(*g("kz", 2))
            with pe.Fori(0, NKV - 1) as i:
                n.enter(i, [1, 0] if s0 == 0 else [0, 1])
                heads(i, True)
            n.leave(NKV - 1)
            heads(NKV - 1, False)
            out_pe(pe, n, g, 1 - s0, KV_ROWS, lambda k: o_hi[:, k, :], lambda k: o_lo[:, k, :],
                   lambda k: pe.wait_ge(*g("o_done", 4 * (k // 2) + 6)) if k % 2 == 0 else None)

        def attn_act(act, n, g, s0, seen, more):
            out_start_act(act, g)
            act.sem_inc(g("exped"), 2)
            operand_act(act, g, 0, 2, seen, 6)
            for m in range(2):
                act.wait_ge(*g("scaled", m + 1))
                nc.scalar.activation(ch(hn, m), ch(hn, m), ACT.Identity,
                                     bias=col(vec_r, QD // P + m)).then_inc(g("linear"), 1)
            split_hi(act, n, s0)
            split_hi(act, n, 1 - s0)

            def previous(i, b):
                act.wait_ge(*g("scored", 4 * i + b + 1))
                act.wait_ge(*g("exped", 4 * i + b + 1))
                nc.scalar.activation(merged[:, b % 2, :, :], ps[:, 6 + b % 2, :].rearrange("p (h k) -> p h k", k=P),
                                     ACT.Copy).then_inc(g("previous"), 1)

            def exps(i, b):
                act.wait_ge(*g("n_top", 4 * i + b + 1))
                act.wait_ge(*g("transposed", 4 * i + b + 1))
                for h in range(GRP):
                    nc.scalar.activation(prob[:, b % 2, h, :], merged[:, b % 2, h, :], ACT.Exp,
                                         bias=n_top[:, b % 2, h:h + 1], scale=SCALE,
                                         accum_out=den[:, b % 2, h:h + 1])
                nc.scalar.activation(sink_d[:, b % 2, :], sink_d[:, b % 2, :], ACT.Exp).then_inc(g("exped"), 1)

            def out_hi(i, b):
                act.wait_ge(*g("weighed", 4 * i + b + 3))
                nc.scalar.activation(o_hi[:, bass.ds(2 * i, 2), b * P:(b + 1) * P],
                                     ps[:, 2, 0:2 * P].rearrange("p (m q) -> p m q", q=P),
                                     ACT.Copy).then_inc(g("o_hi"), 1)

            def linear(i):
                for m in range(2):
                    act.wait_ge(*g("scaled", 2 * i + 3 + m))
                    nc.scalar.activation(ch(hn, m), ch(hn, m), ACT.Identity,
                                         bias=col(vec_r, 2 * i + m)).then_inc(g("linear"), 1)

            def heads(i, ahead):
                previous(i, 1)
                exps(i, 0)
                for b in range(1, NB):
                    if b + 1 < NB:
                        previous(i, b + 1)
                    exps(i, b)
                    out_hi(i, b - 1)
                    if ahead and b == 2:
                        linear(i + 1)
                if ahead:
                    split_hi(act, n, s0)
                out_hi(i, NB - 1)

            linear(0)
            split_hi(act, n, s0)
            with act.Fori(0, NKV - 1) as i:
                n.enter(i, [1, 0] if s0 == 0 else [0, 1])
                heads(i, True)
            n.leave(NKV - 1)
            heads(NKV - 1, False)
            out_act(act, n, g, 1 - s0, KV_ROWS, y_ffn, more, late=not more)

        def rope(dve, g, at, m, bank, write):
            dve.wait_ge(*g("rotated", at + 1))
            dve.wait_ge(*g("rope_free", at + 1))
            nc.vector.tensor_tensor(t1, hn[:, m, :], cos_t[:], ALU.mult)
            nc.vector.tensor_tensor(t2, ps[:, bank, :], sin_t[:], ALU.mult).then_inc(g("turned"), 1)
            dve.wait_ge(*g("turned", at + 1))
            write()

        def attn_dve(dve, n, g, s0, seen, more, low):
            out_start(g)
            dve.sem_inc(g("o_done"), 2)
            dve.sem_inc(g("rope_free"), 1)

            def scale():
                wait_used(dve, n, s0)
                for m in range(2):
                    nc.vector.tensor_tensor(ch(hn, m), ch(ps, m), rstd[:].unsqueeze(1),
                                            ALU.mult).then_inc(g("scaled"), 1)

            dve.wait_ge(*g("rstd", 1))
            scale()
            dve.wait_ge(*g("const", ATT_CONSTS))
            nc.vector.tensor_scalar(n_sink[:], sink[:], -1.0, None, ALU.mult).then_inc(g("n_sink"), 1)
            split_lo(dve, n, s0)
            dve.wait_ge(*g("by_token", 1))
            nc.vector.tensor_copy(r_tok[:].unsqueeze(2), ps[:, 7, :].rearrange("p (t q) -> p t q", q=P)[:, :, 0:1]
                                  ).then_inc(g("r_tok"), 1)
            dve.wait_ge(*g("r_tok", 1))
            wait_used(dve, n, 1 - s0)
            for t in range(NB):
                end = nc.vector.scalar_tensor_tensor(
                    v_sb[:, t, :], ps[:, 4 + t // 2, (t % 2) * PANEL:(t % 2 + 1) * PANEL], r_tok[:, t:t + 1],
                    v_bias[:], ALU.mult, ALU.add)
            end.then_inc(g("v"), 1)
            split_lo(dve, n, 1 - s0)
            dve.wait_ge(*g("kz_zero", 2))
            for m in range(2):
                def write():
                    for half in range(2):
                        at = slice(half * HD, (half + 1) * HD)
                        for par in range(2):
                            o = kz[par * HD:(par + 1) * HD, 2 * m + half, :, par, :]
                            end = nc.vector.tensor_tensor(
                                o, t1[at].rearrange("p (b k) -> p b k", k=P),
                                t2[at].rearrange("p (b k) -> p b k", k=P), ALU.add)
                            if half == 1 and par == 1:
                                end.then_inc(g("roped"), 1)
                            elif half == 1:
                                end.then_inc(g("kz_part"), 1)
                rope(dve, g, m, m, 2 + m, write)
                dve.wait_ge(*g("roped", m + 1))
                dve.sem_inc(g("kz"), 1)
                dve.sem_inc(g("rope_free"), 1)

            def merge(i, b):
                if b == 0:
                    dve.wait_ge(*g("cleared", i + 1))
                else:
                    dve.wait_ge(*g("previous", 3 * i + b))
                dve.wait_ge(*g("scored", 4 * i + b + 1))
                dve.sem_inc(g("merging"), 1)
                nc.vector.copy_predicated(merged[:, b % 2, :, :], tri_i[:].unsqueeze(1).to_broadcast([P, GRP, P]),
                                          ps[:, 4 + b % 2, :].rearrange("p (h k) -> p h k", k=P)
                                          ).then_inc(g("merged"), 1)
                dve.wait_ge(*g("merged", 4 * i + b + 1))
                nc.vector.reduce_max(top[:, b % 2, :], merged[:, b % 2, :, :], AX.X).then_inc(g("top"), 1)
                dve.wait_ge(*g("top", 4 * i + b + 1))
                nc.vector.scalar_tensor_tensor(n_top[:, b % 2, :], top[:, b % 2, :], -SCALE,
                                               n_sink[:, bass.ds(GRP * i, GRP)], ALU.mult,
                                               ALU.min).then_inc(g("n_top0"), 1)
                dve.wait_ge(*g("n_top0", 4 * i + b + 1))
                nc.vector.tensor_tensor(sink_d[:, b % 2, :], n_top[:, b % 2, :], sink[:, bass.ds(GRP * i, GRP)],
                                        ALU.add).then_inc(g("n_top"), 1)

            def normalize(i, b):
                dve.wait_ge(*g("exped", 4 * i + b + 3))
                nc.vector.tensor_tensor(den[:, b % 2, :], den[:, b % 2, :], sink_d[:, b % 2, :],
                                        ALU.add).then_inc(g("den"), 1)
                dve.wait_ge(*g("den", 4 * i + b + 1))
                nc.vector.reciprocal(top[:, b % 2, :], den[:, b % 2, :]).then_inc(g("rden"), 1)
                dve.wait_ge(*g("rden", 4 * i + b + 1))
                nc.vector.tensor_tensor(prob[:, b % 2, :, :], prob[:, b % 2, :, :],
                                        top[:, b % 2, :].unsqueeze(2).to_broadcast([P, GRP, P]),
                                        ALU.mult).then_inc(g("normed"), 1)

            def mask(i, b):
                dve.wait_ge(*g("transposed", 4 * i + b + 3))
                dve.wait_ge(*g("weighed", 4 * i + b + 1))
                pt = ps[:, 3, :].rearrange("p (h q) -> p h q", q=P)
                end = nc.vector.tensor_tensor(prob_t[:, b % 2, 0, :, :], pt,
                                              tri_t[:].unsqueeze(1).to_broadcast([P, GRP, P]), ALU.mult)
                if b > 0:
                    end = nc.vector.tensor_tensor(prob_t[:, b % 2, 1, :, :], pt,
                                                  tri_u[:].unsqueeze(1).to_broadcast([P, GRP, P]), ALU.mult)
                end.then_inc(g("prob_t"), 1)

            def out_low(i, b):
                dve.wait_ge(*g("o_hi", 4 * i + b + 1))
                at = (slice(None), bass.ds(2 * i, 2), slice(b * P, (b + 1) * P))
                nc.vector.tensor_tensor(o_lo[at], ps[:, 2, 0:2 * P].rearrange("p (m q) -> p m q", q=P),
                                        o_hi[at].bitcast(F32), ALU.subtract).then_inc(g("o_done"), 1)

            def rope_query(i, m):
                def write():
                    nc.vector.tensor_tensor(q_rot[:, m, :], t1, t2, ALU.add).then_inc(g("roped"), 1)
                rope(dve, g, 2 * i + 2 + m, m, m, write)
                dve.wait_ge(*g("roped", 2 * i + 3 + m))
                dve.sem_inc(g("rope_free"), 1)

            def heads(i, ahead):
                merge(i, 0)
                for b in range(NB):
                    if b + 1 < NB:
                        merge(i, b + 1)
                    normalize(i, b)
                    if b >= 1:
                        out_low(i, b - 1)
                    if ahead and b == NB - 2:
                        scale()
                    if ahead and b == NB - 1:
                        rope_query(i + 1, 1)
                    mask(i, b)
                    if ahead and b == NB - 2:
                        rope_query(i + 1, 0)
                if ahead:
                    split_lo(dve, n, s0)
                out_low(i, NB - 1)

            scale()
            for m in range(2):
                rope_query(0, m)
            split_lo(dve, n, s0)
            with dve.Fori(0, NKV - 1) as i:
                n.enter(i, [1, 0] if s0 == 0 else [0, 1])
                heads(i, True)
            n.leave(NKV - 1)
            heads(NKV - 1, False)
            out_dve(dve, n, g, 1 - s0, KV_ROWS, y_ffn, (vec_n, gain(0, 3, 0)), seen, more, low,
                    late=not more)

        def attn_pool(pool, g, before, seen):
            pool.wait_ge(*before("y_mean", 1))
            for par in range(2):
                nc.gpsimd.memset(kz[(1 - par) * HD:(2 - par) * HD, :, :, par, :], 0.0).then_inc(g("kz_zero"), 1)
                pool.wait_ge(*g("kz_zero", par + 1))
            pool.wait_ge(*g("v", 1))
            with pool.Fori(0, NKV) as i:
                pool.wait_ge(*g("weighed", 4 * i + 2))
                nc.gpsimd.tensor_copy(v_g[:], v_sb[:, :, bass.ds(HD * i, HD)]).then_inc(g("v_g"), 1)
                pool.wait_ge(*g("v_g", i + 1))
                pool.wait_ge(*g("exped", 4 * i + 1))
                pool.sem_inc(g("clearing"), 1)
                nc.gpsimd.memset(merged[:, 0, :, :], -1e30).then_inc(g("cleared"), 1)
                pool.wait_ge(*g("cleared", i + 1))
            out_pool(pool, g, seen)

        HEAD = 64
        LEVELS = P.bit_length() - 1
        UNITS = 2 * NB
        LORA = [("rwkv_w1", 64), ("rwkv_a1", 64), ("rwkv_g1", 160)]
        FILLS = 6
        DECAY = -math.exp(-0.5)
        V_MIX, V_W0 = 12, 12 + 6 * C
        V_A0, V_KK, V_KA, V_RK, V_LG, V_LB = (V_W0 + j * C for j in range(1, 7))

        m_at["at"] = o_arena
        h_pad = arena("h_pad", [P, C, S + 1])
        rkv = arena("rkv", [P, 3, C, S])
        y_rwkv = sb("y_rwkv", [P, C, S], F32, o_arena + C * (S + 1) * 4 + 2 * C * S * 4)
        sg = arena("sg", [P, 2, S])
        wa2 = arena("wa2", [P, 2, D])
        g2 = arena("g2", [P, 2, D])
        twa = sb("twa", [P, S], F32, take(S * 4))
        o_h = {"at": o_arena}

        def over(region, size, name, shape, dt=F32):
            n_bytes = 4
            for d in shape[1:]:
                n_bytes *= d
            at = region["at"]
            region["at"] = at + (n_bytes + 31) // 32 * 32
            assert region["at"] <= region.setdefault("end", at + size), name
            return sb(name, shape, dt, at)

        HB = C * (S + 1) * 4
        lvl = over(o_h, HB, "lvl", [P, LEVELS, P])
        lvl0_t = over(o_h, HB, "lvl0_t", [P, P])
        low2 = over(o_h, HB, "low2", [P, 2, P])
        blk = over(o_h, HB, "blk", [P, 2, P])
        ind_b = over(o_h, HB, "ind_b", [P, D])
        ind_s = over(o_h, HB, "ind_s", [P, C, 2 * C])
        k_norm = over(o_h, HB, "k_norm", [P, S])
        o_r = {"at": o_raw}
        mb = over(o_r, 16384, "mb", [P, NB, 2, 2, P])
        mk = over(o_r, 16384, "mk", [P, NB, 2, 2, P])
        o_w = {"at": o_whi}
        inv = over(o_w, 32768, "inv", [P, UNITS, P])
        inv_t = over(o_w, 32768, "inv_t", [P, UNITS, P])
        pair = over(o_w, 32768, "pair", [P, UNITS, P])
        toks = over(o_w, 32768, "toks", [P, NB, 3, P])
        v_tok, k_tok, b_tok = (toks[:, :, j, :] for j in range(3))
        ar = over(o_w, 32768, "ar", [P, 2, NB, 2, P])
        bt = over(o_w, 32768, "bt", [P, S])
        kt = over(o_w, 32768, "kt", [P, S])
        v_c = over(o_w, 32768, "v_c", [P, S])
        o_n = {"at": o_xnh}
        ar1 = over(o_n, 32768, "ar1", [P, 2, NB, 2, P])
        last_x = over(o_n, 32768, "last_x", [P, UNITS, P])
        m2 = over(o_n, 32768, "m2", [P, 2, S])
        yb = over(o_n, 32768, "yb", [P, S])
        qs = over(o_n, 32768, "qs", [P, S])
        wa_c = over(o_n, 32768, "wa_c", [P, 2, P])
        g_c = over(o_n, 32768, "g_c", [P, 2, P])
        ind_c = over(o_n, 32768, "ind_c", [P, P])
        state = over(o_n, 32768, "state", [P, 2, HEAD])
        grown = over(o_n, 32768, "grown", [P, HEAD])
        u0 = over(o_n, 32768, "u0", [P, 2, HEAD])
        u = over(o_n, 32768, "u", [P, 2, HEAD])
        mid = over(o_n, 32768, "mid", [P, NB])
        n_mid = over(o_n, 32768, "n_mid", [P, NB])
        carry = over(o_n, 32768, "carry", [P, 2, NB])
        ars = (ar, ar1)
        o_t = {"at": o_tmp}
        dl = over(o_t, 16384, "dl", [P, S])
        lc = over(o_t, 16384, "lc", [P, S])
        kk = over(o_t, 16384, "kk", [P, S])
        rate = over(o_t, 16384, "rate", [P, S])
        kp = over(o_t, 16384, "kp", [P, S])
        m1 = over(o_t, 16384, "m1", [P, S])
        ex = sb("ex", [P, NB, P + 1], F32, take(NB * (P + 1) * 4))
        ones_row = sb("ones_row", [P, P], F32, take(P * 4))
        omka = sb("omka", [P, C], F32, take(C * 4))
        w0h = sb("w0h", [P, 2 * C], F32, take(2 * C * 4))
        eps_ln = sb("eps_ln", [P, 1], F32, take(32))
        half_decay = sb("half_decay", [P, 1], F32, take(32))
        half = sb("half", [P, 1], F32, take(32))
        assert start + place["at"] <= nc.sbuf_usable_end, (start, place, nc.sbuf_usable_end)
        R_CONST = [(lvl, "lvl"), (lvl0_t, "lvl0_t"), (low2, "low2"), (blk, "blk"), (ind_b, "ind_b"), (ind_s, "ind_s")]

        def rkv_panel(i, p):
            return a["rwkv_w_rkv"][0].rearrange("i (k p) n -> i p k n", p=P)[bass.ds(i, 1), :, :,
                                                                           bass.ds(p * PANEL, PANEL)].rearrange(
                "i p k n -> (i p) k n")

        def rwkv_sp(sp, n, g, before, s0):
            for j, (name, cols) in enumerate(LORA):
                load(sp, n, (s0 + j) % 2, a[name][0].rearrange("(k p) n -> p k n", p=P), cols)
                if j == 1:
                    sp.wait_ge(*g("zeros", 4))
                    sp.dma_start(wa2[0:64, 0, :], a["rwkv_w2"][0]).then_inc(g("lora_in"), 16)
                    sp.dma_start(wa2[64:128, 1, :], a["rwkv_a2"][0]).then_inc(g("lora_in"), 16)
                    sp.dma_start(g2[:, 0, :], a["rwkv_g2"][0, 0:P, :]).then_inc(g("lora_in"), 16)
                    sp.dma_start(g2[0:32, 1, :], a["rwkv_g2"][0, P:P + 32, :]).then_inc(g("lora_in"), 16)
            with sp.Fori(0, 3) as i:
                n.enter(i, [2, 2])
                for p in range(D // PANEL):
                    load(sp, n, (s0 + 1 + p) % 2, rkv_panel(i, p))
            n.leave(3)
            sp.wait_ge(*g("mixed", 2 + C * FILLS))
            for t, name in R_CONST:
                sp.dma_start(t[:], a[name]).then_inc(g("const"), 16)
            sp.wait_ge(*g("y_mm", NB * C))
            for p in range(D // PANEL):
                load(sp, n, (s0 + 1 + p) % 2, out_panel(a["rwkv_w_o"][0], 0, C, p))

        R_CONSTS = 16 * len(R_CONST)
        xh, xl = (lambda k: xn_hi[:, k, :]), (lambda k: xn_lo[:, k, :])

        def rwkv_proj_pe(pe, n, g, s0):
            for f in range(3):
                b0 = (4, 6, 2)[f]
                nb = 2 if f == 2 else 1
                products(pe, n, (s0 + f) % 2, C, [ps[:, b0 + m, :] for m in range(nb)], xh, xl, True, True,
                         arrived=lambda k: pe.wait_ge(*g("mixed_lo", C * f + k + 3)), freed=g("freed"))
            with pe.Fori(0, 3) as i:
                n.enter(i, [2, 2])
                for p in range(D // PANEL):
                    b0 = 4 + 2 * (p % 2)
                    pe.wait_ge(*g("projected", 4 * i + p + 1))
                    products(pe, n, (s0 + 1 + p) % 2, C, [ps[:, b0, :], ps[:, b0 + 1, :]], xh, xl, True, True,
                             arrived=(lambda k: pe.wait_ge(*g("mixed_lo", C * i + 3 * C + k + 3))) if p == 0 else None,
                             freed=g("freed") if p == 3 else None)
            n.leave(3)

        def chunks(eng, prepare, body):
            prepare()
            body(0, 0, True, True, False)
            with eng.Fori(0, (C - 2) // 2) as i:
                body(2 * i + 1, 1, True, True, True)
                body(2 * i + 2, 0, True, True, True)
            body(C - 1, 1, False, True, True)
            body(C, 0, False, False, True)

        L2, X2, T2 = 2 * LEVELS, 2 * (LEVELS - 1), 2 * (LEVELS - 2)

        def decay_pe(pe, g, k):
            pe.wait_ge(*g("statics", 2 * k + 2))
            nc.tensor.matmul(ps[:, 0, :], wa_c[:, 0, :], twa[:], start=True, stop=True).then_inc(g("pre"), 1)
            nc.tensor.matmul(ps[:, 1, :], wa_c[:, 1, :], twa[:], start=True, stop=True).then_inc(g("pre"), 1)

        def key_pe(pe, g):
            nc.tensor.matmul(ps[:, 3, :], ind_c[:], k_norm[:], start=True, stop=True).then_inc(g("pre"), 1)

        def chunk_pe(pe, g, c, par, ahead, here, tail):
            q, a_q, a_c = c - 1, ars[1 - par], ars[par]

            def attn(t, j):
                if j == 0 and t >= 2:
                    pe.wait_ge(*g("masked", 8 * c + 2 * t - 2))
                nc.tensor.matmul(ps[:, 4 + 2 * (t % 2) + j, :], (bt, kt)[j][:, t * P:(t + 1) * P],
                                 a_c[:, :, t, :, :], start=True, stop=True).then_inc(g("attn"), 1)

            if here:
                pe.wait_ge(*g("gates", 2 * c + 2))
                pe.wait_ge(*g("kb", c + 1))
                pe.wait_ge(*g("ar", c + 1))
                pe.wait_ge(*g("v_c", c + 1))
            for t in range(NB):
                if tail:
                    pe.wait_ge(*g("state", NB * q + t + 1))
                    for h in range(2):
                        o = ps[:, 0, h * HEAD:(h + 1) * HEAD]
                        nc.tensor.matmul(o, a_q[:, h, t, 0, :], state[:, t % 2, :], start=True, stop=False)
                        end = nc.tensor.matmul(o, mk[:, t, h, 0, :], v_tok[:, t, h * HEAD:(h + 1) * HEAD],
                                               start=False, stop=True)
                    end.then_inc(g("u0_mm"), 1)
                if here:
                    attn(t, 0)
                if tail:
                    pe.wait_ge(*g("u0", NB * q + t + 1))
                    for h in range(2):
                        end = nc.tensor.matmul(ps[:, 1, h * HEAD:(h + 1) * HEAD], inv_t[:, 2 * t + h, :], u0[:, h, :],
                                               start=True, stop=True)
                    end.then_inc(g("u_mm"), 1)
                if here:
                    attn(t, 1)
                if tail:
                    pe.wait_ge(*g("u", NB * q + t + 1))
                    if t < NB - 1:
                        for h in range(2):
                            o = ps[h * HEAD:(h + 1) * HEAD, 0, 256:256 + HEAD]
                            at = slice(h * HEAD, (h + 1) * HEAD)
                            nc.tensor.matmul(o, b_tok[:, t, at], u[:, h, :], start=True, stop=False)
                            end = nc.tensor.matmul(o, k_tok[:, t, at], v_tok[:, t, at], start=False, stop=True)
                        end.then_inc(g("s_mm"), 1)
                    if t == 0:
                        pe.wait_ge(*g("gated", c + 1))
                    for h in range(2):
                        o = ps[h * HEAD:(h + 1) * HEAD, 2, t * P:(t + 1) * P]
                        vt = v_tok[:, t, h * HEAD:(h + 1) * HEAD]
                        nc.tensor.matmul(o, state[:, t % 2, :], a_q[:, h, t, 1, :], start=True, stop=False)
                        nc.tensor.matmul(o, u[:, h, :], mb[:, t, h, 1, :], start=False, stop=False)
                        end = nc.tensor.matmul(o, vt, mk[:, t, h, 1, :], start=False, stop=True)
                    end.then_inc(g("y_mm"), 1)
                if here:
                    if t > 0:
                        pe.wait_ge(*g("tok_sb", NB * c + t))
                    for j, src in enumerate((v_c, kt, bt)):
                        end = nc.tensor.transpose(ps[:, 3, j * P:(j + 1) * P], src[:, t * P:(t + 1) * P], ident[:])
                    end.then_inc(g("tok"), 1)

            def post(part):
                if part == 0:
                    pe.wait_ge(*g("y_sb", c))
                    if ahead:
                        pe.wait_ge(*g("gates", 2 * c + 4))
                    nc.tensor.matmul(ps[:, 1, :], blk[:, 1, :], yb[:], start=True, stop=True).then_inc(g("mean"), 1)
                elif part == 1:
                    pe.wait_ge(*g("bonus_in", c))
                    if ahead:
                        pe.wait_ge(*g("kk", c + 2))
                    nc.tensor.matmul(ps[:, 3, :], blk[:, 0, :], m2[:, 1 - par, :], start=True,
                                     stop=True).then_inc(g("bonus"), 1)
                    pe.wait_ge(*g("g_c", c))
                    nc.tensor.matmul(ps[:, 2, :], g_c[:, 0, :], sg[:, 0, :], start=True, stop=False)
                    nc.tensor.matmul(ps[:, 2, :], g_c[:, 1, :], sg[:, 1, :], start=False,
                                     stop=True).then_inc(g("gate"), 1)
                else:
                    pe.wait_ge(*g("dev_sq", c))
                    nc.tensor.matmul(ps[:, 0, :], blk[:, 1, :], qs[:], start=True, stop=True).then_inc(g("var"), 1)

            if not here:
                for part in range(3):
                    post(part)
                return
            for l in range(LEVELS):
                x_l = last_x if l == LEVELS - 1 else pair
                for G in range(2):
                    if l > 0:
                        pe.wait_ge(*g("inv", L2 * c + 2 * (l - 1) + G + 1))
                    else:
                        pe.wait_ge(*g("masked", 8 * c + 6 + G))
                    for w in range(4):
                        un = 4 * G + w
                        o, m_t = ps[:, 4 + G, w * P:(w + 1) * P], mb[:, un // 2, un % 2, 0, :]
                        if l == 0:
                            end = nc.tensor.transpose(o, m_t, ident[:])
                        else:
                            end = nc.tensor.matmul(o, m_t, inv[:, un, :], start=True, stop=True)
                    end.then_inc(g("x_mm"), 1)
                if l == 0 and ahead:
                    pe.wait_ge(*g("tok_sb", NB * c + NB))
                    decay_pe(pe, g, c + 1)
                    key_pe(pe, g)
                for G in range(2 if l > 1 else 0):
                    for w in range(4):
                        end = nc.tensor.transpose(ps[:, 6 + G, w * P:(w + 1) * P], inv[:, 4 * G + w, :], ident[:])
                    end.then_inc(g("t_mm"), 1)
                if tail and 2 <= l < 5:
                    post(l - 2)
                for G in range(2 if l > 0 else 0):
                    pe.wait_ge(*g("x_sb", X2 * c + 2 * (l - 1) + G + 1))
                    if l > 1:
                        pe.wait_ge(*g("inv_t_sb", T2 * c + 2 * (l - 2) + G + 1))
                    for w in range(4):
                        un = 4 * G + w
                        o = ps[:, 6 + G, w * P:(w + 1) * P]
                        if l < LEVELS - 1:
                            end = nc.tensor.matmul(o, inv_t[:, un, :], x_l[:, un, :], start=True, stop=True)
                        else:
                            end = nc.tensor.matmul(o, x_l[:, un, :], inv_t[:, un, :], start=True, stop=True)
                    end.then_inc(g("upd"), 1)
            pe.wait_ge(*g("inv", L2 * c + L2))

        def rwkv_pe(pe, n, g, s0):
            norm_in_pe(pe, g)
            rwkv_proj_pe(pe, n, g, s0)
            pe.wait_ge(*g("const", R_CONSTS))
            pe.wait_ge(*g("lora_in", 64))
            decay_pe(pe, g, 0)
            for c in range(C):
                pe.wait_ge(*g("k_sq", c + 1))
                nc.tensor.matmul(ps[0:2 * C, 2, :], ind_s[:, c, :], (m1 if c % 2 == 0 else kk)[:], start=c == 0,
                                 stop=c == C - 1).then_inc(g("k_sums"), 1)
            pe.wait_ge(*g("k_norm", 1))
            pe.sem_inc(g("bonus"), 1)
            pe.sem_inc(g("gate"), 1)
            chunks(pe, lambda: key_pe(pe, g), lambda *at: chunk_pe(pe, g, *at))
            out_pe(pe, n, g, (s0 + 1) % 2, KV_ROWS, xh, xl, lambda k: pe.wait_ge(*g("out_lo", k + 1)))

        def gates_act(act, g, k, first=False):
            act.wait_ge(*g("pre", 3 * k + 1))
            if not first:
                act.wait_ge(*g("sums", k))
                act.wait_ge(*g("bonus_in", k))
                act.wait_ge(*g("ar", k))
            nc.scalar.activation(dl[:], ps[:, 0, :], ACT.Tanh, bias=col(w0h, k), scale=0.5).then_inc(g("tanh"), 1)
            act.wait_ge(*g("tanh", 2 * k + 1))
            nc.scalar.activation(dl[:], dl[:], ACT.Identity, bias=half_decay[:],
                                 scale=0.5 * DECAY).then_inc(g("gates"), 1)
            act.wait_ge(*g("pre", 3 * k + 2))
            nc.scalar.activation(rate[:], ps[:, 1, :], ACT.Tanh, bias=col(w0h, k + C), scale=0.5).then_inc(g("tanh"), 1)
            act.wait_ge(*g("tanh", 2 * k + 2))
            nc.scalar.activation(rate[:], rate[:], ACT.Identity, bias=half[:], scale=0.5).then_inc(g("gates"), 1)
            act.wait_ge(*g("gates", 2 * k + 2))
            nc.scalar.activation(kp[:], rate[:], ACT.Identity, bias=col(omka, k),
                                 scale=col(vec_r, V_KA + k)).then_inc(g("kp0"), 1)

        def exps_act(act, g, k, par):
            act.wait_ge(*g("sums", k + 1))
            nc.scalar.activation(ex[:, :, 1:P + 1], lc[:].rearrange("p (b t) -> p b t", t=P), ACT.Exp)
            nc.scalar.activation(ex[:, :, 0:1], n_mid[:].unsqueeze(2), ACT.Exp)
            nc.scalar.activation(carry[:, par, :], carry[:, par, :], ACT.Exp).then_inc(g("exps"), 1)
            act.wait_ge(*g("exps", 2 * k + 1))
            nc.scalar.activation(lc[:], lc[:], ACT.Exp, scale=-1.0).then_inc(g("exps"), 1)

        def chunk_act(act, g, c, par, ahead, here, tail):
            for t in range(NB):
                if tail:
                    act.wait_ge(*g("u0_mm", NB * (c - 1) + t + 1))
                    nc.scalar.activation(u0[:], ps[:, 0, 0:P].rearrange("p (h v) -> p h v", h=2),
                                         ACT.Copy).then_inc(g("u0"), 1)
                    act.wait_ge(*g("u_mm", NB * (c - 1) + t + 1))
                    if t > 0:
                        act.wait_ge(*g("y_mm", NB * (c - 1) + t))
                    nc.scalar.activation(u[:], ps[:, 1, 0:P].rearrange("p (h v) -> p h v", h=2),
                                         ACT.Copy).then_inc(g("u"), 1)
                if here:
                    act.wait_ge(*g("tok", NB * c + t + 1))
                    nc.scalar.activation(toks[:, t, :, :], ps[:, 3, 0:3 * P].rearrange("p (j t) -> p j t", t=P),
                                         ACT.Copy).then_inc(g("tok_sb"), 1)
                    if t % 2 == 1:
                        nc.scalar.activation(inv_t[:, 2 * t - 2:2 * t + 2, :], ident[:].unsqueeze(1).to_broadcast(
                            [P, 4, P]), ACT.Copy).then_inc(g("inv_t_start"), 1)

            def post(part):
                if part == 0:
                    act.wait_ge(*g("dev", c))
                    act.wait_ge(*g("gated", c + 1))
                    nc.scalar.activation(qs[:], yb[:], ACT.Square).then_inc(g("dev_sq"), 1)
                else:
                    act.preload_act_table_set(NORM_SET)
                    act.wait_ge(*g("var", c))
                    nc.scalar.activation(qs[:], ps[:, 0, :], ACT.Ln, bias=eps_ln[:]).then_inc(g("var_log"), 1)
                    act.wait_ge(*g("var_log", c))
                    nc.scalar.activation(qs[:], qs[:], ACT.Exp, scale=-0.5).then_inc(g("dev_rstd"), 1)

            def inv_ts(l):
                for G in range(2):
                    act.wait_ge(*g("t_mm", T2 * c + 2 * (l - 2) + G + 1))
                    nc.scalar.activation(inv_t[:, 4 * G:4 * G + 4, :], ps[:, 6 + G, :].rearrange(
                        "p (w t) -> p w t", t=P), ACT.Copy).then_inc(g("inv_t_sb"), 1)

            if tail:
                act.wait_ge(*g("y_mm", NB * c))
                nc.scalar.activation(yb[:], ps[:, 2, :], ACT.Copy).then_inc(g("y_sb"), 1)
            if ahead:
                gates_act(act, g, c + 1)
            if here:
                inv_ts(2)
            if ahead:
                exps_act(act, g, c + 1, 1 - par)
            if here:
                inv_ts(3)
            if tail:
                post(0)
            if here:
                inv_ts(4)
            if tail:
                post(1)
            if here:
                inv_ts(5)
                inv_ts(6)

        def rwkv_act(act, n, g, s0, seen, more):
            out_start_act(act, g)
            norm_in_squares(act, g, seen)

            def fill(f, s_last):
                for c in range(C):
                    act.wait_ge(*g("mixed", C * f + c + 3))
                    if not isinstance(f, int) or f > 0:
                        if c < C - 1:
                            act.wait_ge(*g("freed", (C - 1) * f + c + 1 - (C - 1)))
                        else:
                            wait_used(act, n, s_last)
                    nc.scalar.activation(ch(xn_hi, c), ch(hn, c % 2), ACT.Copy).then_inc(g("mixed_hi"), 1)

            fill(0, None)
            for f in range(3):
                s = (s0 + f) % 2
                fill(f + 1, s)
                wait_used(act, n, s)
                if f == 0:
                    nc.scalar.activation(twa[0:64, :], ps[0:64, 4, :], ACT.Tanh).then_inc(g("lora"), 1)
                elif f == 1:
                    nc.scalar.activation(twa[64:128, :], ps[0:64, 6, :], ACT.Copy).then_inc(g("projected"), 2)
                else:
                    act.wait_ge(*g("zeros", 4))
                    nc.scalar.activation(sg[:, 0, :], ps[:, 2, :], ACT.Tanh, scale=0.5)
                    nc.scalar.activation(sg[0:32, 1, :], ps[0:32, 3, :], ACT.Tanh, scale=0.5).then_inc(g("lora"), 1)
                split_hi(act, n, s)

            def project(i, p, split):
                s = (s0 + 1 + p) % 2
                b0 = 4 + 2 * (p % 2)
                act.wait_ge(used[s], n.peek(s) + 1)
                for m in range(2):
                    end = nc.scalar.activation(rkv[:, bass.ds(i, 1), 2 * p + m, :], ch(ps, b0 + m), ACT.Copy)
                end.then_inc(g("projected"), 1)
                if split:
                    split_hi(act, n, s)
            with act.Fori(0, 2) as i:
                n.enter(i, [2, 2])
                for p in range(4):
                    if p == 3:
                        fill(i + 4, s0 % 2)
                    project(i, p, True)
            n.leave(2)
            for p in range(4):
                project(2, p, p < 2)
            act.wait_ge(*g("const", R_CONSTS))
            act.wait_ge(*g("projected", 2 + 12))
            act.wait_ge(*g("mixed_lo", 2 + C * FILLS))
            act.preload_act_table(ACT.Sqrt)
            for c in range(C):
                if c >= 2:
                    act.wait_ge(*g("k_sums", c - 1))
                nc.scalar.activation((m1 if c % 2 == 0 else kk)[:], rkv[:, 1, c, :], ACT.Square,
                                     scale=col(vec_r, V_KK + c)).then_inc(g("k_sq"), 1)
            act.wait_ge(*g("k_sums", C))
            act.wait_ge(*g("k_zero", 1))
            nc.scalar.activation(k_norm[0:2 * C, :], ps[0:2 * C, 2, :], ACT.Sqrt).then_inc(g("k_len"), 1)
            def prepare():
                act.wait_ge(*g("tables", 1))
                gates_act(act, g, 0, first=True)
                exps_act(act, g, 0, 0)

            chunks(act, prepare, lambda *at: chunk_act(act, g, *at))
            split_hi(act, n, (s0 + 1) % 2)
            act.wait_ge(*g("gated", C + 2))
            for c in range(C):
                nc.scalar.activation(ch(xn_hi, c), rkv[:, 0, c:c + 1, :], ACT.Copy).then_inc(g("out_hi"), 1)
            split_hi(act, n, s0)
            out_act(act, n, g, (s0 + 1) % 2, KV_ROWS, y_rwkv, more)

        V = nc.vector
        by_block = lambda t: t.rearrange("p (b t) -> p b t", t=P)
        flat = lambda t: t.rearrange("p o t -> p (o t)")

        def scan_dve(dve, g, k, first=False):
            dve.wait_ge(*g("gates", 2 * k + 1))
            if not first:
                dve.wait_ge(*g("kb", k))
            for t in range(NB):
                ins = V.tensor_tensor_scan(lc[:, t * P:(t + 1) * P], ones_row[:], dl[:, t * P:(t + 1) * P], 0.0,
                                           ALU.mult, ALU.add)
            ins.then_inc(g("scanned"), 1)

        def sums_dve(dve, g, k, par):
            done = [0]

            def step(ins):
                done[0] += 1
                ins.then_inc(g("sum_steps"), 1)
                dve.wait_ge(*g("sum_steps", 2 * k + done[0]))

            dve.wait_ge(*g("scanned", k + 1))
            V.tensor_copy(mid[:].unsqueeze(2), by_block(lc[:])[:, :, P // 2 - 1:P // 2])
            step(V.tensor_scalar(n_mid[:].unsqueeze(2), by_block(lc[:])[:, :, P // 2 - 1:P // 2], -1.0, None, ALU.mult))
            step(V.tensor_tensor(by_block(lc[:]), by_block(lc[:]), n_mid[:].unsqueeze(2).to_broadcast([P, NB, P]),
                                 ALU.add))
            V.tensor_copy(carry[:, par, NB - 1:NB], lc[:, S - 1:S])
            V.tensor_tensor(carry[:, par, 0:NB - 1].unsqueeze(2), by_block(lc[:])[:, 0:NB - 1, P - 1:P],
                            mid[:, 1:NB].unsqueeze(2), ALU.add).then_inc(g("sums"), 1)
            assert done[0] == 2

        def key_dve(dve, g, k):
            dve.wait_ge(*g("pre", 3 * k + 3))
            V.scalar_tensor_tensor(kk[:], flat(rkv[:, 1, bass.ds(k, 1), :]), col(vec_r, V_KK + k), ps[:, 3, :],
                                   ALU.mult, ALU.mult).then_inc(g("kk"), 1)

        def ar_dve(dve, g, k, par):
            dve.wait_ge(*g("exps", 2 * k + 1))
            dve.wait_ge(*g("kk", k + 1))
            for h in range(2):
                at = slice(h * HEAD, (h + 1) * HEAD)
                V.scalar_tensor_tensor(ars[par][at, h, :, 0, :], by_block(kk[at]), -1.0, ex[at, :, 0:P],
                                       ALU.mult, ALU.mult)
                ins = V.tensor_tensor(ars[par][at, h, :, 1, :], by_block(flat(rkv[at, 0, bass.ds(k, 1), :])),
                                      ex[at, :, 1:P + 1], ALU.mult)
            ins.then_inc(g("ar"), 1)

        def chunk_dve(dve, g, c, par, ahead, here, tail):
            done = [0]

            def step(ins):
                done[0] += 1
                ins.then_inc(g("tail_steps"), 1)
                dve.wait_ge(*g("tail_steps", (NB + 2) * (c - 1) + done[0]))

            for t in range(NB):
                if tail and t < NB - 1:
                    dve.wait_ge(*g("s_mm", (NB - 1) * (c - 1) + t + 1))
                    dve.wait_ge(*g("state", NB * (c - 1) + t + 1))
                    step(V.tensor_tensor(grown[:], state[:, t % 2, :], ps[:, 0, 256:256 + HEAD], ALU.add))
                    V.tensor_scalar(state[:, (t + 1) % 2, :], grown[:], carry[:, 1 - par, t:t + 1], None,
                                    ALU.mult).then_inc(g("state"), 1)
                if tail:
                    dve.wait_ge(*g("y_mm", NB * (c - 1) + t + 1))
                for j in range(2 if here else 0):
                    dve.wait_ge(*g("attn", 8 * c + 2 * t + j + 1))
                    V.tensor_tensor((mb, mk)[j][:, t, :, :, :],
                                    ps[:, 4 + 2 * (t % 2) + j, :].rearrange("p (h a t) -> p h a t", h=2, a=2),
                                    low2[:].unsqueeze(1).to_broadcast([P, 2, 2, P]), ALU.mult).then_inc(g("masked"), 1)

            bank = lambda k: ps[:, k, :].rearrange("p (w t) -> p w t", t=P)

            def level(l):
                b, x_l = 1 << l, last_x if l == LEVELS - 1 else pair
                split = lambda t, side: t.rearrange("p w (q two b) -> p w q two b", two=2, b=b)[:, :, :, side, :]
                units = [slice(4 * G, 4 * G + 4) for G in range(2)]
                mask = lambda t, side: split(t.unsqueeze(1).to_broadcast([P, 4, P]), side)
                if l == 0:
                    dve.wait_ge(*g("masked", 8 * c + 8))
                    for G, us in enumerate(units):
                        V.tensor_tensor(split(x_l[:, us, :], 1), split(
                            mb[:, 2 * G:2 * G + 2, :, 0, :].rearrange("p b h t -> p (b h) t"), 1),
                            mask(lvl0_t[:], 1), ALU.mult)
                    for G, us in enumerate(units):
                        dve.wait_ge(*g("x_mm", L2 * c + G + 1))
                        V.tensor_tensor(split(x_l[:, us, :], 0), split(bank(4 + G), 0), mask(lvl[:, l, :], 0),
                                        ALU.mult).then_inc(g("x0"), 1)
                    for G, us in enumerate(units):
                        dve.wait_ge(*g("inv_start", c + 1))
                        dve.wait_ge(*g("inv_t_start", 2 * c + G + 1))
                        dve.wait_ge(*g("x0", 2 * c + G + 1))
                        V.tensor_tensor(split(inv[:, us, :], 0), split(inv[:, us, :], 0), split(x_l[:, us, :], 0),
                                        ALU.add)
                        V.tensor_tensor(split(inv_t[:, us, :], 1), split(inv_t[:, us, :], 1),
                                        split(x_l[:, us, :], 1), ALU.add).then_inc(g("inv"), 1)
                    return
                dve.wait_ge(*g("inv", L2 * c + 2 * l))
                for G, us in enumerate(units):
                    dve.wait_ge(*g("x_mm", L2 * c + 2 * l + G + 1))
                    V.tensor_tensor(split(x_l[:, us, :], 0), split(bank(4 + G), 0), mask(lvl[:, l, :], 0),
                                    ALU.mult).then_inc(g("x_sb"), 1)
                for G, us in enumerate(units):
                    dve.wait_ge(*g("upd", X2 * c + 2 * (l - 1) + G + 1))
                    t, side = (inv, 0) if l < LEVELS - 1 else (inv_t, 1)
                    V.tensor_tensor(split(t[:, us, :], side), split(t[:, us, :], side), split(bank(6 + G), side),
                                    ALU.add).then_inc(g("inv"), 1)

            def post(part):
                if part == 0:
                    dve.wait_ge(*g("mean", c))
                    V.tensor_tensor(yb[:], yb[:], ps[:, 1, :], ALU.subtract).then_inc(g("dev"), 1)
                    return
                if part == 1:
                    dve.wait_ge(*g("dev_rstd", c))
                    dve.wait_ge(*g("dev", c))
                    step(V.tensor_tensor(yb[:], yb[:], qs[:], ALU.mult))
                    dve.wait_ge(*g("bonus", c + 1))
                    V.tensor_tensor(qs[:], flat(rkv[:, 2, bass.ds(c - 1, 1), :]), ps[:, 3, :], ALU.mult)
                    return
                step(V.tensor_scalar(yb[:], yb[:], col(vec_r, V_LG - 1 + c), col(vec_r, V_LB - 1 + c),
                                     ALU.mult, ALU.add))
                step(V.tensor_tensor(yb[:], yb[:], qs[:], ALU.add))
                dve.wait_ge(*g("gate", c + 1))
                V.tensor_tensor(flat(rkv[:, 0, bass.ds(c - 1, 1), :]), yb[:], ps[:, 2, :],
                                ALU.mult).then_inc(g("gated"), 1)

            if here:
                V.memset(state[:, 0, :], 0.0).then_inc(g("state"), 1)
                level(0)
            if ahead:
                scan_dve(dve, g, c + 1)
            if here:
                level(1)
            if ahead:
                sums_dve(dve, g, c + 1, 1 - par)
            if here:
                level(2)
            if ahead:
                key_dve(dve, g, c + 1)
            if tail:
                post(0)
            if here:
                level(3)
            if ahead:
                ar_dve(dve, g, c + 1, 1 - par)
            if here:
                level(4)
            if tail:
                post(1)
            if here:
                level(5)
                level(6)
            if tail:
                post(2)
            assert not tail or done[0] == NB + 2, done

        def rwkv_dve(dve, n, g, s0, seen, more, low):
            dve.sem_inc(g("mixed"), 2)
            dve.sem_inc(g("mixed_lo"), 2)
            dve.wait_ge(*g("rstd", 1))
            nc.vector.memset(h_pad[:, :, 0:1], 0.0)
            for c in range(C):
                nc.vector.scalar_tensor_tensor(h_pad[:, c, 1:S + 1], x[:, c, :], col(vec_n, gain(1, 2, c)),
                                               rstd[:], ALU.mult, ALU.mult).then_inc(g("h"), 1)
            dve.wait_ge(*g("h", C))

            def fill(f):
                for c in range(C + 1):
                    if c < C:
                        dve.wait_ge(*g("xx", C * f + c + 1))
                        dve.wait_ge(*g("mixed_lo", C * f + c + 1))
                        nc.vector.scalar_tensor_tensor(hn[:, c % 2, :], sil[:, c % 2, :],
                                                       col(vec_r, C * f + (V_MIX + c)), h_pad[:, c, 1:S + 1],
                                                       ALU.mult, ALU.add).then_inc(g("mixed"), 1)
                    if c >= 1:
                        dve.wait_ge(*g("mixed_hi", C * f + c))
                        nc.vector.tensor_tensor(ch(xn_lo, c - 1), ch(hn, (c - 1) % 2),
                                                ch(xn_hi, c - 1).bitcast(F32), ALU.subtract).then_inc(g("mixed_lo"), 1)

            fill(0)
            for f in range(3):
                fill(f + 1)
                if f == 2:
                    dve.wait_ge(*g("lora", 2))
                    nc.vector.tensor_scalar(sg[:, 0, :], sg[:, 0, :], 0.5, 0.5, ALU.mult, ALU.add)
                    nc.vector.tensor_scalar(sg[0:32, 1, :], sg[0:32, 1, :], 0.5, 0.5, ALU.mult,
                                            ALU.add).then_inc(g("sg"), 1)
                split_lo(dve, n, (s0 + f) % 2)
            with dve.Fori(0, 2) as i:
                n.enter(i, [2, 2])
                for p in range(4):
                    if p == 3:
                        fill(i + 4)
                    split_lo(dve, n, (s0 + 1 + p) % 2)
            n.leave(2)
            for p in range(4):
                if p < 2:
                    split_lo(dve, n, (s0 + 1 + p) % 2)
            nc.vector.tensor_scalar(omka[:], vec_r[:, V_KA:V_KA + C], -1.0, 1.0, ALU.mult, ALU.add)
            nc.vector.tensor_scalar(w0h[:], vec_r[:, V_W0:V_W0 + 2 * C], 0.5, None, ALU.mult)
            nc.vector.memset(ones_row[:], 1.0)
            nc.vector.memset(half_decay[:], 0.5 * DECAY)
            nc.vector.memset(half[:], 0.5)
            nc.vector.memset(eps_ln[:], 64e-5).then_inc(g("tables"), 1)
            dve.wait_ge(*g("tables", 1))
            dve.wait_ge(*g("k_len", 1))
            nc.vector.tensor_scalar(k_norm[0:2 * C, :], k_norm[0:2 * C, :], 1e-12, None,
                                    ALU.max).then_inc(g("k_max"), 1)
            dve.wait_ge(*g("k_max", 1))
            nc.vector.reciprocal(k_norm[0:2 * C, :], k_norm[0:2 * C, :]).then_inc(g("k_norm"), 1)
            dve.wait_ge(*g("ar_zero", 5))
            dve.sem_inc(g("gated"), 2)

            def prepare():
                scan_dve(dve, g, 0, first=True)
                sums_dve(dve, g, 0, 0)
                key_dve(dve, g, 0)
                ar_dve(dve, g, 0, 0)

            chunks(dve, prepare, lambda *at: chunk_dve(dve, g, *at))
            split_lo(dve, n, (s0 + 1) % 2)
            for c in range(C):
                dve.wait_ge(*g("out_hi", c + 1))
                nc.vector.tensor_tensor(ch(xn_lo, c), rkv[:, 0, c:c + 1, :], ch(xn_hi, c).bitcast(F32),
                                        ALU.subtract).then_inc(g("out_lo"), 1)
            out_start(g)
            split_lo(dve, n, s0)
            out_dve(dve, n, g, (s0 + 1) % 2, KV_ROWS, y_rwkv, (vec_n, gain(1, 3, 0)), seen, more, low)


        def rwkv_pool(pool, g, before, seen):
            pool.wait_ge(*before("y_mean", 1))
            for j, t in enumerate((wa2, g2, sg)):
                nc.gpsimd.memset(t[:], 0.0).then_inc(g("zeros"), 1)
                pool.wait_ge(*g("zeros", j + 1))
            pool.sem_inc(g("zeros"), 1)
            def fill(f):
                for c in range(C):
                    if isinstance(f, int):
                        pool.wait_ge(*g("h", c + 1))
                    pool.wait_ge(*g("mixed", C * f + c + 1))
                    nc.gpsimd.tensor_tensor(sil[:, c % 2, :], h_pad[:, c, 0:S], h_pad[:, c, 1:S + 1],
                                            ALU.subtract).then_inc(g("xx"), 1)
                    pool.wait_ge(*g("xx", C * f + c + 1))

            fill(0)
            with pool.Fori(1, FILLS) as f:
                fill(f)
            pool.wait_ge(*g("const", R_CONSTS))
            pool.wait_ge(*g("mixed_lo", 2 + C * FILLS))
            nc.gpsimd.memset(k_norm[:], 0.0).then_inc(g("k_zero"), 1)
            pool.wait_ge(*g("k_zero", 1))
            pool.wait_ge(*g("lora_in", 64))
            pool.wait_ge(*g("projected", 14))
            statics(pool, g, 0)
            zeroed = [(t[(1 - h) * HEAD:(2 - h) * HEAD, h, :, :, :]) for t in ars for h in range(2)] + [
                last_x[:]]
            for j, t in enumerate(zeroed):
                nc.gpsimd.memset(t, 0.0).then_inc(g("ar_zero"), 1)
                pool.wait_ge(*g("ar_zero", j + 1))
            v_copy(pool, g, 0)

            chunks(pool, lambda: prepare_pool(pool, g, 0, 0, first=True), lambda *at: chunk_pool(pool, g, *at))
            out_pool(pool, g, seen)

        def one(pool, g, name, at, ins):
            ins.then_inc(g(name), 1)
            pool.wait_ge(*g(name, at))

        def statics(pool, g, k):
            one(pool, g, "statics", 2 * k + 1, nc.gpsimd.tensor_copy(wa_c[:], wa2[:, :, bass.ds(k * P, P)]))
            one(pool, g, "statics", 2 * k + 2, nc.gpsimd.tensor_copy(ind_c[:], ind_b[:, bass.ds(k * P, P)]))

        def v_copy(pool, g, k):
            one(pool, g, "v_c", k + 1, nc.gpsimd.tensor_copy(v_c[:].unsqueeze(1), rkv[:, 2, bass.ds(k, 1), :]))

        def prepare_pool(pool, g, k, par, first=False):
            r_c, k_c = (flat(rkv[:, j, bass.ds(k, 1), :]) for j in range(2))
            G = nc.gpsimd
            pool.wait_ge(*g("kp0", k + 1))
            one(pool, g, "pool", 4 * k + 1, G.tensor_tensor(kp[:], kp[:], k_c, ALU.mult))
            pool.wait_ge(*g("kk", k + 1))
            one(pool, g, "pool", 4 * k + 2, G.tensor_tensor(rate[:], rate[:], kk[:], ALU.mult))
            pool.wait_ge(*g("exps", 2 * k + 2))
            if not first:
                pool.wait_ge(*g("tok", NB * k))
            one(pool, g, "pool", 4 * k + 3, G.tensor_tensor(kt[:], kp[:], lc[:], ALU.mult))
            one(pool, g, "kb", k + 1, G.tensor_tensor(bt[:], rate[:], lc[:], ALU.mult))
            if not first:
                pool.wait_ge(*g("bonus", k))
            one(pool, g, "pool", 4 * k + 4, G.tensor_tensor(m2[:, par, :], kp[:], r_c, ALU.mult))
            one(pool, g, "bonus_in", k + 1, G.tensor_tensor(m2[:, par, :], m2[:, par, :],
                                                            col(vec_r, V_RK + k).to_broadcast([P, S]), ALU.mult))

        def chunk_pool(pool, g, c, par, ahead, here, tail):
            if ahead:
                pool.wait_ge(*g("pre", 3 * c + 3))
                statics(pool, g, c + 1)
            if here:
                if tail:
                    pool.wait_ge(*g("t_mm", T2 * c))
                pool.sem_inc(g("copying"), 1)
                one(pool, g, "inv_start", c + 1, nc.gpsimd.tensor_copy(
                    inv[:], ident[:].unsqueeze(1).to_broadcast([P, UNITS, P])))
            if ahead:
                pool.wait_ge(*g("tok", NB * c + NB))
                v_copy(pool, g, c + 1)
            if tail:
                pool.wait_ge(*g("gate", c))
                one(pool, g, "g_c", c, nc.gpsimd.tensor_copy(g_c[:], g2[:, :, bass.ds((c - 1) * P, P)]))
            if ahead:
                prepare_pool(pool, g, c + 1, 1 - par)

        st = signals("start")
        fin = signals("end")

        def start_sp(sp):
            sp.dma_start(xt[:], a["x"].rearrange("b (t p) d -> p (b t) d", p=P)).then_inc(x_in, 16)
            sp.dma_start(ident[:], a["consts"][:, 0:P]).then_inc(consts_in, 16)
            sp.dma_start(ones_d[:], a["consts"][:, P:2 * P]).then_inc(consts_in, 16)
            sp.dma_start(rows_n[:], a["norm_g"].rearrange("l i (c p) -> (l i c) p", p=P)).then_inc(consts_in, 16)
            at = 0
            for name in [r for n in ROWS for r in (MIXES if n == "rwkv_mix" else [n])]:
                if isinstance(name, int):
                    v = a["rwkv_mix"][0, name:name + 1].rearrange("m (c p) -> (m c) p", p=P)
                    sp.dma_start(rows_r[at:at + C, :], v).then_inc(consts_in, 16)
                    at += C
                    continue
                sizes = {"h": 2} if name == "rwkv_r_k" else {"p": P}
                v = a[name].rearrange(VIEWS.get(name, "o (c p) -> (o c) p"), **sizes)
                sp.dma_start(rows_r[at:at + v.shape[0], :], v).then_inc(consts_in, 16)
                at += v.shape[0]

        def start_pe(pe):
            pe.wait_ge(consts_in, 48 + 16 * (len(ROWS) + 5))
            nr = 2 * NG * C
            nc.tensor.transpose(ps[:, 6, 0:nr], rows_n[:], ident[0:nr, 0:nr]).then_inc(st("vec"), 1)
            nc.tensor.transpose(ps[:, 7, 0:N_ROWS], rows_r[0:N_ROWS, :],
                                ident[0:N_ROWS, 0:N_ROWS]).then_inc(st("vec"), 1)
            pe.wait_ge(x_in, 16)
            for c in range(C):
                if c >= 6:
                    pe.wait_ge(x_loaded, c - 5)
                for t in range(S // P):
                    end = nc.tensor.transpose(ps[:, c % 6, t * P:(t + 1) * P], xt[:, t, c * P:(c + 1) * P], ident[:])
                end.then_inc(st("x"), 1)
            pe.wait_ge(x_loaded, C)

        def start_dve(dve):
            for s in range(2):
                dve.sem_inc(lo_done[s], 1)
            nc.vector.memset(eps_rms[:], 1e-6).then_inc(st("eps"), 1)
            dve.wait_ge(*st("vec", 2))
            nc.vector.tensor_copy(vec_r[:, 0:N_ROWS], ps[:, 7, 0:N_ROWS]).then_inc(st("vecs"), 1)
            nr = 2 * NG * C
            nc.vector.tensor_copy(vec_n[:, 0:nr], ps[:, 6, 0:nr])
            nc.vector.tensor_scalar(vec_h[:, 0:nr], ps[:, 6, 0:nr], 0.5, None, ALU.mult).then_inc(st("vecs"), 1)
            dve.wait_ge(*st("vecs", 2))
            for c in range(C):
                dve.wait_ge(*st("x", c + 1))
                nc.vector.tensor_copy(ch(x, c), ch(ps, c % 6)).then_inc(x_loaded, 1)
            n_dve = SlotCount()
            split_lo(dve, n_dve, 0)
            return n_dve

        def start_act(act):
            n_act = SlotCount()
            act.preload_act_table_set(NORM_SET)
            act.wait_ge(*st("eps", 1))
            for s in range(2):
                split_hi(act, n_act, s)
            act.wait_ge(*st("vecs", 2))
            return n_act

        def end_pe(pe, seen):
            for c in range(C):
                pe.wait_ge(*x_at(seen, c + 1))
                for t in range(S // P):
                    b = 2 * t + c // 4
                    end = nc.tensor.transpose(ps[:, b, (c % 4) * P:(c % 4 + 1) * P], x[:, c, t * P:(t + 1) * P],
                                              ident[:])
                end.then_inc(fin("x"), 1)

        def end_evac(eng, copy, t, g):
            eng.wait_ge(*fin("x", C))
            for h in range(2):
                end = copy(ot[:, t, h * 512:(h + 1) * 512], ps[:, 2 * t + h, :])
                end.then_inc(g, 1)

        def end_sp(sp):
            o = out.rearrange("b (t p) d -> p (b t) d", p=P)
            for t in range(S // P):
                sp.wait_ge(*fin(f"done{t % 2}", 2 * (t // 2 + 1)))
                sp.dma_start(o[:, t:t + 1, :], ot[:, t:t + 1, :]).then_inc(out_done, 16)
            sp.wait_ge(out_done, 16 * (S // P))

        sig = {name: signals(name, stages[:e]) for e, name in enumerate(stages)}
        layer = {"ffn0a": (0, 0), "ffn0b": (0, 1), "ffn1a": (1, 0), "ffn1b": (1, 1)}
        slot0 = {}
        s = 0
        for name in stages:
            slot0[name] = s
            if name == "rwkv":
                s = 1 - s
        block = ctx.enter_context(nc.Block())

        @block.sync
        def _(sp):
            start_sp(sp)
            n = SlotCount()
            for e, name in enumerate(stages):
                if name in layer:
                    ffn_sp(sp, n, *layer[name], slot0[name])
                if name == "attn":
                    attn_sp(sp, n, sig[name], sig[stages[e - 1]], slot0[name])
                if name == "rwkv":
                    rwkv_sp(sp, n, sig[name], sig[stages[e - 1]], slot0[name])
            end_sp(sp)

        @block.scalar
        def _(act):
            n = start_act(act)
            for e, name in enumerate(stages):
                if name in layer:
                    ffn_act(act, n, sig[name], slot0[name], *layer[name], e * C, e < len(stages) - 1)
                if name == "attn":
                    attn_act(act, n, sig[name], slot0[name], e * C, e < len(stages) - 1)
                if name == "rwkv":
                    rwkv_act(act, n, sig[name], slot0[name], e * C, e < len(stages) - 1)
            end_evac(act, lambda o, i: nc.scalar.activation(o, i, ACT.Copy), 1, fin("done1"))
            end_evac(act, lambda o, i: nc.scalar.activation(o, i, ACT.Copy), 3, fin("done1"))

        @block.vector
        def _(dve):
            def low(e):
                if e == len(stages) or stages[e] == "rwkv":
                    return None
                if stages[e] == "attn":
                    return operand_dve(dve, sig["attn"], 0, 2, False)
                l, f = layer[stages[e]]
                return operand_dve(dve, sig[stages[e]], l, 4 * f, True)

            n = start_dve(dve)
            for c in range(C):
                low(0)(c)
            split_lo(dve, n, 1)
            for e, name in enumerate(stages):
                rest = ((e + 1) * C, e < len(stages) - 1, low(e + 1))
                if name in layer:
                    ffn_dve(dve, n, sig[name], slot0[name], *layer[name], *rest)
                if name == "attn":
                    attn_dve(dve, n, sig[name], slot0[name], *rest)
                if name == "rwkv":
                    rwkv_dve(dve, n, sig[name], slot0[name], *rest)
            end_evac(dve, nc.vector.tensor_copy, 0, fin("done0"))
            end_evac(dve, nc.vector.tensor_copy, 2, fin("done0"))

        @block.tensor
        def _(pe):
            for s in range(2):
                pe.sem_inc(used[s], 1)
            start_pe(pe)
            n = SlotCount()
            for name in stages:
                if name in layer:
                    ffn_pe(pe, n, sig[name], slot0[name])
                if name == "attn":
                    attn_pe(pe, n, sig[name], slot0[name])
                if name == "rwkv":
                    rwkv_pe(pe, n, sig[name], slot0[name])
            end_pe(pe, len(stages) * C)


        @block.gpsimd
        def _(pool):
            for e, name in enumerate(stages):
                seen = (e + 1) * C
                if name in layer:
                    ffn_pool(pool, sig[name], seen)
                if name == "attn":
                    attn_pool(pool, sig[name], sig[stages[e - 1]], seen)
                if name == "rwkv":
                    rwkv_pool(pool, sig[name], sig[stages[e - 1]], seen)


def constants():
    import numpy as np
    small = np.concatenate([np.eye(P), np.full((P, P), 1.0 / D)], axis=1).astype(np.float32)
    inv = (np.float32(10000.0) ** (-np.arange(0, 64, 2, dtype=np.float32) / np.float32(64))).astype(np.float32)
    ang = np.arange(S, dtype=np.float32)[None, :] * inv[:, None]
    cos, sin = np.cos(ang), np.sin(ang)
    i = np.arange(P)
    swap = np.zeros((P, P), np.float32)
    swap[i ^ 32, i] = 1.0
    head = i[:, None] // 64 == i[None, :] // 64
    lower_of_pair = lambda i, b: ((i[:, None] // b) % 2 == 1) & (i[None, :] // b == i[:, None] // b - 1)
    return {
        "consts": small,
        "cos": np.concatenate([cos] * 4).astype(np.float32),
        "sin": np.concatenate([-sin, sin] * 2).astype(np.float32),
        "rot_m": swap,
        "tri_i": (i[None, :] <= i[:, None]).astype(np.int32),
        "tri_t": (i[:, None] <= i[None, :]).astype(np.float32),
        "lvl": np.concatenate([lower_of_pair(i, 1 << l) for l in range(7)], axis=1).astype(np.float32),
        "lvl0_t": lower_of_pair(i, 1).T.astype(np.float32),
        "low2": np.concatenate([i[:, None] < i[None, :], i[:, None] <= i[None, :]], axis=1).astype(np.float32),
        "blk": np.concatenate([head, head / 64], axis=1).astype(np.float32),
        "ind_b": (i[:, None] == np.arange(D)[None, :] // 64).astype(np.float32),
        "ind_s": np.concatenate([2 * c + i[:, None] // 64 == np.arange(16)[None, :] for c in range(C)],
                                axis=1).astype(np.float32),
        "tri_u": (i[:, None] > i[None, :]).astype(np.float32),
    }


STAGES = ["ffn0a", "attn", "ffn0b", "ffn1a", "rwkv", "ffn1b"]


def kernel(**inputs):
    import numpy as np
    import concourse.bacc as bacc
    from concourse.bass_utils import run_bass_kernel_spmd as run
    nc = bacc.Bacc("TRN2", target_bir_lowering=False, num_devices=1)
    arrays = {k: np.ascontiguousarray(v) for k, v in {**inputs, **constants()}.items()}
    a = {k: nc.dram_tensor(k, v.shape, mybir.dt.from_np(v.dtype), kind="ExternalInput").ap()
         for k, v in arrays.items()}
    out = nc.dram_tensor("out", (1, S, D), F32, kind="ExternalOutput").ap()
    build(nc, a, out, STAGES)
    r = run(nc, [arrays], core_ids=[0])
    return r.results[0]["out"]
```
